# Optimizing a Trainium2 kernel written in Bass

```python
import jax, jax.numpy as jnp
from jax import lax
import numpy as np

D_MODEL = 1024
BATCH = 1
SEQ = 1024
DEPTH = 1
DEC_BATCH = 8
DEC_SEQ = 16
PAST_LEN = 256

CHUNK = 64
QBLK = 128
H_A = 8
DH_A = 64
FOX_W = H_A * DH_A
H_B = 4
DK_B = 128
DV_B = 256
GLA_K = H_B * DK_B
GLA_V = H_B * DV_B
GLA_RANK = 16
GLA_TAU = 16
D_FF = 2816
CONV_W = 3
PLE_DIM = 256
LN_EPS = 1e-5
ALPHA = (2 * DEPTH) ** 0.25
BETA = (8 * DEPTH) ** -0.25
IN_SIZES = (FOX_W, FOX_W, FOX_W, H_A, GLA_K, GLA_K, GLA_V, GLA_V, GLA_RANK, D_MODEL, D_MODEL)
D_IN = FOX_W * 3 + H_A + GLA_K * 2 + GLA_V * 2 + GLA_RANK + D_MODEL * 2

kernel_name = "fox_gla_convffn_deepnorm_stream_step"

def _split_points():
    pts, acc = [], 0
    for s in IN_SIZES[:-1]:
        acc += s
        pts.append(acc)
    return pts

def layer_norm(x, g, b):
    xf = x.astype(jnp.float32)
    mu = jnp.mean(xf, axis=-1, keepdims=True)
    var = jnp.mean(jnp.square(xf - mu), axis=-1, keepdims=True)
    y = (xf - mu) * lax.rsqrt(var + LN_EPS) * g.astype(jnp.float32) + b.astype(jnp.float32)
    return y.astype(x.dtype)

def fox_attend(q, k, v, cq, ck, q_pos, k_pos):
    s = jnp.einsum('bqhd,bkhd->bhqk', q, k).astype(jnp.float32) * (DH_A ** -0.5)
    s = s + jnp.transpose(cq, (0, 2, 1))[..., :, None] - jnp.transpose(ck, (0, 2, 1))[..., None, :]
    mask = k_pos[None, :] <= q_pos[:, None]
    s = jnp.where(mask, s, -jnp.inf)
    p = jax.nn.softmax(s, axis=-1)
    return jnp.einsum('bhqk,bkhd->bqhd', p.astype(v.dtype), v)

def fox_mixer(q, k, v, logf, past):
    T = q.shape[1]
    if past is None:
        c = jnp.cumsum(logf, axis=1)
        outs = []
        for i in range(T // QBLK):
            lo, hi = i * QBLK, (i + 1) * QBLK
            outs.append(fox_attend(q[:, lo:hi], k[:, :hi], v[:, :hi], c[:, lo:hi], c[:, :hi],
                                   jnp.arange(lo, hi), jnp.arange(hi)))
        return jnp.concatenate(outs, axis=1)
    past_k, past_v, past_logf = past
    P = past_k.shape[1]
    k_all = jnp.concatenate([past_k.astype(k.dtype), k], axis=1)
    v_all = jnp.concatenate([past_v.astype(v.dtype), v], axis=1)
    c = jnp.cumsum(jnp.concatenate([past_logf.astype(jnp.float32), logf], axis=1), axis=1)
    return fox_attend(q, k_all, v_all, c[:, P:], c, P + jnp.arange(T), jnp.arange(P + T))

def gla_block(S, inp):
    q, k, v, la = inp
    L = q.shape[2]
    b = jnp.cumsum(la, axis=2)
    tri = jnp.tril(jnp.ones((L, L), dtype=bool))
    diff = b[:, :, :, None, :] - b[:, :, None, :, :]
    decay = jnp.exp(jnp.where(tri[:, :, None], diff, -jnp.inf))
    a = jnp.einsum('bhtc,bhtsc,bhsc->bhts', q, decay, k)
    o = jnp.einsum('bhts,bhsv->bhtv', a, v) + jnp.einsum('bhtc,bhcv->bhtv', q * jnp.exp(b), S)
    b_last = b[:, :, -1:, :]
    S_new = jnp.exp(b_last[:, :, 0, :])[..., None] * S + jnp.einsum('bhsc,bhsv->bhcv', k * jnp.exp(b_last - b), v)
    return S_new, o

def gla_mixer(q, k, v, la, S0):
    B, T, H, _ = q.shape
    L = min(CHUNK, T)
    n = T // L

    def to_blocks(a):
        return a.astype(jnp.float32).reshape(B, n, L, H, a.shape[-1]).transpose(1, 0, 3, 2, 4)

    S_fin, o = lax.scan(gla_block, S0.astype(jnp.float32), (to_blocks(q), to_blocks(k), to_blocks(v), to_blocks(la)))
    o = o.transpose(1, 0, 3, 2, 4).reshape(B, T, H, v.shape[-1])
    return o, S_fin

def trunk_layer(x, p, fox_past, gla_S0, conv_prev,
                w_in, b_fgate, w_a2, b_a2, g_gla, w_a_out, w_b_out, w_o, ln1_g, ln1_b,
                w_up, conv_w, conv_b, w_down, ln2_g, ln2_b, w_pl, w_plg, ln3_g, ln3_b):
    B, T, _ = x.shape
    proj = x @ w_in
    qa, ka, va, fa, qb, kb, vb, rb, a1, ga, gb = jnp.split(proj, _split_points(), axis=-1)

    qa = qa.reshape(B, T, H_A, DH_A)
    ka = ka.reshape(B, T, H_A, DH_A)
    va = va.reshape(B, T, H_A, DH_A)
    logf = jax.nn.log_sigmoid((fa + b_fgate).astype(jnp.float32))
    oa = fox_mixer(qa, ka, va, logf, fox_past)
    ya = oa.reshape(B, T, FOX_W) @ w_a_out

    la = jax.nn.log_sigmoid((a1 @ w_a2 + b_a2).astype(jnp.float32)) / GLA_TAU
    ob, S_fin = gla_mixer(qb.reshape(B, T, H_B, DK_B) * (DK_B ** -0.5), kb.reshape(B, T, H_B, DK_B),
                          vb.reshape(B, T, H_B, DV_B), la.reshape(B, T, H_B, DK_B), gla_S0)
    ob = ob * lax.rsqrt(jnp.mean(jnp.square(ob), axis=-1, keepdims=True) + LN_EPS) \
        * g_gla.astype(jnp.float32).reshape(H_B, DV_B)
    yb = (ob.astype(x.dtype) * jax.nn.silu(rb.reshape(B, T, H_B, DV_B))).reshape(B, T, GLA_V) @ w_b_out

    merged = jax.nn.sigmoid(ga) * ya + jax.nn.sigmoid(gb) * yb
    x1 = layer_norm(ALPHA * x + merged @ w_o, ln1_g, ln1_b)

    up = x1 @ w_up
    ext = jnp.concatenate([conv_prev.astype(up.dtype), up], axis=1)
    conv = conv_b + sum(conv_w[j] * ext[:, j:j + T] for j in range(CONV_W))
    conv_new = ext[:, T:]
    val, gate = jnp.split(conv, 2, axis=-1)
    ffn = (val * jax.nn.gelu(gate)) @ w_down
    x2 = layer_norm(ALPHA * x1 + ffn, ln2_g, ln2_b)

    e = (p @ w_pl) * jax.nn.sigmoid(x2 @ w_plg)
    y = layer_norm(ALPHA * x2 + e, ln3_g, ln3_b)
    return y, ka, va, logf.astype(x.dtype), S_fin.astype(x.dtype), conv_new

def setup_inputs(seed: int = 0) -> dict:
    key = jax.random.key(seed)
    ks = jax.random.split(key, 32)

    def nrm(k, shape, scale):
        return jax.random.normal(k, shape, jnp.float32) * scale

    D = D_MODEL
    return {
        "x_prompt": nrm(ks[0], (BATCH, SEQ, D), 1.0),
        "x_sample": nrm(ks[1], (DEC_BATCH, DEC_SEQ, D), 1.0),
        "cache_fox_k": nrm(ks[2], (DEPTH, DEC_BATCH, PAST_LEN, H_A, DH_A), 1.0),
        "cache_fox_v": nrm(ks[3], (DEPTH, DEC_BATCH, PAST_LEN, H_A, DH_A), 1.0),
        "cache_fox_logf": jax.nn.log_sigmoid(nrm(ks[4], (DEPTH, DEC_BATCH, PAST_LEN, H_A), 1.0) + 3.0),
        "state_gla": nrm(ks[5], (DEPTH, DEC_BATCH, H_B, DK_B, DV_B), 0.1),
        "cache_ffn_conv": nrm(ks[6], (DEPTH, DEC_BATCH, CONV_W - 1, 2 * D_FF), 1.0),
        "p_prompt": nrm(ks[7], (DEPTH, BATCH, SEQ, PLE_DIM), 1.0),
        "p_sample": nrm(ks[8], (DEPTH, DEC_BATCH, DEC_SEQ, PLE_DIM), 1.0),
        "w_in": nrm(ks[9], (DEPTH, D, D_IN), D ** -0.5),
        "b_fgate": jax.random.uniform(ks[10], (DEPTH, H_A), jnp.float32, 1.0, 4.0),
        "w_a2": nrm(ks[11], (DEPTH, GLA_RANK, GLA_K), GLA_RANK ** -0.5),
        "b_a2": nrm(ks[12], (DEPTH, GLA_K), 0.1),
        "g_gla": 1.0 + nrm(ks[13], (DEPTH, GLA_V), 0.05),
        "w_a_out": nrm(ks[14], (DEPTH, FOX_W, D), FOX_W ** -0.5),
        "w_b_out": nrm(ks[15], (DEPTH, GLA_V, D), GLA_V ** -0.5),
        "w_o": nrm(ks[16], (DEPTH, D, D), D ** -0.5 * BETA),
        "ln1_g": 1.0 + nrm(ks[17], (DEPTH, D), 0.05),
        "ln1_b": nrm(ks[18], (DEPTH, D), 0.02),
        "w_up": nrm(ks[19], (DEPTH, D, 2 * D_FF), D ** -0.5),
        "conv_w": nrm(ks[20], (DEPTH, CONV_W, 2 * D_FF), CONV_W ** -0.5),
        "conv_b": nrm(ks[21], (DEPTH, 2 * D_FF), 0.02),
        "w_down": nrm(ks[22], (DEPTH, D_FF, D), D_FF ** -0.5 * BETA),
        "ln2_g": 1.0 + nrm(ks[23], (DEPTH, D), 0.05),
        "ln2_b": nrm(ks[24], (DEPTH, D), 0.02),
        "w_pl": nrm(ks[25], (DEPTH, PLE_DIM, D), PLE_DIM ** -0.5 * BETA),
        "w_plg": nrm(ks[26], (DEPTH, D, D), D ** -0.5),
        "ln3_g": 1.0 + nrm(ks[27], (DEPTH, D), 0.05),
        "ln3_b": nrm(ks[28], (DEPTH, D), 0.02),
    }

def reference(x_prompt, x_sample, cache_fox_k, cache_fox_v, cache_fox_logf, state_gla, cache_ffn_conv,
              p_prompt, p_sample, w_in, b_fgate, w_a2, b_a2, g_gla, w_a_out, w_b_out, w_o, ln1_g, ln1_b,
              w_up, conv_w, conv_b, w_down, ln2_g, ln2_b, w_pl, w_plg, ln3_g, ln3_b):
    hp, hs = x_prompt, x_sample
    kp_l, vp_l, fp_l, sp_l, cp_l = [], [], [], [], []
    ks_l, vs_l, fs_l, ss_l, cs_l = [], [], [], [], []
    for i in range(DEPTH):
        lp = (w_in[i], b_fgate[i], w_a2[i], b_a2[i], g_gla[i], w_a_out[i], w_b_out[i], w_o[i],
              ln1_g[i], ln1_b[i], w_up[i], conv_w[i], conv_b[i], w_down[i], ln2_g[i], ln2_b[i],
              w_pl[i], w_plg[i], ln3_g[i], ln3_b[i])
        S0_p = jnp.zeros((hp.shape[0], H_B, DK_B, DV_B), jnp.float32)
        conv0_p = jnp.zeros((hp.shape[0], CONV_W - 1, 2 * D_FF), hp.dtype)
        hp, kp, vp, fp, sp, cp = trunk_layer(hp, p_prompt[i], None, S0_p, conv0_p, *lp)
        hs, k_s, v_s, f_s, s_s, c_s = trunk_layer(
            hs, p_sample[i], (cache_fox_k[i], cache_fox_v[i], cache_fox_logf[i]),
            state_gla[i], cache_ffn_conv[i], *lp)
        kp_l.append(kp); vp_l.append(vp); fp_l.append(fp); sp_l.append(sp); cp_l.append(cp)
        ks_l.append(k_s); vs_l.append(v_s); fs_l.append(f_s); ss_l.append(s_s); cs_l.append(c_s)
    return (hp, hs,
            jnp.stack(kp_l), jnp.stack(vp_l), jnp.stack(fp_l), jnp.stack(sp_l), jnp.stack(cp_l),
            jnp.stack(ks_l), jnp.stack(vs_l), jnp.stack(fs_l), jnp.stack(ss_l), jnp.stack(cs_l))


_drawn_inputs = setup_inputs


def setup_inputs(seed=0):
    import zlib

    import numpy as np

    out = dict(_drawn_inputs(seed))
    spreads = {}
    factors = {'cache_fox_logf': 6.366,
     'state_gla': 3.613,
     'g_gla': 6.581,
     'ln1_b': 2.852,
     'conv_b': 6.448,
     'ln2_b': 2.945,
     'ln3_b': 2.741}
    for name, (base, spread) in spreads.items():
        noise = np.random.default_rng([zlib.crc32(name.encode()), seed]).standard_normal(out[name].shape)
        drawn = base * np.exp(spread * noise) if base else spread * noise
        out[name] = __import__('jax').numpy.asarray(drawn.astype(out[name].dtype))
    for name, factor in factors.items():
        out[name] = (out[name] * factor).astype(out[name].dtype)
    return out
```

```python
from contextlib import ExitStack

import numpy as np

import concourse.bass as bass
from concourse import mybir

F32 = mybir.dt.float32
U32 = mybir.dt.uint32
ALU = mybir.AluOpType
ACT = mybir.ActivationFunctionType
AX = mybir.AxisListType

P = 128
D = 1024
KT = D // P
SEQ, DEC_B, DEC_T = 1024, 8, 16
PAST = 256
T = SEQ + DEC_B * DEC_T
NP = SEQ // P
NT = T // P
THIRD = T // 3
H_A, DH = 8, 64
H_B, DK, DV = 4, 128, 256
RANK, TAU = 16, 16
D_FF, PLE = 2816, 256
NC_FF = D_FF // P
LN_EPS = 1e-5
ALPHA = 2.0 ** 0.25
NEG = -1e30
O_Q, O_K, O_V, O_F = 0, 512, 1024, 1536
O_QB, O_KB, O_VB, O_RB = 1544, 2056, 2568, 3592
O_A1, O_GA, O_GB = 4616, 4632, 5656
HALVES = [64, 32, 16, 8, 4, 2, 1]
FF_GROUPS = [8, 8, 6]
GROUP_STARTS = [sum(FF_GROUPS[:g]) for g in range(len(FF_GROUPS) + 1)]
W_SLOTS = 4

C_ID = 0
C_LEV = C_ID + P
C_CAUSAL = C_LEV + 7 * P
C_NEG1 = C_CAUSAL + P
C_NHALF = C_NEG1 + 1
C_BM = C_NHALF + 1
C_ONE = C_BM + DEC_B
C_KEEP = C_ONE + 1
C_HSEL = C_KEEP + 5
C_OMASK = C_HSEL + H_A * P
C_WIN = C_OMASK + H_A * DH
C_HS16 = C_WIN + 240
C_TSEL = C_HS16 + P
C_SCAN = C_TSEL + DEC_T
C_ALL = C_SCAN + T


def shape_constants():
    c = np.zeros((P, C_ALL), np.float32)
    i = np.arange(P)
    c[:, C_ID:C_ID + P] = np.eye(P)
    for n, h in enumerate(HALVES):
        s, t = i[:, None], i[None, :]
        c[:, C_LEV + n * P:C_LEV + (n + 1) * P] = (s // (2 * h) == t // (2 * h)) & (s % (2 * h) < h) & (t % (2 * h) >= h)
    c[:, C_CAUSAL:C_CAUSAL + P] = np.where(i[None, :] > i[:, None], NEG, 0.0)
    c[:, C_NEG1] = -1.0
    c[:, C_NHALF] = -0.5
    c[:, C_BM:C_BM + DEC_B] = i[:, None] // DEC_T == np.arange(DEC_B)[None, :]
    c[:, C_ONE] = 1.0
    for h in range(H_A):
        c[h, C_HSEL + h * P:C_HSEL + (h + 1) * P] = 1.0
        c[h, C_HS16 + h * DEC_T:C_HS16 + (h + 1) * DEC_T] = 1.0
        c[h * DEC_T:(h + 1) * DEC_T, C_OMASK + h * DH:C_OMASK + (h + 1) * DH] = 1.0
    x = np.arange(240)[None, :] - 112
    c[:, C_WIN:C_WIN + 240] = np.where((x >= 0) & (x <= i[:, None] % DEC_T), 0.0, NEG)
    c[:, C_TSEL:C_TSEL + DEC_T] = i[:, None] % DEC_T == np.arange(DEC_T)[None, :]
    t = np.arange(T)
    c[:, C_SCAN:] = np.where(np.where(t < SEQ, t % P, t % DEC_T) == 0, 0.0, 1.0)
    return c


def build(nc, x_prompt, x_sample, cache_fox_k, cache_fox_v, cache_fox_logf, state_gla, cache_ffn_conv,
          p_prompt, p_sample, w_in, b_fgate, w_a2, b_a2, g_gla, w_a_out, w_b_out, w_o, ln1_g, ln1_b,
          w_up, conv_w, conv_b, w_down, ln2_g, ln2_b, w_pl, w_plg, ln3_g, ln3_b, consts,
          y_p, y_s, fk_p, fv_p, fl_p, st_p, cv_p, fk_s, fv_s, fl_s, st_s, cv_s):
    ctx = ExitStack()
    with ctx:
        def sem(name):
            return ctx.enter_context(nc.semaphore(name))

        M_ALL = 52900
        sb = ctx.enter_context(nc.sbuf_tensor("sb", [P, M_ALL], F32))
        ps = ctx.enter_context(nc.psum_tensor("ps", [P, 4, 1024], F32))

        def at(off, *dims, parts=P):
            n = int(np.prod(dims))
            assert off + n <= M_ALL, (off, n)
            v = sb[0:parts, off:off + n]
            if len(dims) == 2:
                v = v.rearrange("p (a b) -> p a b", a=dims[0])
            if len(dims) == 3:
                v = v.rearrange("p (a b c) -> p a b c", a=dims[0], b=dims[1])
            return v

        off = {}

        def place(base, *items):
            for name, n in items:
                off[name] = base
                base += n
            return base

        e0 = place(0, ("keep", C_KEEP + 5), ("cw", 176), ("cacheT", 704), ("cols", 192), ("stat", 256))
        e0 = place(e0, ("ring", W_SLOTS * 1024), ("xT", 9216), ("oaT", 4608))
        ea = place(e0, ("qT", 4608), ("kT", 4608), ("va", 4608), ("work", 0))
        PSR = ea
        place(PSR, ("xs", 3072), ("cvst", 5632), ("lfp", 128))
        place(PSR, ("cb", 2048), ("dg", 2048), ("S", 2048), ("PT", 2048), ("oab", 1024))
        place(off["S"], ("fz", 1152), ("fa", 1152), ("kst", 1024))
        e1 = place(PSR, ("qbd", 1312), ("kp", 2048), ("vp", 2048), ("kpT", 2048), ("sN", 256), ("sP", 768),
                   ("sPT", 768), ("om", 1024))
        e1 = max(e1, PSR + 10304)
        e1 = place(e1, ("hsel", C_SCAN - C_HSEL), ("negC", 1152), ("negCs", 2048 + 128), ("lfo", 72), ("cwst", 512),
                   ("wf", 64))
        assert e1 <= M_ALL, e1
        off["obT"] = M_ALL - 9216
        eb = place(e0, ("qb", 1152), ("kb", 1152), ("zb", 1152), ("b", 1152), ("qs", 1152), ("X", 2 * 1152),
                   ("ks", 1152), ("AT", 1152), ("vb", 2304), ("St", 768), ("S0", 2048), ("ktok", 1024),
                   ("ksm", 1024), ("qsm", 1152), ("on", 768), ("scan", 1152), ("a1T", 1152), ("wa2", 512),
                   ("wa1", 128), ("sq", 256))
        assert eb <= off["obT"], (eb, off["obT"])
        place(e0, ("mT", 9216), ("wo", 8192), ("sg", 4 * 384 * 2))
        off["x1T"], off["x1"] = off["xT"], off["obT"]
        place(off["oaT"], ("xin", 2048), ("g1", 1024), ("b1", 1024))
        place(e0, ("hT", 9216), ("wd", 8192), ("U", 4680))
        assert off["U"] + 4680 <= off["x1"]
        place(off["oaT"], ("y", 2340), ("cn", 72), ("cno", 512))
        off["plg"] = off["x1T"]
        place(off["U"], ("g2", 1024), ("b2", 1024), ("g3", 1024), ("b3", 1024))
        place(off["oaT"], ("pl", 2048))
        place(off["oaT"] + 3072, ("pin", 512), ("pT", 512))
        place(off["hT"], ("x2T", 2048), ("sge", 2048), ("z3", 3072))

        keep = at(off["keep"], C_KEEP)
        ident = keep[:, C_ID:C_ID + P]
        levm = keep[:, C_LEV:C_LEV + 7 * P].bitcast(U32)
        causal = keep[:, C_CAUSAL:C_CAUSAL + P]
        neg1, nhalf, one = keep[:, C_NEG1:C_NEG1 + 1], keep[:, C_NHALF:C_NHALF + 1], keep[:, C_ONE:C_ONE + 1]
        bmask = keep[:, C_BM:C_BM + DEC_B]
        hc = at(off["hsel"], C_SCAN - C_HSEL)
        hsel = hc[0:H_A, 0:H_A * P]
        omask = hc[:, C_OMASK - C_HSEL:C_OMASK - C_HSEL + 512]
        win = hc[:, C_WIN - C_HSEL:C_WIN - C_HSEL + 240]
        hs16 = hc[0:H_A, C_HS16 - C_HSEL:C_HS16 - C_HSEL + P]
        tsel = hc[:, C_TSEL - C_HSEL:C_TSEL - C_HSEL + DEC_T]
        scanm = at(off["scan"], T)

        xT = at(off["xT"], KT, T)
        ring = at(off["ring"], W_SLOTS, KT * P).rearrange("p s (k c) -> p s k c", k=KT)
        oaT = at(off["oaT"], 4, T)
        cols = at(off["cols"], 192)
        bfg, ba2, ggla = cols[0:H_A, 0:1], cols[:, 4:8], cols[:, 8:16]
        dl = cols[:, 16:32]
        stat = at(off["stat"], 256)
        rs, mx, nm, ri = stat[:, 0:4], stat[:, 4:8], stat[:, 8:12], stat[:, 12:16]
        ss, ms, rstd = stat[:, 16:32], stat[:, 32:48], stat[:, 48:64]
        mxb, rsb = stat[:, 64:68], stat[:, 68:72]
        bnst = stat[:, 80:80 + 48].rearrange("p (a b) -> p a b", a=4)
        mv = stat[:, 130:138].rearrange("p (a b) -> p a b", a=4)
        lve, lrs = stat[:, 140:144], stat[:, 144:148]

        xs = at(off["xs"], 3, 1024)
        qT, kT, va = at(off["qT"], 4, T), at(off["kT"], 4, T), at(off["va"], NT, 512)
        cwT = at(off["cw"], 4, 44)
        cacheT = at(off["cacheT"], 44, 16)
        cvst = at(off["cvst"], 5632, parts=16)
        cwst = at(off["cwst"], 4, P, parts=44)
        lfp = at(off["lfp"], 16, H_A)
        wf = at(off["wf"], KT, H_A)
        fz, fa = at(off["fz"], T, parts=H_A), at(off["fa"], T, parts=H_A)
        negC = at(off["negC"], T, parts=H_A)
        negCs = at(off["negCs"], 2176, parts=H_A)
        lfo = at(off["lfo"], NT, H_A)
        kst = at(off["kst"], 2, 512)
        cb, dg = at(off["cb"], 2, 1024), at(off["dg"], 2, 1024)
        S, PT = at(off["S"], 2, 1024), at(off["PT"], 2, 1024)
        oab = at(off["oab"], NP, P)
        qbd = at(off["qbd"], 2, 656)
        kp, vp, kpT = at(off["kp"], 2, 1024), at(off["vp"], 2, 1024), at(off["kpT"], 2, 1024)
        sN, sP, sPT, om = at(off["sN"], 2, 128), at(off["sP"], 2, 384), at(off["sPT"], 2, 384), at(off["om"], 2, 512)

        qb, kb, zb, b16, qs = (at(off[n], T) for n in ("qb", "kb", "zb", "b", "qs"))
        X = at(off["X"], 2, T)
        ks = at(off["ks"], T)
        AT = at(off["AT"], T)
        vb, St = at(off["vb"], NT, DV), at(off["St"], 3, DV)
        S0 = at(off["S0"], DEC_B, DV)
        ktok, ksm = at(off["ktok"], NP, P), at(off["ksm"], DEC_B, P)
        qsm = at(off["qsm"], 1152)
        on = at(off["on"], 3, DV)
        a1T = at(off["a1T"], T, parts=RANK)
        wa2 = at(off["wa2"], 512, parts=RANK)
        wa1 = at(off["wa1"], KT, RANK)
        sq = at(off["sq"], 256)
        obT = at(off["obT"], 8, T)
        mT = at(off["mT"], KT, T)
        wo = at(off["wo"], KT, D)
        sg = at(off["sg"], 2, 4, 384)
        x1T, x1 = at(off["x1T"], KT, T), at(off["x1"], NT, D)
        xin, g1, b1 = at(off["xin"], 2, D), at(off["g1"], D), at(off["b1"], D)
        hT, wd = at(off["hT"], 8, T), at(off["wd"], 8, D)
        U = at(off["U"], 2, 2, 1170)
        y = at(off["y"], 2, 1170)
        cn, cno = at(off["cn"], 2, 2, 18), at(off["cno"], 2, 256, parts=18)
        plg, pl = at(off["plg"], KT, D), at(off["pl"], 2, D)
        g2, b2, g3, b3 = (at(off[n], D) for n in ("g2", "b2", "g3", "b3"))
        pin, pT = at(off["pin"], 2, PLE), at(off["pT"], 2, 2, P)
        x2T, sge, z3 = at(off["x2T"], 2, KT, P), at(off["sge"], 2, D), at(off["z3"], 3, D)

        full = [sem(f"psum_full{s}") for s in range(4)]
        free = [sem(f"psum_free{s}") for s in range(4)]
        turn = {}

        def take(pe, key):
            n = len(turn)
            turn[key] = n
            if n >= 4:
                pe.wait_ge(free[n % 4], n // 4)
            return ps[:, n % 4, :]

        def filled(key):
            return full[turn[key] % 4]

        def drained(key):
            return free[turn[key] % 4]

        def count(key):
            return turn[key] // 4 + 1

        def product(eng, key):
            eng.wait_ge(filled(key), count(key))
            return ps[:, turn[key] % 4, :]

        def copied(eng, *keys):
            last = {}
            for k in keys:
                last[turn[k] % 4] = max(last.get(turn[k] % 4, 0), count(k))
            for s, v in last.items():
                eng.wait_ge(free[s], v)

        def past_pe(eng, *keys):
            last = {}
            for k in keys:
                last[turn[k] % 4] = max(last.get(turn[k] % 4, 0), count(k))
            for s, v in last.items():
                eng.wait_ge(full[s], v)

        chunks = []

        def w_cols(w, c0, kt=KT):
            return w[0].rearrange("(k p) n -> p k n", p=P)[:, :, c0:c0 + P], kt

        for j in range(4):
            chunks.append((("qa", j), *w_cols(w_in, O_Q + j * P)))
        for j in range(4):
            chunks.append((("ka", j), *w_cols(w_in, O_K + j * P)))
        for j in range(4):
            chunks.append((("va", j), *w_cols(w_in, O_V + j * P)))
        for h in range(H_B):
            chunks.append((("qb", h), *w_cols(w_in, O_QB + h * P)))
            chunks.append((("kb", h), *w_cols(w_in, O_KB + h * P)))
            for c in range(2):
                chunks.append((("rb", h, c), *w_cols(w_in, O_RB + h * DV + c * P)))
            for c in range(2):
                chunks.append((("vb", h, c), *w_cols(w_in, O_VB + h * DV + c * P)))
        for j in range(KT):
            chunks.append((("ga", j), *w_cols(w_in, O_GA + j * P)))
            chunks.append((("gb", j), *w_cols(w_in, O_GB + j * P)))
            chunks.append((("ya", j), *w_cols(w_a_out, j * P, 4)))
            chunks.append((("yb", j), *w_cols(w_b_out, j * P)))
        for c in range(NC_FF):
            chunks.append((("uv", c), *w_cols(w_up, c * P)))
            chunks.append((("ug", c), *w_cols(w_up, D_FF + c * P)))
        w_index = {c[0]: n for n, c in enumerate(chunks)}
        w_last = {}
        w_in_sem = [sem(f"weights_in{s}") for s in range(W_SLOTS)]

        def weights(pe, name):
            n = w_index[name]
            pe.wait_ge(w_in_sem[n % W_SLOTS], 16 * (n // W_SLOTS + 1))
            return ring[:, n % W_SLOTS]

        s_const = sem("const_in")
        s_const2 = sem("const2_in")
        s_small = sem("small_in")
        s_x = [sem(f"x_in{i}") for i in range(3)]
        s_cv = sem("conv_cache_in")
        s_lf = sem("logf_past_in")
        s_kv = [sem(f"kv_past_in{i}") for i in range(2)]
        s_b = sem("gla_small_in")
        s_s0 = sem("state_in")
        s_wo = sem("wo_in")
        s_g1 = sem("ln1_in")
        s_xin = [sem(f"x_again_in{i}") for i in range(2)]
        s_wd = sem("wdown_in")
        s_ple = sem("embedding_weights_in")
        s_pin = [sem(f"p_in{i}") for i in range(2)]
        s_o = sem("stores_done")
        s_ok = [sem(f"k_stored{i}") for i in range(2)]
        s_ov = sem("v_stored")
        s_ol = sem("logf_stored")
        s_cols = sem("gla_columns_in")
        s_ost = sem("state_stored")
        s_ocn = [sem(f"conv_stored{i}") for i in range(2)]
        s_oy = [sem(f"y_stored{i}") for i in range(3)]

        s_dve = sem("dve_step")
        s_act = sem("act_step")
        s_pool = sem("pool_step")
        s_fz = sem("fgate_exp")
        s_lf8 = sem("logf_ready")
        s_negc = sem("negC_ready")
        s_dg = sem("diag_bias_ready")
        s_max = sem("row_max_ready")
        s_exp = sem("probs_ready")
        s_exs = sem("sample_probs_ready")
        s_qbd = sem("qbd_ready")
        s_smx = sem("sample_max_ready")
        s_lnz = sem("gate_log_ready")
        s_bsc = sem("cumsum_ready")
        s_kd = sem("k_decay_log_ready")
        s_ee = sem("decays_ready")
        s_qs = sem("qs_ready")
        s_ksr = sem("ks_ready")
        s_at0 = sem("AT_cleared")
        s_qsm = sem("qsm_ready")
        s_xl = sem("level_log_ready")
        s_xe = sem("level_exp_ready")
        s_xm = sem("level_ready")
        s_ssq = sem("square_sum_ready")
        s_rst = sem("rstd_ready")
        s_mt = sem("merged_ready")
        s_var = sem("ln_var_ready")
        s_lve = sem("ln_var_eps_ready")
        s_msq = sem("mean_square_ready")
        s_lrs = sem("ln_rstd_ready")
        s_x1 = sem("x1_ready")
        s_u0 = sem("U_cleared")
        s_up = sem("cache_columns_ready")
        s_ygt = sem("conv_gate_ready")
        s_gel = sem("gelu_ready")
        s_cnr = sem("conv_new_ready")
        s_hT = sem("h_ready")
        s_x2 = sem("x2_ready")
        s_y = sem("y_ready")

        block = ctx.enter_context(nc.Block())

        def store_new(eng, c):
            copied(eng, ("cn", c))
            src = cno[:, c % 2, :].rearrange("r (v p) -> r v p", v=2)
            for rows_, dst in (((0, 2), cv_p[0, 0]), ((2, 18), cv_s[0].rearrange("b r c -> (b r) c"))):
                eng.dma_start(dst.rearrange("r (v c) -> r v c", v=2)[:, :, c * P:(c + 1) * P], src[rows_[0]:rows_[1]])\
                    .then_inc(s_ocn[c % 2], 16)

        UNITS = [(h, i) for h in range(H_A) for i in reversed(range(NP))]

        @block.tensor
        def _(pe):
            mm, tr = pe.matmul, pe.transpose

            def chain(out, pairs):
                for n, (l, r) in enumerate(pairs):
                    m = mm(out, l, r, start=(n == 0), stop=(n == len(pairs) - 1))
                return m

            def thirds(key, chunk, rhs, kt=KT, lhs=None):
                w = weights(pe, chunk) if lhs is None else lhs
                for g in range(3):
                    o = take(pe, (*key, g))
                    t = slice(g * THIRD, (g + 1) * THIRD)
                    m = chain(o[0:w.shape[-1], 0:THIRD], [(w[:, k, :], rhs[:, k, t]) for k in range(kt)])
                    m.then_inc(filled((*key, g)), 1)
                if chunk is not None:
                    w_last[chunk] = (*key, 2)

            pe.wait_ge(s_const, 16)
            for n in range(NT):
                pe.wait_ge(s_x[n % 3], 16 * (n // 3 + 1))
                o = take(pe, ("xT", n))
                for k in range(KT):
                    m = tr(o[:, k * P:(k + 1) * P], xs[:, n % 3, k * P:(k + 1) * P], ident)
                m.then_inc(filled(("xT", n)), 1)
            pe.wait_ge(s_cv, 32 + 16)
            o = take(pe, "cacheT")
            for c in range(44):
                m = tr(o[:, c * 16:(c + 1) * 16], cvst[:, c * P:(c + 1) * P], ident[0:16, 0:16])
            m.then_inc(filled("cacheT"), 1)
            o = take(pe, "cwT")
            for c in range(4):
                m = tr(o[:, c * 44:(c + 1) * 44], cwst[:, c, :], ident[0:44, 0:44])
            m.then_inc(filled("cwT"), 1)
            pe.wait_ge(s_lf, 16)
            for n in range(2):
                o = take(pe, ("lfp", n))
                for c in range(8):
                    m = tr(o[0:H_A, c * P:(c + 1) * P], lfp[:, n * 8 + c, :], ident)
                m.then_inc(filled(("lfp", n)), 1)
            copied(pe, *[("xT", n) for n in range(NT)])
            pe.wait_ge(s_small, 32)
            thirds(("f",), None, xT, lhs=wf)
            for j in range(4):
                thirds(("qa", j), ("qa", j), xT)
            for j in range(4):
                thirds(("ka", j), ("ka", j), xT)
            for j in range(4):
                weights(pe, ("va", j))
            for n in range(NT):
                o = take(pe, ("va", n))
                m = chain(o[:, 0:512], [(xT[:, k, n * P:(n + 1) * P], ring[:, :, k, :]) for k in range(KT)])
                m.then_inc(filled(("va", n)), 1)
            for j in range(4):
                w_last[("va", j)] = ("va", NT - 1)
            pe.wait_ge(s_lf8, 1)
            o = take(pe, "lfT")
            for n in range(NT):
                m = tr(o[:, n * H_A:(n + 1) * H_A], fz[:, n * P:(n + 1) * P], ident[0:H_A, 0:H_A])
            m.then_inc(filled("lfT"), 1)
            copied(pe, *[("ka", j, g) for j in range(4) for g in range(3)])
            for n in range(NT):
                o = take(pe, ("kt", n))
                for j in range(4):
                    m = tr(o[:, j * P:(j + 1) * P], kT[:, j, n * P:(n + 1) * P], ident)
                m.then_inc(filled(("kt", n)), 1)

            def bias_rows(h):
                if h == 0:
                    pe.wait_ge(s_negc, 1)
                    pe.wait_ge(s_const2, 16)
                o = take(pe, ("cb", h))
                for c in range(2):
                    m = mm(o[:, c * 512:(c + 1) * 512], hsel[:, h * P:(h + 1) * P], negC[:, c * 512:(c + 1) * 512],
                           start=True, stop=True)
                m.then_inc(filled(("cb", h)), 1)

            def scores(u):
                h, i = UNITS[u]
                r = (h % 2) * DH
                o = take(pe, ("s", u))
                n = (i + 1) * P
                for c in range(0, n, 512):
                    e = min(n, c + 512)
                    m = mm(o[:, c:e], qT[r:r + DH, h // 2, i * P:(i + 1) * P], kT[r:r + DH, h // 2, c:e],
                           start=True, stop=True)
                m.then_inc(filled(("s", u)), 1)

            def turn_probs(u):
                h, i = UNITS[u]
                pe.wait_ge(s_exp, u + 1)
                o = take(pe, ("pt", u))
                for c in range(i + 1):
                    m = tr(o[:, c * P:(c + 1) * P], S[:, u % 2, c * P:(c + 1) * P], ident)
                m.then_inc(filled(("pt", u)), 1)

            def probs_v(u):
                h, i = UNITS[u]
                copied(pe, ("pt", u))
                o = take(pe, ("pv", u))
                chain(o[:, 0:DH], [(PT[:, u % 2, c * P:(c + 1) * P], va[:, c, h * DH:(h + 1) * DH])
                                   for c in range(i + 1)]).then_inc(filled(("pv", u)), 1)
                if h % 2 == 1 and i == 0:
                    copied(pe, *[("pv", v) for v in range(u - 15, u + 1)])
                    o = take(pe, ("oT", h // 2))
                    for c in range(NP):
                        m = tr(o[:, c * P:(c + 1) * P], oab[:, c, :], ident)
                    m.then_inc(filled(("oT", h // 2)), 1)

            copied(pe, ("qa", 3, 0), ("qa", 3, 1), ("qa", 3, 2), *[("va", n) for n in range(NT)])
            bias_rows(0)
            NU = len(UNITS)
            for u in range(NU + 2):
                if u < NU:
                    if u % 8 == 6 and UNITS[u][0] + 1 < H_A:
                        bias_rows(UNITS[u][0] + 1)
                    scores(u)
                if 1 <= u <= NU:
                    turn_probs(u - 1)
                if u >= 2:
                    probs_v(u - 2)

            def past_keys(b):
                pe.wait_ge(s_kv[b % 2], 32 * (b // 2 + 1))
                o = take(pe, ("kpT", b))
                for s in range(2):
                    for j in range(4):
                        m = tr(o[:, j * 256 + s * P:j * 256 + (s + 1) * P], kp[:, b % 2, s * 512 + j * P:s * 512 + (j + 1) * P], ident)
                m.then_inc(filled(("kpT", b)), 1)

            def sample_scores(b):
                pe.wait_ge(s_qbd, b + 1)
                copied(pe, ("kpT", b))
                o = take(pe, ("ss", b))
                chain(o[:, 0:256], [(qbd[:, b % 2, j * P:(j + 1) * P], kpT[:, b % 2, j * 256:(j + 1) * 256]) for j in range(4)]
                      + [(hs16, negCs[:, b * 256:(b + 1) * 256])])
                chain(o[:, 256:384], [(qbd[:, b % 2, j * P:(j + 1) * P], kT[:, j, SEQ:T]) for j in range(4)]
                      + [(hs16, negCs[:, 2048:2176])]).then_inc(filled(("ss", b)), 1)

            def sample_turn(b):
                pe.wait_ge(s_exs, b + 1)
                o = take(pe, ("spt", b))
                for c in range(3):
                    m = tr(o[:, c * P:(c + 1) * P], sP[:, b % 2, c * P:(c + 1) * P], ident)
                m.then_inc(filled(("spt", b)), 1)

            def sample_v(b):
                copied(pe, ("spt", b))
                o = take(pe, ("spv", b))
                v = [vp[:, b % 2, 0:512], vp[:, b % 2, 512:1024], va[:, NP, :]]
                chain(o[:, 0:512], [(sPT[:, b % 2, c * P:(c + 1) * P], v[c]) for c in range(3)]).then_inc(filled(("spv", b)), 1)

            def sample_out(b):
                copied(pe, ("spv", b))
                o = take(pe, ("soT", b))
                for j in range(4):
                    m = mm(o[:, j * 16:(j + 1) * 16], om[:, b % 2, j * P:(j + 1) * P], tsel, start=True, stop=True)
                m.then_inc(filled(("soT", b)), 1)

            for b in range(DEC_B + 3):
                if 2 <= b <= DEC_B + 1:
                    sample_v(b - 2)
                if b < DEC_B:
                    past_keys(b)
                    sample_scores(b)
                if 1 <= b <= DEC_B:
                    sample_turn(b - 1)
                if b >= 3:
                    sample_out(b - 3)

            pe.wait_ge(s_b, 16 * 3)
            thirds(("a1",), None, xT, lhs=wa1)
            copied(pe, ("a1", 0), ("a1", 1), ("a1", 2))
            for h in range(H_B):
                thirds(("qb", h), ("qb", h), xT)
                thirds(("kb", h), ("kb", h), xT)
                for g in range(3):
                    o = take(pe, ("la", h, g))
                    mm(o[:, 0:THIRD], wa2[:, h * P:(h + 1) * P], a1T[:, g * THIRD:(g + 1) * THIRD],
                       start=True, stop=True).then_inc(filled(("la", h, g)), 1)
                thirds(("rb", h, 0), ("rb", h, 0), xT)
                thirds(("rb", h, 1), ("rb", h, 1), xT)
                pe.wait_ge(s_ksr, h + 1)
                o = take(pe, ("kst", h, 0))
                for n in range(NP):
                    m = tr(o[:, n * P:(n + 1) * P], ks[:, n * P:(n + 1) * P], ident)
                m.then_inc(filled(("kst", h, 0)), 1)
                o = take(pe, ("kst", h, 1))
                tr(o[:, 0:P], ks[:, SEQ:T], ident).then_inc(filled(("kst", h, 1)), 1)

                def level(l):
                    if l < 7:
                        pe.wait_ge(s_xm, 7 * h + l + 1)
                        a = c = X[:, l % 2, :]
                    else:
                        a, c = kb, qb
                    o = take(pe, ("lv", h, l, 0))
                    for n in range(NP):
                        t = slice(n * P, (n + 1) * P)
                        m = mm(o[:, t], a[:, t], c[:, t], start=True, stop=True)
                    m.then_inc(filled(("lv", h, l, 0)), 1)
                    if l >= 3:
                        o = take(pe, ("lv", h, l, 1))
                        mm(o[:, 0:P], a[:, SEQ:T], c[:, SEQ:T], start=True, stop=True)\
                            .then_inc(filled(("lv", h, l, 1)), 1)

                weights(pe, ("vb", h, 0))
                weights(pe, ("vb", h, 1))
                s0 = w_index[("vb", h, 0)] % W_SLOTS
                assert s0 % 2 == 0
                for n in range(NT):
                    o = take(pe, ("vb", h, n))
                    chain(o[:, 0:DV], [(xT[:, k, n * P:(n + 1) * P], ring[:, s0:s0 + 2, k, :]) for k in range(KT)])\
                        .then_inc(filled(("vb", h, n)), 1)
                    if n < 8:
                        level(n)
                w_last[("vb", h, 0)] = w_last[("vb", h, 1)] = ("vb", h, NT - 1)
                copied(pe, ("kst", h, 0), ("kst", h, 1), *[("lv", h, 7, g) for g in range(2)],
                       *[("lv", h, l, 0) for l in range(8)], *[("vb", h, n) for n in range(NT)])
                pe.wait_ge(s_qs, h + 1)

                def turn_out(n):
                    copied(pe, ("o", h, n))
                    o = take(pe, ("ot", h, n))
                    for c in range(2):
                        m = tr(o[:, c * P:(c + 1) * P], on[:, n % 3, c * P:(c + 1) * P], ident)
                    m.then_inc(filled(("ot", h, n)), 1)

                for n in range(NP):
                    o = take(pe, ("u", h, n))
                    mm(o[:, 0:DV], ktok[:, n, :], vb[:, n, :], start=True, stop=True).then_inc(filled(("u", h, n)), 1)
                    t = slice(n * P, (n + 1) * P)
                    pairs = [(AT[:, t], vb[:, n, :])]
                    if n > 0:
                        copied(pe, ("u", h, n - 1))
                        pairs.append((qs[:, t], St[:, n % 3, :]))
                    o = take(pe, ("o", h, n))
                    chain(o[:, 0:DV], pairs).then_inc(filled(("o", h, n)), 1)
                    if n >= 2:
                        turn_out(n - 2)
                pe.wait_ge(s_s0, 16 * (h + 1))
                pe.wait_ge(s_qsm, h + 1)
                o = take(pe, ("o", h, NP))
                chain(o[:, 0:DV], [(AT[:, SEQ:T], vb[:, NP, :])]
                      + [(qsm[:, b * P:(b + 1) * P], S0[:, b, :]) for b in range(DEC_B)])\
                    .then_inc(filled(("o", h, NP)), 1)
                turn_out(NP - 2)
                for c in range(4):
                    o = take(pe, ("us", h, c))
                    for b in range(2):
                        m = mm(o[:, b * DV:(b + 1) * DV], ksm[:, 2 * c + b, :], vb[:, NP, :], start=True, stop=True)
                    m.then_inc(filled(("us", h, c)), 1)
                    if c < 2:
                        turn_out(NP - 1 + c)

            copied(pe, *[("ot", 3, n) for n in range(NT)], *[("soT", b) for b in range(DEC_B)],
                   *[("oT", j) for j in range(4)])
            for j in range(KT):
                wg, wh, wy, wz = (weights(pe, (n, j)) for n in ("ga", "gb", "ya", "yb"))
                for g in range(3):
                    t = slice(g * THIRD, (g + 1) * THIRD)
                    for name, w, r, kt in (("ga", wg, xT, KT), ("gb", wh, xT, KT), ("ya", wy, oaT, 4), ("yb", wz, obT, KT)):
                        o = take(pe, (name, j, g))
                        chain(o[:, 0:THIRD], [(w[:, k, :], r[:, k, t]) for k in range(kt)])\
                            .then_inc(filled((name, j, g)), 1)
                for name in ("ga", "gb", "ya", "yb"):
                    w_last[(name, j)] = (name, j, 2)

            pe.wait_ge(s_wo, 16)

            def turn_x1(n):
                pe.wait_ge(s_x1, n + 1)
                o = take(pe, ("x1T", n))
                for k in range(KT):
                    m = tr(o[:, k * P:(k + 1) * P], x1[:, n, k * P:(k + 1) * P], ident)
                m.then_inc(filled(("x1T", n)), 1)

            pe.wait_ge(s_mt, 3 * KT)
            for n in range(NT):
                o = take(pe, ("wo", n))
                for c in range(2):
                    m = chain(o[:, c * 512:(c + 1) * 512],
                              [(mT[:, k, n * P:(n + 1) * P], wo[:, k, c * 512:(c + 1) * 512]) for k in range(KT)])
                m.then_inc(filled(("wo", n)), 1)
                if n >= 1:
                    turn_x1(n - 1)
            turn_x1(NT - 1)
            copied(pe, *[("x1T", n) for n in range(NT)])

            def turn_new(c):
                pe.wait_ge(s_cnr, c + 1)
                o = take(pe, ("cn", c))
                for v in range(2):
                    m = tr(o[0:18, v * P:(v + 1) * P], cn[:, c % 2, v, :], ident)
                m.then_inc(filled(("cn", c)), 1)

            def embed_turn(n):
                pe.wait_ge(s_x2, n + 1)
                o = take(pe, ("x2T", n))
                for k in range(KT):
                    m = tr(o[:, k * P:(k + 1) * P], x1[:, n, k * P:(k + 1) * P], ident)
                m.then_inc(filled(("x2T", n)), 1)
                pe.wait_ge(s_pin[n % 2], 16 * (n // 2 + 1))
                o = take(pe, ("pT", n))
                for k in range(2):
                    m = tr(o[:, k * P:(k + 1) * P], pin[:, n % 2, k * P:(k + 1) * P], ident)
                m.then_inc(filled(("pT", n)), 1)

            def embed(n):
                if n == 0:
                    pe.wait_ge(s_ple, 16 * 6)
                copied(pe, ("x2T", n), ("pT", n))
                for name, w, a, kt in (("pg", plg, x2T, KT), ("pp", pl, pT, 2)):
                    o = take(pe, (name, n))
                    for c in range(2):
                        m = chain(o[:, c * 512:(c + 1) * 512],
                                  [(a[:, n % 2, k, :], w[:, k, c * 512:(c + 1) * 512]) for k in range(kt)])
                    m.then_inc(filled((name, n)), 1)

            c0 = 0
            for grp, size in enumerate(FF_GROUPS):
                for c in range(c0, c0 + size):
                    thirds(("uv", c), ("uv", c), x1T)
                    thirds(("ug", c), ("ug", c), x1T)
                    if c > c0:
                        turn_new(c - 1)
                turn_new(c0 + size - 1)
                pe.wait_ge(s_hT, c0 + size)
                pe.wait_ge(s_wd, 16 * (grp + 1))
                last = grp == len(FF_GROUPS) - 1
                for n in range(NT):
                    o = take(pe, ("dn", grp, n))
                    for c in range(2):
                        m = chain(o[:, c * 512:(c + 1) * 512],
                                  [(hT[:, k, n * P:(n + 1) * P], wd[:, k, c * 512:(c + 1) * 512]) for k in range(size)])
                    m.then_inc(filled(("dn", grp, n)), 1)
                c0 += size
            embed_turn(0)
            for n in range(NT):
                if n + 1 < NT:
                    embed_turn(n + 1)
                embed(n)

        @block.scalar
        def _(act):
            steps = [0]

            def link(ins):
                steps[0] += 1
                ins.then_inc(s_act, 1)
                act.wait_ge(s_act, steps[0])

            def copy(out, in_, scale=1.0):
                return act.activation(out, in_, ACT.Copy, scale=scale)

            for n in range(1, NT, 2):
                o = product(act, ("xT", n))
                copy(xT[:, :, n * P:(n + 1) * P], o.rearrange("p (k t) -> p k t", k=KT)).then_inc(drained(("xT", n)), 1)
            o = product(act, "cacheT")
            copy(cacheT, o[:, 0:704].rearrange("p (c r) -> p c r", c=44)).then_inc(drained("cacheT"), 1)
            act.wait_ge(s_small, 32)
            past_pe(act, ("xT", NT - 1), "cacheT")
            for g in range(3):
                o = product(act, ("f", g))
                act.activation(fz[:, g * THIRD:(g + 1) * THIRD], o[0:H_A, 0:THIRD], ACT.Identity, bias=bfg)\
                    .then_inc(drained(("f", g)), 1)
            copied(act, ("f", 0), ("f", 1), ("f", 2))
            link(act.activation(fa, fz, ACT.Abs))
            link(act.activation(fa, fa, ACT.Exp, scale=-1.0))
            act.activation(fa, fa, ACT.Ln, bias=one[0:H_A, :]).then_inc(s_fz, 1)
            for j in range(4):
                for g in range(3):
                    o = product(act, ("qa", j, g))
                    copy(qT[:, j, g * THIRD:(g + 1) * THIRD], o[:, 0:THIRD], DH ** -0.5).then_inc(drained(("qa", j, g)), 1)
            for n in range(NT):
                o = product(act, ("va", n))
                copy(va[:, n, :], o[:, 0:512]).then_inc(drained(("va", n)), 1)

            def bias_rows(h):
                if h == 0:
                    copied(act, ("kt", NT - 1), ("kt", NT - 2))
                if h >= 2:
                    act.wait_ge(s_max, NP * (h - 1))
                    act.wait_ge(s_dg, h - 1)
                o = product(act, ("cb", h))
                copy(cb[:, h % 2, :], o).then_inc(drained(("cb", h)), 1)

            def probs(u):
                h, i = UNITS[u]
                act.wait_ge(s_max, u + 1)
                n = (i + 1) * P
                act.activation(S[:, u % 2, 0:n], S[:, u % 2, 0:n], ACT.Exp, bias=nm[:, u % 4:u % 4 + 1],
                               accum_out=rs[:, u % 4:u % 4 + 1]).then_inc(s_exp, 1)

            def copy_probs(u):
                if u % 2 == 1:
                    h, i = UNITS[u]
                    o = product(act, ("pt", u))
                    if u >= 2:
                        past_pe(act, ("pv", u - 2))
                    copy(PT[:, u % 2, 0:(i + 1) * P], o[:, 0:(i + 1) * P]).then_inc(drained(("pt", u)), 1)

            NU = len(UNITS)
            bias_rows(0)
            for u in range(NU + 2):
                if u < NU:
                    if u % 8 == 6 and UNITS[u][0] + 1 < H_A:
                        bias_rows(UNITS[u][0] + 1)
                    if u >= 4:
                        copied(act, ("pv", u - 4))
                    probs(u)
                if 1 <= u <= NU:
                    copy_probs(u - 1)
                if u >= 2:
                    h, i = UNITS[u - 2]
                    if h % 2 == 1 and i == 0:
                        o = product(act, ("oT", h // 2))
                        copy(oaT[:, h // 2, 0:SEQ], o).then_inc(drained(("oT", h // 2)), 1)

            past_pe(act, ("pv", NU - 1), ("oT", 3))
            for b in range(DEC_B + 1):
                if b < DEC_B:
                    o = product(act, ("kpT", b))
                    if b >= 2:
                        past_pe(act, ("ss", b - 2))
                    copy(kpT[:, b % 2, :], o).then_inc(drained(("kpT", b)), 1)
                    act.wait_ge(s_smx, b + 1)
                    if b >= 2:
                        past_pe(act, ("spt", b - 2))
                        copied(act, ("spv", b - 2))
                    o = product(act, ("ss", b))
                    act.activation(sP[:, b % 2, 256:384], sN[:, b % 2, :], ACT.Exp, bias=nm[:, b % 2:b % 2 + 1],
                                   accum_out=rsb[:, b % 2:b % 2 + 1])
                    act.activation(sP[:, b % 2, 0:256], o[:, 0:256], ACT.Exp, bias=nm[:, b % 2:b % 2 + 1],
                                   accum_out=rs[:, b % 2:b % 2 + 1]).then_inc(s_exs, 1)
                if b >= 1:
                    o = product(act, ("spt", b - 1))
                    if b >= 3:
                        past_pe(act, ("spv", b - 3))
                    copy(sPT[:, (b - 1) % 2, :], o[:, 0:384]).then_inc(drained(("spt", b - 1)), 1)

            act.wait_ge(s_ov, 32)
            act.wait_ge(s_ol, 32)
            act.wait_ge(s_qbd, DEC_B)
            act.wait_ge(s_cols, 32)
            for g in range(3):
                o = product(act, ("a1", g))
                copy(a1T[:, g * THIRD:(g + 1) * THIRD], o[0:RANK, 0:THIRD]).then_inc(drained(("a1", g)), 1)
            for h in range(H_B):
                for g in range(3):
                    o = product(act, ("qb", h, g))
                    copy(qb[:, g * THIRD:(g + 1) * THIRD], o[:, 0:THIRD], DK ** -0.5).then_inc(drained(("qb", h, g)), 1)
                for g in range(3):
                    o = product(act, ("la", h, g))
                    act.activation(zb[:, g * THIRD:(g + 1) * THIRD], o[:, 0:THIRD], ACT.Identity, bias=ba2[:, h:h + 1])\
                        .then_inc(drained(("la", h, g)), 1)
                copied(act, *[("la", h, g) for g in range(3)])
                if h:
                    past_pe(act, ("lv", h - 1, 6, 1))
                link(act.activation(X[:, 0, :], zb, ACT.Abs))
                link(act.activation(X[:, 0, :], X[:, 0, :], ACT.Exp, scale=-1.0))
                act.activation(X[:, 0, :], X[:, 0, :], ACT.Ln, bias=one).then_inc(s_lnz, 1)
                act.wait_ge(s_bsc, h + 1)
                link(act.activation(X[:, 1, :], b16, ACT.Exp, scale=1.0 / TAU))
                if h:
                    copied(act, ("u", h - 1, NP - 1), *[("us", h - 1, c) for c in range(4)])
                act.wait_ge(s_kd, h + 1)
                link(act.activation(ks, ks, ACT.Exp, scale=1.0 / TAU))
                link(act.activation(dl[:, 0:8], b16[:, 0:SEQ].rearrange("p (n t) -> p n t", t=P)[:, :, P - 1], ACT.Exp,
                                    scale=1.0 / TAU))
                act.activation(dl[:, 8:16], b16[:, SEQ:T].rearrange("p (n t) -> p n t", t=DEC_T)[:, :, DEC_T - 1], ACT.Exp,
                               scale=1.0 / TAU).then_inc(s_ee, 1)
                for c in range(2):
                    for g in range(3):
                        o = product(act, ("rb", h, c, g))
                        act.activation(obT[:, 2 * h + c, g * THIRD:(g + 1) * THIRD], o[:, 0:THIRD], ACT.Silu)\
                            .then_inc(drained(("rb", h, c, g)), 1)
                for n in range(NT):
                    if n < 7:
                        act.wait_ge(s_xl, 7 * h + n + 1)
                        t = SEQ if HALVES[n] > 8 else T
                        act.activation(X[:, n % 2, 0:t], X[:, n % 2, 0:t], ACT.Exp, scale=1.0 / TAU).then_inc(s_xe, 1)
                    o = product(act, ("vb", h, n))
                    copy(vb[:, n, :], o[:, 0:DV]).then_inc(drained(("vb", h, n)), 1)
                for n in range(NT):
                    o = product(act, ("o", h, n))
                    if n:
                        act.wait_ge(s_ssq, NT * h + n)
                    act.activation(sq, o[:, 0:DV], ACT.Square, accum_out=ss[:, n:n + 1]).then_inc(s_ssq, 1)
                    act.wait_ge(s_rst, NT * h + n + 1)
                    if n >= 3:
                        past_pe(act, ("ot", h, n - 3))
                    act.activation(on[:, n % 3, :], o[:, 0:DV], ACT.Copy, scale=rstd[:, n:n + 1])\
                        .then_inc(drained(("o", h, n)), 1)

            for j in range(KT):
                for g in range(3):
                    n = 3 * j + g
                    if n >= 2:
                        act.wait_ge(s_mt, n - 1)
                    for q, name in enumerate(("ga", "gb")):
                        o = product(act, (name, j, g))
                        act.activation(sg[:, n % 2, q, :], o[:, 0:THIRD], ACT.Sigmoid).then_inc(drained((name, j, g)), 1)
            for n in range(NT):
                o = product(act, ("x1T", n))
                copy(x1T[:, :, n * P:(n + 1) * P], o.rearrange("p (k t) -> p k t", k=KT)).then_inc(drained(("x1T", n)), 1)

            def new_columns(c):
                o = product(act, ("cn", c))
                if c >= 2:
                    act.wait_ge(s_ocn[c % 2], 32 * (c // 2))
                copy(cno[:, c % 2, :], o[0:18, 0:256]).then_inc(drained(("cn", c)), 1)

            act.wait_ge(s_u0, 1)
            for c in range(NC_FF):
                for v, name in enumerate(("uv", "ug")):
                    if c >= 2:
                        act.wait_ge(s_hT, c - 1)
                        act.wait_ge(s_cnr, c - 1)
                    u = U[:, c % 2, v, :]
                    for g in range(3):
                        o = product(act, (name, c, g))
                        if g < 2:
                            copy(u[:, 2 + g * THIRD:2 + (g + 1) * THIRD], o[:, 0:THIRD]).then_inc(drained((name, c, g)), 1)
                        else:
                            link(copy(u[:, 2 + 2 * THIRD:2 + SEQ], o[:, 0:SEQ - 2 * THIRD]))
                            copy(u[:, 2 + SEQ:2 + SEQ + 144].rearrange("p (b t) -> p b t", t=18)[:, :, 2:18],
                                 o[:, SEQ - 2 * THIRD:THIRD].rearrange("p (b t) -> p b t", t=16)).then_inc(drained((name, c, g)), 1)
                if c not in GROUP_STARTS:
                    new_columns(c - 1)
                act.wait_ge(s_ygt, c + 1)
                act.activation(y[:, 1, 0:1168], y[:, 1, 0:1168], ACT.Gelu_apprx_tanh).then_inc(s_gel, 1)
                if c + 1 in GROUP_STARTS:
                    new_columns(c)

            past_pe(act, ("dn", 2, NT - 1), ("dn", 2, NT - 2), ("dn", 2, NT - 3))

            def turn_in(n):
                o = product(act, ("x2T", n))
                if n >= 2:
                    past_pe(act, ("pg", n - 2))
                copy(x2T[:, n % 2], o.rearrange("p (k t) -> p k t", k=KT)).then_inc(drained(("x2T", n)), 1)
                o = product(act, ("pT", n))
                if n >= 2:
                    past_pe(act, ("pp", n - 2))
                copy(pT[:, n % 2], o[:, 0:256].rearrange("p (k t) -> p k t", k=2)).then_inc(drained(("pT", n)), 1)

            turn_in(0)
            for n in range(NT):
                if n + 1 < NT:
                    turn_in(n + 1)
                o = product(act, ("pg", n))
                if n >= 2:
                    copied(act, ("pp", n - 2))
                act.activation(sge[:, n % 2, :], o, ACT.Sigmoid).then_inc(drained(("pg", n)), 1)

        @block.vector
        def _(dve):
            steps = [0]

            def link(ins):
                steps[0] += 1
                ins.then_inc(s_dve, 1)
                dve.wait_ge(s_dve, steps[0])

            def stt(out, in0, scalar, in1, op0, op1):
                return dve.scalar_tensor_tensor(out=out, in0=in0, scalar=scalar, in1=in1, op0=op0, op1=op1)

            def rows(ap, n, w):
                return ap.rearrange("p (n w) -> p n w", w=w)[:, 0:n]

            for n in range(0, NT, 2):
                o = product(dve, ("xT", n))
                dve.tensor_copy(xT[:, :, n * P:(n + 1) * P], o.rearrange("p (k t) -> p k t", k=KT))\
                    .then_inc(drained(("xT", n)), 1)
            o = product(dve, "cwT")
            dve.tensor_copy(cwT, o[:, 0:176].rearrange("p (a c) -> p a c", a=4)).then_inc(drained("cwT"), 1)
            for n in range(2):
                o = product(dve, ("lfp", n))
                for c in range(4):
                    b = 4 * n + c
                    ins = dve.tensor_tensor_scan(negCs[:, b * 256:(b + 1) * 256], one[0:H_A, :].to_broadcast([H_A, 256]),
                                                 o[0:H_A, c * 256:(c + 1) * 256], 0.0, ALU.mult, ALU.subtract)
                ins.then_inc(drained(("lfp", n)), 1)
            dve.wait_ge(s_fz, 1)
            stt(fz, fz, 0.0, fa, ALU.min, ALU.subtract).then_inc(s_lf8, 1)
            dve.wait_ge(s_lf8, 1)
            copied(dve, ("lfp", 0), ("lfp", 1))
            for b in range(DEC_B):
                dve.tensor_tensor_scan(negCs[:, 2048 + b * 16:2048 + (b + 1) * 16], one[0:H_A, :].to_broadcast([H_A, 16]),
                                       fz[:, SEQ + b * 16:SEQ + (b + 1) * 16], negCs[:, b * 256 + 255:b * 256 + 256],
                                       ALU.mult, ALU.subtract)
            dve.tensor_tensor_scan(negC[:, 0:SEQ], one[0:H_A, :].to_broadcast([H_A, SEQ]), fz[:, 0:SEQ], 0.0,
                                   ALU.mult, ALU.subtract).then_inc(s_negc, 1)
            for j in range(4):
                for g in range(3):
                    o = product(dve, ("ka", j, g))
                    dve.tensor_copy(kT[:, j, g * THIRD:(g + 1) * THIRD], o[:, 0:THIRD]).then_inc(drained(("ka", j, g)), 1)
            o = product(dve, "lfT")
            dve.tensor_copy(lfo, o[:, 0:72].rearrange("p (n h) -> p n h", n=NT)).then_inc(drained("lfT"), 1)
            for n in range(NT):
                o = product(dve, ("kt", n))
                if n >= 2:
                    dve.wait_ge(s_ok[n % 2], 16 * (n // 2))
                dve.tensor_copy(kst[:, n % 2, :], o[:, 0:512]).then_inc(drained(("kt", n)), 1)

            def row_max(u):
                h, i = UNITS[u]
                n = i * P
                o = product(dve, ("s", u))
                if i == NP - 1:
                    copied(dve, ("cb", h))
                    dve.wait_ge(s_dg, h + 1)
                if u >= 2:
                    past_pe(dve, ("pt", u - 2))
                m, v = mx[:, u % 4:u % 4 + 1], nm[:, u % 4:u % 4 + 1]
                init = -3e38
                if i:
                    link(dve.tensor_tensor_reduce(S[:, u % 2, 0:n], o[:, 0:n], cb[:, h % 2, 0:n], 1.0, -3e38, ALU.add,
                                                  ALU.max, m))
                    init = m
                dve.tensor_tensor_reduce(S[:, u % 2, n:n + P], o[:, n:n + P], dg[:, h % 2, n:n + P], 1.0, init,
                                         ALU.add, ALU.max, m).then_inc(drained(("s", u)), 1)
                copied(dve, ("s", u))
                dve.tensor_scalar(v, m, -1.0, None, ALU.mult).then_inc(s_max, 1)

            def copy_probs(u):
                if u % 2 == 0:
                    h, i = UNITS[u]
                    o = product(dve, ("pt", u))
                    if u >= 2:
                        past_pe(dve, ("pv", u - 2))
                    dve.tensor_copy(PT[:, u % 2, 0:(i + 1) * P], o[:, 0:(i + 1) * P]).then_inc(drained(("pt", u)), 1)

            def norm_out(u):
                h, i = UNITS[u]
                dve.wait_ge(s_exp, u + 1)
                link(dve.reciprocal(ri[:, u % 4:u % 4 + 1], rs[:, u % 4:u % 4 + 1]))
                if h >= 2 and h % 2 == 0 and i == NP - 1:
                    past_pe(dve, ("oT", h // 2 - 1))
                o = product(dve, ("pv", u))
                dve.tensor_scalar(oab[:, i, (h % 2) * DH:(h % 2 + 1) * DH], o[:, 0:DH], ri[:, u % 4:u % 4 + 1], None,
                                  ALU.mult).then_inc(drained(("pv", u)), 1)

            NU = len(UNITS)
            dve.wait_ge(s_ok[0], 16 * 5)
            dve.wait_ge(s_ok[1], 16 * 4)
            for u in range(NU + 2):
                if u < NU:
                    row_max(u)
                if 1 <= u <= NU:
                    copy_probs(u - 1)
                if u >= 2:
                    norm_out(u - 2)

            past_pe(dve, ("oT", 3))
            for b in range(DEC_B + 2):
                if b < DEC_B:
                    o = product(dve, ("ss", b))
                    q = slice(b % 2, b % 2 + 1)
                    if b >= 2:
                        dve.wait_ge(s_exs, b - 1)
                    link(dve.tensor_tensor_reduce(sN[:, b % 2, :], o[:, 256:384], win[:, 112 - 16 * b:240 - 16 * b], 1.0,
                                                  -3e38, ALU.add, ALU.max, mxb[:, q]))
                    link(dve.tensor_reduce(mx[:, q], o[:, 0:256], AX.X, ALU.max))
                    stt(nm[:, q], mx[:, q], mxb[:, q], neg1, ALU.max, ALU.mult).then_inc(s_smx, 1)
                    dve.wait_ge(s_exs, b + 1)
                    dve.tensor_tensor(ri[:, q], rs[:, q], rsb[:, q], ALU.add).then_inc(drained(("ss", b)), 1)
                    copied(dve, ("ss", b))
                    link(dve.reciprocal(ri[:, q], ri[:, q]))
                if 1 <= b <= DEC_B:
                    o = product(dve, ("spv", b - 1))
                    if b >= 3:
                        past_pe(dve, ("soT", b - 3))
                    q = slice((b - 1) % 2, (b - 1) % 2 + 1)
                    stt(om[:, (b - 1) % 2, :], o[:, 0:512], ri[:, q], omask, ALU.mult, ALU.mult)\
                        .then_inc(drained(("spv", b - 1)), 1)
                if b >= 2:
                    o = product(dve, ("soT", b - 2))
                    t = SEQ + 16 * (b - 2)
                    dve.tensor_copy(oaT[:, :, t:t + 16], o[:, 0:64].rearrange("p (j t) -> p j t", j=4))\
                        .then_inc(drained(("soT", b - 2)), 1)

            dve.wait_ge(s_qbd, DEC_B)
            dve.wait_ge(s_b, 16 * 3)
            dve.wait_ge(s_cols, 32)
            for h in range(H_B):
                for g in range(3):
                    o = product(dve, ("kb", h, g))
                    dve.tensor_copy(kb[:, g * THIRD:(g + 1) * THIRD], o[:, 0:THIRD]).then_inc(drained(("kb", h, g)), 1)
                dve.wait_ge(s_lnz, h + 1)
                link(stt(zb, zb, 0.0, X[:, 0, :], ALU.min, ALU.subtract))
                dve.tensor_tensor_scan(b16, scanm, zb, 0.0, ALU.mult, ALU.add).then_inc(s_bsc, 1)
                dve.wait_ge(s_bsc, h + 1)
                if h:
                    past_pe(dve, ("kst", h - 1, 1))
                bp, bs = rows(b16[:, 0:SEQ], NP, P), rows(b16[:, SEQ:T], DEC_B, DEC_T)
                kp_, ks_ = rows(ks[:, 0:SEQ], NP, P), rows(ks[:, SEQ:T], DEC_B, DEC_T)
                dve.tensor_tensor(kp_, bp[:, :, P - 1:P].to_broadcast([P, NP, P]), bp, ALU.subtract)
                dve.tensor_tensor(ks_, bs[:, :, DEC_T - 1:DEC_T].to_broadcast([P, DEC_B, DEC_T]), bs, ALU.subtract)\
                    .then_inc(s_kd, 1)
                dve.wait_ge(s_ee, h + 1)
                dve.tensor_tensor(qs, qb, X[:, 1, :], ALU.mult).then_inc(s_qs, 1)
                dve.tensor_tensor(ks, ks, kb, ALU.mult).then_inc(s_ksr, 1)
                dve.wait_ge(s_qs, h + 1)

                def level_log(l):
                    if l >= 2:
                        past_pe(dve, ("lv", h, l - 2, 0))
                        if l - 2 >= 3:
                            past_pe(dve, ("lv", h, l - 2, 1))
                    hf = HALVES[l]
                    t = SEQ if hf > 8 else T
                    xv = X[:, l % 2, 0:t].rearrange("p (n a j) -> p n a j", a=2, j=hf)
                    bv = b16[:, 0:t].rearrange("p (n a j) -> p n a j", a=2, j=hf)
                    ref = bv[:, :, 0, hf - 1:hf].to_broadcast([P, t // (2 * hf), hf])
                    dve.tensor_tensor(xv[:, :, 0, :], ref, bv[:, :, 0, :], ALU.subtract)
                    dve.tensor_tensor(xv[:, :, 1, :], bv[:, :, 1, :], ref, ALU.subtract).then_inc(s_xl, 1)

                def level_scale(l):
                    hf = HALVES[l]
                    t = SEQ if hf > 8 else T
                    dve.wait_ge(s_xe, 7 * h + l + 1)
                    v = [a[:, 0:t].rearrange("p (n a j) -> p n a j", a=2, j=hf) for a in (X[:, l % 2, :], kb, qb)]
                    dve.tensor_tensor(v[0][:, :, 0, :], v[0][:, :, 0, :], v[1][:, :, 0, :], ALU.mult)
                    dve.tensor_tensor(v[0][:, :, 1, :], v[0][:, :, 1, :], v[2][:, :, 1, :], ALU.mult).then_inc(s_xm, 1)

                def level_take(l):
                    mask = levm[:, l * P:(l + 1) * P] if l < 7 else ident.bitcast(U32)
                    o = product(dve, ("lv", h, l, 0))
                    if l:
                        copied(dve, ("lv", h, l - 1, 0))
                    dve.copy_predicated(rows(AT[:, 0:SEQ], NP, P), mask.rearrange("p (a t) -> p a t", a=1).to_broadcast([P, NP, P]),
                                        rows(o, NP, P)).then_inc(drained(("lv", h, l, 0)), 1)
                    if l >= 3:
                        o = product(dve, ("lv", h, l, 1))
                        if l > 3:
                            copied(dve, ("lv", h, l - 1, 1))
                        dve.copy_predicated(AT[:, SEQ:T], mask, o[:, 0:P]).then_inc(drained(("lv", h, l, 1)), 1)

                level_log(0)
                o = product(dve, ("kst", h, 0))
                dve.tensor_copy(ktok, rows(o, NP, P)).then_inc(drained(("kst", h, 0)), 1)
                o = product(dve, ("kst", h, 1))
                dve.tensor_tensor(ksm, o[:, 0:P].rearrange("p (a t) -> p a t", a=1).to_broadcast([P, DEC_B, P]),
                                  bmask.rearrange("p (b a) -> p b a", a=1).to_broadcast([P, DEC_B, P]), ALU.mult)\
                    .then_inc(drained(("kst", h, 1)), 1)
                dve.wait_ge(s_at0, h + 1)
                for l in range(8):
                    if l + 1 < 7:
                        level_log(l + 1)
                    if l < 7:
                        level_scale(l)
                    level_take(l)

                def out_turned(n):
                    o = product(dve, ("ot", h, n))
                    for c in range(2):
                        v = obT[:, 2 * h + c, n * P:(n + 1) * P]
                        ins = stt(v, o[:, c * P:(c + 1) * P], ggla[:, 2 * h + c:2 * h + c + 1], v, ALU.mult, ALU.mult)
                    ins.then_inc(drained(("ot", h, n)), 1)

                for n in range(NP):
                    o = product(dve, ("u", h, n))
                    if n >= 2:
                        past_pe(dve, ("o", h, n - 2))
                    if n == 1 and h:
                        dve.wait_ge(s_ost, 32 * h)
                    if n == 0:
                        ins = dve.tensor_copy(St[:, 1, :], o[:, 0:DV])
                    else:
                        copied(dve, ("u", h, n - 1))
                        ins = stt(St[:, (n + 1) % 3, :], St[:, n % 3, :], dl[:, n:n + 1], o[:, 0:DV], ALU.mult, ALU.add)
                    ins.then_inc(drained(("u", h, n)), 1)
                    if n >= 2:
                        out_turned(n - 2)
                out_turned(NP - 2)
                past_pe(dve, ("o", h, NP))
                for c in range(4):
                    o = product(dve, ("us", h, c))
                    for b in range(2):
                        v = S0[:, 2 * c + b, :]
                        ins = stt(v, v, dl[:, 8 + 2 * c + b:9 + 2 * c + b], o[:, b * DV:(b + 1) * DV], ALU.mult, ALU.add)
                    ins.then_inc(drained(("us", h, c)), 1)
                    if c < 2:
                        out_turned(NP - 1 + c)

            for j in range(KT):
                for g in range(3):
                    n = 3 * j + g
                    for q, (name, gate) in enumerate((("ya", "ga"), ("yb", "gb"))):
                        o = product(dve, (name, j, g))
                        copied(dve, (gate, j, g))
                        dve.tensor_tensor(sg[:, n % 2, 2 + q, :], o[:, 0:THIRD], sg[:, n % 2, q, :], ALU.mult)\
                            .then_inc(drained((name, j, g)), 1)

            norms = [0]

            def stats(z):
                q = norms[0] % 4
                for c in range(2):
                    ins = dve.bn_stats(bnst[:, q, c * 6:(c + 1) * 6], z[:, c * 512:(c + 1) * 512])
                link(ins)
                dve.bn_aggr(mv[:, q, :], bnst[:, q, :]).then_inc(s_var, 1)
                norms[0] += 1

            def normed(z, out, gain, bias):
                q = (norms[0] - 1) % 4
                dve.wait_ge(s_lrs, norms[0])
                link(dve.tensor_scalar(z, z, mv[:, q, 0:1], lrs[:, q:q + 1], ALU.subtract, ALU.mult))
                link(dve.tensor_tensor(z, z, gain, ALU.mult))
                return dve.tensor_tensor(out, z, bias, ALU.add)

            dve.wait_ge(s_g1, 32)
            for n in range(NT):
                dve.wait_ge(s_xin[n % 2], 16 * (n // 2 + 1))
                o = product(dve, ("wo", n))
                z = x1[:, n, :]
                stt(z, xin[:, n % 2, :], ALPHA, o, ALU.mult, ALU.add).then_inc(drained(("wo", n)), 1)
                copied(dve, ("wo", n))
                stats(z)
                normed(z, z, g1, b1).then_inc(s_x1, 1)

            for c in range(NC_FF):
                for v, name in enumerate(("uv", "ug")):
                    copied(dve, *[(name, c, g) for g in range(3)])
                    dve.wait_ge(s_up, 2 * c + v + 1)
                    if c == 0:
                        past_pe(dve, ("x1T", NT - 1))
                    if c:
                        dve.wait_ge(s_hT, c)
                    u = U[:, c % 2, v, :]
                    cc = v * NC_FF + c
                    w = [cwT[:, a, cc:cc + 1] for a in range(4)]
                    yv = y[:, v, 0:1168]
                    link(dve.tensor_scalar(yv, u[:, 0:1168], w[0], w[3], ALU.mult, ALU.add))
                    link(stt(yv, u[:, 1:1169], w[1], yv, ALU.mult, ALU.add))
                    ins = stt(yv, u[:, 2:1170], w[2], yv, ALU.mult, ALU.add)
                    if v == 0:
                        link(ins)
                    else:
                        ins.then_inc(s_ygt, 1)
                grp = [g for g in range(3) if sum(FF_GROUPS[:g]) <= c][-1]
                k = c - sum(FF_GROUPS[:grp])
                if k == 0 and grp:
                    past_pe(dve, ("dn", grp - 1, NT - 1))
                dve.wait_ge(s_gel, c + 1)
                dve.tensor_tensor(hT[:, k, 0:SEQ], y[:, 0, 0:SEQ], y[:, 1, 0:SEQ], ALU.mult)
                ya, yb = (rows(y[:, v, SEQ + 2:SEQ + 146], DEC_B, 18)[:, :, 0:DEC_T] for v in range(2))
                dve.tensor_tensor(rows(hT[:, k, SEQ:T], DEC_B, DEC_T), ya, yb, ALU.mult).then_inc(s_hT, 1)
                if k == FF_GROUPS[grp] - 1:
                    for n in range(NT):
                        o = product(dve, ("dn", grp, n))
                        z = x1[:, n, :]
                        stt(z, z, ALPHA if grp == 0 else 1.0, o, ALU.mult, ALU.add).then_inc(drained(("dn", grp, n)), 1)

            dve.wait_ge(s_ple, 16 * 6)

            def second(n):
                copied(dve, ("dn", 2, n))
                z = x1[:, n, :]
                stats(z)
                normed(z, z, g2, b2).then_inc(s_x2, 1)
                dve.wait_ge(s_x2, n + 1)

            past_pe(dve, ("dn", 2, NT - 1))
            second(0)
            for n in range(NT):
                if n + 1 < NT:
                    second(n + 1)
                copied(dve, ("pg", n))
                o = product(dve, ("pp", n))
                if n >= 3:
                    dve.wait_ge(s_oy[n % 3], 16 * (n // 3))
                z = z3[:, n % 3, :]
                dve.tensor_tensor(z, o, sge[:, n % 2, :], ALU.mult).then_inc(drained(("pp", n)), 1)
                copied(dve, ("pp", n))
                link(stt(z, x1[:, n, :], ALPHA, z, ALU.mult, ALU.add))
                stats(z)
                normed(z, z, g3, b3).then_inc(s_y, 1)

        @block.gpsimd
        def _(pool):
            copied(pool, *[("va", n) for n in range(NT)])
            rows_p, rows_s = (lambda ap: ap[0, 0].rearrange("t h d -> t (h d)")), (lambda ap: ap[0].rearrange("b t h d -> (b t) (h d)"))
            pool.dma_start(rows_p(fv_p).rearrange("(n p) c -> p n c", p=P), va[:, 0:NP, :]).then_inc(s_ov, 16)
            pool.dma_start(rows_s(fv_s), va[:, NP, :]).then_inc(s_ov, 16)
            copied(pool, "lfT")
            with nc.allow_non_contiguous_dma(reason="8 log-forgets of a token in a row"):
                pool.dma_start(fl_p[0, 0].rearrange("(n p) h -> p n h", p=P), lfo[:, 0:NP, :]).then_inc(s_ol, 16)
                pool.dma_start(fl_s[0].rearrange("b t h -> (b t) h"), lfo[:, NP, :]).then_inc(s_ol, 16)
            for n in range(NT):
                copied(pool, ("kt", n))
                dst = rows_p(fk_p)[n * P:(n + 1) * P, :] if n < NP else rows_s(fk_s)
                pool.dma_start(dst, kst[:, n % 2, :]).then_inc(s_ok[n % 2], 16)

            for h in range(H_A):
                copied(pool, ("cb", h))
                if h >= 2:
                    pool.wait_ge(s_max, NP * (h - 1))
                pool.tensor_tensor(dg[:, h % 2, :].rearrange("p (n t) -> p n t", t=P), cb[:, h % 2, :].rearrange("p (n t) -> p n t", t=P),
                                   causal.rearrange("p (a t) -> p a t", a=1).to_broadcast([P, NP, P]), ALU.add).then_inc(s_dg, 1)

            NU = len(UNITS)
            copied(pool, ("pv", NU - 1), ("pv", NU - 2), ("oT", 3))
            pool.memset(at(off["qbd"], 1312), 0.0).then_inc(s_pool, 1)
            pool.wait_ge(s_pool, 1)
            for b in range(DEC_B):
                if b >= 2:
                    past_pe(pool, ("ss", b - 2))
                for hh in range(2):
                    v = qbd[hh * DH:(hh + 1) * DH, b % 2, hh * 16:hh * 16 + 640].rearrange("p (j x) -> p j x", x=160)[:, :, 0:16]
                    ins = pool.tensor_copy(v, qT[hh * DH:(hh + 1) * DH, :, SEQ + 16 * b:SEQ + 16 * (b + 1)])
                ins.then_inc(s_qbd, 1)

            pool.wait_ge(s_ov, 32)
            copied(pool, ("soT", DEC_B - 1), ("soT", DEC_B - 2), ("spv", DEC_B - 1))
            pool.memset(qsm, 0.0).then_inc(s_pool, 1)
            for h in range(H_B):
                if h:
                    pool.wait_ge(s_ost, 32 * h)
                pool.dma_start(S0, state_gla[0].rearrange("b h c v -> h c b v")[h]).then_inc(s_s0, 16)
                pool.memset(AT, 0.0).then_inc(s_at0, 1)
                if h == 0:
                    pool.wait_ge(s_pool, 2)
                pool.wait_ge(s_qs, h + 1)
                pool.tensor_copy(qsm.rearrange("p (b x) -> p b x", x=P + DEC_T)[:, :, 0:DEC_T],
                                 qs[:, SEQ:T].rearrange("p (b t) -> p b t", t=DEC_T)).then_inc(s_qsm, 1)
                for n in range(NT):
                    pool.wait_ge(s_ssq, NT * h + n + 1)
                    pool.tensor_scalar(ms[:, n:n + 1], ss[:, n:n + 1], 1.0 / DV, LN_EPS, ALU.mult, ALU.add).then_inc(s_msq, 1)
                    pool.wait_ge(s_msq, NT * h + n + 1)
                    pool.tensor_tensor(rstd[:, n:n + 1], ms[:, n:n + 1], nhalf, ALU.pow).then_inc(s_rst, 1)
                copied(pool, ("u", h, NP - 1))
                pool.dma_start(st_p[0, 0, h], St[:, NP % 3, :]).then_inc(s_ost, 16)
                copied(pool, *[("us", h, c) for c in range(4)])
                pool.dma_start(st_s[0].rearrange("b h c v -> h c b v")[h], S0).then_inc(s_ost, 16)

            for j in range(KT):
                for g in range(3):
                    n = 3 * j + g
                    copied(pool, ("ya", j, g), ("yb", j, g))
                    pool.tensor_tensor(mT[:, j, g * THIRD:(g + 1) * THIRD], sg[:, n % 2, 2, :], sg[:, n % 2, 3, :], ALU.add)\
                        .then_inc(s_mt, 1)

            norms = [0]

            def row_rstd():
                i = norms[0]
                q = i % 4
                norms[0] += 1
                pool.wait_ge(s_var, i + 1)
                pool.tensor_scalar(lve[:, q:q + 1], mv[:, q, 1:2], LN_EPS, None, ALU.add).then_inc(s_lve, 1)
                pool.wait_ge(s_lve, i + 1)
                pool.tensor_tensor(lrs[:, q:q + 1], lve[:, q:q + 1], nhalf, ALU.pow).then_inc(s_lrs, 1)

            pool.wait_ge(s_mt, 3 * KT)
            pool.memset(U[:, :, :, 0:2], 0.0).then_inc(s_u0, 1)
            for n in range(NT):
                row_rstd()

            for c in range(NC_FF):
                if c >= 2:
                    pool.wait_ge(s_hT, c - 1)
                    past_pe(pool, ("cn", c - 2))
                for v in range(2):
                    u = U[:, c % 2, v, SEQ + 2:SEQ + 146].rearrange("p (b t) -> p b t", t=18)
                    pool.tensor_copy(u[:, :, 0:2], cacheT[:, v * NC_FF + c, :].rearrange("p (b r) -> p b r", r=2)).then_inc(s_up, 1)
                for v in range(2):
                    u = U[:, c % 2, v, :]
                    copied(pool, *[(("uv", "ug")[v], c, g) for g in range(3)])
                    pool.tensor_copy(cn[:, c % 2, v, 0:2], u[:, SEQ:SEQ + 2])
                    ins = pool.tensor_copy(cn[:, c % 2, v, 2:18].rearrange("p (b r) -> p b r", r=2),
                                           u[:, SEQ + 2:SEQ + 146].rearrange("p (b t) -> p b t", t=18)[:, :, 16:18])
                ins.then_inc(s_cnr, 1)
                if c:
                    store_new(pool, c - 1)
            store_new(pool, NC_FF - 1)

            row_rstd()
            for n in range(NT):
                if n + 1 < NT:
                    row_rstd()
                row_rstd()
                pool.wait_ge(s_y, n + 1)
                dst = y_p[0, n * P:(n + 1) * P, :] if n < NP else y_s.rearrange("b t d -> (b t) d")
                pool.dma_start(dst, z3[:, n % 3, :]).then_inc(s_oy[n % 3], 16)
            for i in range(3):
                pool.wait_ge(s_oy[i], 16 * 3)
            for i in range(2):
                pool.wait_ge(s_ocn[i], 32 * NC_FF // 2)
                pool.wait_ge(s_ok[i], 16 * (5 - i))
            pool.wait_ge(s_ost, 32 * H_B)
            pool.wait_ge(s_ov, 32)
            pool.wait_ge(s_ol, 32)

        @block.sync
        def _(sp):
            def load(n):
                name, src, kt = chunks[n]
                if n >= W_SLOTS:
                    past_pe(sp, w_last[chunks[n - W_SLOTS][0]])
                sp.dma_start(ring[:, n % W_SLOTS, 0:kt, :], src).then_inc(w_in_sem[n % W_SLOTS], 16)

            def tokens(p_, s_, n):
                return p_[n * P:(n + 1) * P, :] if n < NP else s_.rearrange("b t d -> (b t) d")

            def bcast(v, dst, s):
                sp.dma_start(dst, v.partition_broadcast(P)).then_inc(s, 16)

            sp.dma_start(keep, consts[:, 0:C_KEEP]).then_inc(s_const, 16)
            for n in range(3):
                sp.dma_start(xs[:, n, :], tokens(x_prompt[0], x_sample, n)).then_inc(s_x[n % 3], 16)
            with nc.allow_non_contiguous_dma(reason="small columns"):
                sp.dma_start(bfg, b_fgate.rearrange("o h -> h o")).then_inc(s_small, 16)
                sp.dma_start(wf, w_in[0].rearrange("(k p) n -> p k n", p=P)[:, :, O_F:O_F + H_A]).then_inc(s_small, 16)
                sp.dma_start(cvst, cache_ffn_conv[0].rearrange("b r c -> (b r) c")).then_inc(s_cv, 16)
                sp.dma_start(cwst[:, 0:3, :], conv_w[0].rearrange("j (c p) -> c j p", p=P)).then_inc(s_cv, 16)
                sp.dma_start(cwst[:, 3, :], conv_b[0].rearrange("(c p) -> c p", p=P)).then_inc(s_cv, 16)
                sp.dma_start(lfp.rearrange("p (b n) h -> p b n h", n=2), cache_fox_logf[0].rearrange("b (n p) h -> p b n h", p=P)).then_inc(s_lf, 16)
            for n in range(3, NT):
                past_pe(sp, ("xT", n - 3))
                sp.dma_start(xs[:, n % 3, :], tokens(x_prompt[0], x_sample, n)).then_inc(s_x[n % 3], 16)
            for n in range(4):
                load(n)
            sp.dma_start(hc, consts[:, C_HSEL:C_SCAN]).then_inc(s_const2, 16)
            with nc.allow_non_contiguous_dma(reason="small columns"):
                sp.dma_start(ba2, b_a2[0].rearrange("(c p) -> p c", p=P)).then_inc(s_cols, 16)
                sp.dma_start(ggla, g_gla[0].rearrange("(c p) -> p c", p=P)).then_inc(s_cols, 16)
            for n in range(4, 16):
                load(n)
            NU = len(UNITS)
            copied(sp, ("pv", NU - 1), ("pv", NU - 2), ("oT", 3))
            for b in range(DEC_B):
                if b >= 2:
                    past_pe(sp, ("spv", b - 2))
                for dst, src in ((kp, cache_fox_k), (vp, cache_fox_v)):
                    sp.dma_start(dst[:, b % 2, :].rearrange("p (n c) -> p n c", n=2),
                                 src[0, b].rearrange("(n p) h d -> p n (h d)", p=P)).then_inc(s_kv[b % 2], 16)
            copied(sp, ("soT", DEC_B - 1), ("soT", DEC_B - 2), ("spv", DEC_B - 1))
            sp.dma_start(wa2, w_a2[0]).then_inc(s_b, 16)
            with nc.allow_non_contiguous_dma(reason="16 columns"):
                sp.dma_start(wa1, w_in[0].rearrange("(k p) n -> p k n", p=P)[:, :, O_A1:O_A1 + RANK]).then_inc(s_b, 16)
            sp.dma_start(scanm, consts[:, C_SCAN:C_ALL]).then_inc(s_b, 16)
            first_up = w_index[("uv", 0)]
            for n in range(16, first_up + 4):
                load(n)
                if n == w_index[("yb", 1)]:
                    sp.wait_ge(s_ost, 32 * H_B)
                    past_pe(sp, ("us", 3, 3))
                    sp.dma_start(wo, w_o[0].rearrange("(k p) n -> p k n", p=P)).then_inc(s_wo, 16)
            bcast(ln1_g[0], g1, s_g1)
            bcast(ln1_b[0], b1, s_g1)
            for n in range(NT):
                if n >= 2:
                    copied(sp, ("wo", n - 2))
                sp.dma_start(xin[:, n % 2, :], tokens(x_prompt[0], x_sample, n)).then_inc(s_xin[n % 2], 16)
            c0 = 0
            for grp, size in enumerate(FF_GROUPS):
                past_pe(sp, ("wo", NT - 1) if grp == 0 else ("dn", grp - 1, NT - 1))
                sp.dma_start(wd[:, 0:size, :], w_down[0].rearrange("(k p) n -> p k n", p=P)[:, c0:c0 + size, :]).then_inc(s_wd, 16)
                for n in range(first_up + 2 * c0 + 4, min(first_up + 2 * (c0 + size) + 4, len(chunks))):
                    load(n)
                c0 += size
            for n in range(2):
                sp.dma_start(pin[:, n, :], tokens(p_prompt[0, 0], p_sample[0], n)).then_inc(s_pin[n], 16)
            past_pe(sp, ("ug", NC_FF - 1, 2))
            sp.dma_start(plg, w_plg[0].rearrange("(k p) n -> p k n", p=P)).then_inc(s_ple, 16)
            sp.wait_ge(s_hT, NC_FF)
            sp.wait_ge(s_cnr, NC_FF)
            sp.dma_start(pl, w_pl[0].rearrange("(k p) n -> p k n", p=P)).then_inc(s_ple, 16)
            for v, dst in ((ln2_g, g2), (ln2_b, b2), (ln3_g, g3), (ln3_b, b3)):
                bcast(v[0], dst, s_ple)
            for n in range(2, NT):
                past_pe(sp, ("pT", n - 2))
                sp.dma_start(pin[:, n % 2, :], tokens(p_prompt[0, 0], p_sample[0], n)).then_inc(s_pin[n % 2], 16)


_INS = ["x_prompt", "x_sample", "cache_fox_k", "cache_fox_v", "cache_fox_logf", "state_gla", "cache_ffn_conv",
        "p_prompt", "p_sample", "w_in", "b_fgate", "w_a2", "b_a2", "g_gla", "w_a_out", "w_b_out", "w_o", "ln1_g",
        "ln1_b", "w_up", "conv_w", "conv_b", "w_down", "ln2_g", "ln2_b", "w_pl", "w_plg", "ln3_g", "ln3_b"]
_OUTS = [(1, SEQ, D), (DEC_B, DEC_T, D),
         (1, 1, SEQ, H_A, DH), (1, 1, SEQ, H_A, DH), (1, 1, SEQ, H_A), (1, 1, H_B, DK, DV), (1, 1, 2, 2 * D_FF),
         (1, DEC_B, DEC_T, H_A, DH), (1, DEC_B, DEC_T, H_A, DH), (1, DEC_B, DEC_T, H_A), (1, DEC_B, H_B, DK, DV),
         (1, DEC_B, 2, 2 * D_FF)]


def kernel(**inputs):
    import concourse.bacc as bacc
    from concourse.bass_utils import run_bass_kernel_spmd

    nc = bacc.Bacc("TRN2", target_bir_lowering=False, num_devices=1)
    arrays, args = {}, []
    for name in _INS:
        a = np.ascontiguousarray(inputs[name])
        arrays[f"in_{name}"] = a
        args.append(nc.dram_tensor(f"in_{name}", a.shape, F32, kind="ExternalInput").ap())
    arrays["in_consts"] = shape_constants()
    args.append(nc.dram_tensor("in_consts", arrays["in_consts"].shape, F32, kind="ExternalInput").ap())
    for i, shape in enumerate(_OUTS):
        args.append(nc.dram_tensor(f"out_{i}", shape, F32, kind="ExternalOutput").ap())
    build(nc, *args)
    r = run_bass_kernel_spmd(nc, [arrays], core_ids=[0])
    return tuple(r.results[0][f"out_{i}"] for i in range(len(_OUTS)))
```

```python
from contextlib import ExitStack

import numpy as np

import concourse.bass as bass
from concourse import mybir

F32 = mybir.dt.float32
F32R = mybir.dt.float32r
U32 = mybir.dt.uint32
ALU = mybir.AluOpType
ACT = mybir.ActivationFunctionType
AX = mybir.AxisListType

P = 128
D = 1024
KT = D // P
SEQ, DEC_B, DEC_T = 1024, 8, 16
PAST = 256
T = SEQ + DEC_B * DEC_T
NP = SEQ // P
NT = T // P
THIRD = T // 3
H_A, DH = 8, 64
H_B, DK, DV = 4, 128, 256
RANK, TAU = 16, 16
D_FF, PLE = 2816, 256
NC_FF = D_FF // P
LN_EPS = 1e-5
ALPHA = 2.0 ** 0.25
NEG = -1e30
O_Q, O_K, O_V, O_F = 0, 512, 1024, 1536
O_QB, O_KB, O_VB, O_RB = 1544, 2056, 2568, 3592
O_A1, O_GA, O_GB = 4616, 4632, 5656
HALVES = [64, 32, 16, 8, 4, 2, 1]
W_SLOTS = 4

C_ID = 0
C_LEV = C_ID + P
C_CAUSAL = C_LEV + 7 * P
C_NEG1 = C_CAUSAL + P
C_NHALF = C_NEG1 + 1
C_BM = C_NHALF + 1
C_ONE = C_BM + DEC_B
C_KEEP = C_ONE + 1
C_HSEL = C_KEEP + 5
C_OMASK = C_HSEL + H_A * P
C_WIN = C_OMASK + H_A * DH
C_HS16 = C_WIN + 240
C_TSEL = C_HS16 + P
C_SCAN = C_TSEL + DEC_T
C_ALL = C_SCAN + T


def shape_constants():
    c = np.zeros((P, C_ALL), np.float32)
    i = np.arange(P)
    c[:, C_ID:C_ID + P] = np.eye(P)
    for n, h in enumerate(HALVES):
        s, t = i[:, None], i[None, :]
        c[:, C_LEV + n * P:C_LEV + (n + 1) * P] = (s // (2 * h) == t // (2 * h)) & (s % (2 * h) < h) & (t % (2 * h) >= h)
    c[:, C_CAUSAL:C_CAUSAL + P] = np.where(i[None, :] > i[:, None], NEG, 0.0)
    c[:, C_NEG1] = -1.0
    c[:, C_NHALF] = -0.5
    c[:, C_BM:C_BM + DEC_B] = i[:, None] // DEC_T == np.arange(DEC_B)[None, :]
    c[:, C_ONE] = 1.0
    for h in range(H_A):
        c[h, C_HSEL + h * P:C_HSEL + (h + 1) * P] = 1.0
        c[h, C_HS16 + h * DEC_T:C_HS16 + (h + 1) * DEC_T] = 1.0
        c[h * DEC_T:(h + 1) * DEC_T, C_OMASK + h * DH:C_OMASK + (h + 1) * DH] = 1.0
    x = np.arange(240)[None, :] - 112
    c[:, C_WIN:C_WIN + 240] = np.where((x >= 0) & (x <= i[:, None] % DEC_T), 0.0, NEG)
    c[:, C_TSEL:C_TSEL + DEC_T] = i[:, None] % DEC_T == np.arange(DEC_T)[None, :]
    t = np.arange(T)
    c[:, C_SCAN:] = np.where(np.where(t < SEQ, t % P, t % DEC_T) == 0, 0.0, 1.0)
    return c


def build(nc, x_prompt, x_sample, cache_fox_k, cache_fox_v, cache_fox_logf, state_gla, cache_ffn_conv,
          p_prompt, p_sample, w_in, b_fgate, w_a2, b_a2, g_gla, w_a_out, w_b_out, w_o, ln1_g, ln1_b,
          w_up, conv_w, conv_b, w_down, ln2_g, ln2_b, w_pl, w_plg, ln3_g, ln3_b, consts,
          y_p, y_s, fk_p, fv_p, fl_p, st_p, cv_p, fk_s, fv_s, fl_s, st_s, cv_s):
    ctx = ExitStack()
    with ctx:
        def sem(name):
            return ctx.enter_context(nc.semaphore(name))

        M_ALL = 53200
        SB_BASE = (nc.sbuf_base + 31) // 32 * 32
        sb = ctx.enter_context(nc.sbuf_tensor("sb", [P, M_ALL], F32))
        ps = ctx.enter_context(nc.psum_tensor("ps", [P, 4, 1024], F32))

        def at(off, *dims, parts=P):
            n = int(np.prod(dims))
            assert off + n <= M_ALL, (off, n)
            v = sb[0:parts, off:off + n]
            if len(dims) == 2:
                v = v.rearrange("p (a b) -> p a b", a=dims[0])
            if len(dims) == 3:
                v = v.rearrange("p (a b c) -> p a b c", a=dims[0], b=dims[1])
            return v

        off = {}

        def place(base, *items):
            for name, n in items:
                off[name] = base
                base += n
            return base

        e = place(0, ("keep", C_KEEP + 5), ("cw", 176), ("cacheT", 704), ("cols", 40), ("stat", 152))
        e = place(e, ("ring", W_SLOTS * 1024), ("ringh", W_SLOTS * 1024))
        e = place(e, ("R1", 9216), ("R2", 9216), ("R3", 9216), ("R4", 9216))
        off["R5"] = e
        place(off["R1"], ("xh", 9216), ("xl", 9216))
        place(off["R3"], ("oaT", 4608), ("qT", 4608), ("kT", 4608), ("va", 4608))
        place(off["oaT"], ("fz", 1152), ("fa", 1152), ("kst", 1024), ("cwst", 512), ("lfp", 128))
        off["cvst"], off["xs"] = off["qT"], off["va"]
        e = place(off["R5"], ("hsel", C_SCAN - C_HSEL), ("negC", 1152), ("negCs", 2048 + 128), ("lfo", 72), ("wf", 64),
                  ("wfh", 64))
        assert e <= M_ALL, e
        place(off["R1"], ("cb", 2048), ("dg", 2048), ("S", 2048), ("PT", 2048), ("oab", 1024))
        place(off["R1"], ("qbd", 1312), ("kpT", 2048), ("sN", 256), ("sP", 768), ("sPT", 768), ("om", 1024))
        off["kv"] = off["R2"]
        e = place(off["R3"], ("qb", 1152), ("kb", 1152), ("zb", 1152), ("b", 1152), ("X", 2 * 1152),
                  ("ks", 1152), ("AT", 1152), ("vb", 2304), ("St", 768), ("S0", 2048), ("ktok", 1024),
                  ("ksm", 1024), ("qsm", 1152), ("on", 768), ("scan", 1152), ("a1T", 1152), ("wa2", 512),
                  ("sq", 256), ("wa1", 128), ("wa1h", 128), ("obT", 2304))
        off["qs"] = off["zb"]
        assert e <= M_ALL, e
        off["gate_a"], off["gate_b"] = off["R3"], off["R4"]
        off["oal"], off["oah"] = off["R5"], off["R1"]
        off["obl"] = off["R2"]
        off["obh0"], off["obh1"] = off["R1"] + 4608, off["R1"]
        off["mh"], off["ml"] = off["gate_b"], off["gate_a"]
        off["x1"] = off["R1"]
        place(off["R5"], ("wol0", 4096), ("g1", 1024))
        off["woh0"] = off["ringh"]
        place(off["R2"], ("wol1", 4096), ("woh1", 4096), ("b1", 1024))
        off["x1h"], off["x1l"] = off["mh"], off["ml"]
        place(off["R2"], ("hh", 2304), ("hl", 2304), ("wdr", 2048), ("wdh", 2048))
        e = place(off["R5"], ("U", 2344), ("y", 2344), ("cn", 72), ("cno", 256))
        assert e <= M_ALL, e
        off["plgr"], off["plgh"] = off["x1h"], off["x1l"]
        off["plr"], off["plh"] = off["hh"], off["hh"] + 2048
        place(off["wdr"], ("x2h", 2048), ("x2l", 2048))
        place(off["ring"], ("pin", 512), ("pTh", 512), ("pTl", 512), ("g2", 1024), ("b2", 1024), ("g3", 1024),
              ("b3", 1024))
        place(off["R5"], ("z3", 3072), ("sge", 2048))

        def named(name, base, *dims, kind=F32):
            t = nc.alloc_sbuf_tensor_at(name, [P, int(np.prod(dims))], kind, offset=SB_BASE + 4 * base)
            v = t[:, :]
            if len(dims) == 2:
                v = v.rearrange("p (a b) -> p a b", a=dims[0])
            if len(dims) == 3:
                v = v.rearrange("p (a b c) -> p a b c", a=dims[0], b=dims[1])
            return v

        def rounded(name, base, *dims):
            return named(name, base, *dims, kind=F32R)

        keep = at(off["keep"], C_KEEP)
        ident = keep[:, C_ID:C_ID + P]
        levm = keep[:, C_LEV:C_LEV + 7 * P].bitcast(U32)
        causal = keep[:, C_CAUSAL:C_CAUSAL + P]
        neg1, nhalf, one = keep[:, C_NEG1:C_NEG1 + 1], keep[:, C_NHALF:C_NHALF + 1], keep[:, C_ONE:C_ONE + 1]
        bmask = keep[:, C_BM:C_BM + DEC_B]
        hc = at(off["hsel"], C_SCAN - C_HSEL)
        hsel = hc[0:H_A, 0:H_A * P]
        omask = hc[:, C_OMASK - C_HSEL:C_OMASK - C_HSEL + 512]
        win = hc[:, C_WIN - C_HSEL:C_WIN - C_HSEL + 240]
        hs16 = hc[0:H_A, C_HS16 - C_HSEL:C_HS16 - C_HSEL + P]
        tsel = hc[:, C_TSEL - C_HSEL:C_TSEL - C_HSEL + DEC_T]
        scanm = at(off["scan"], T)

        xh, xl = rounded("x_hi", off["xh"], KT, T), rounded("x_lo", off["xl"], KT, T)
        ring, ringh, ringl = (v.rearrange("p s (k c) -> p s k c", k=KT) for v in (
            named("ring_raw", off["ring"], W_SLOTS, KT * P), rounded("ring_hi", off["ringh"], W_SLOTS, KT * P),
            rounded("ring_lo", off["ring"], W_SLOTS, KT * P)))
        oaT = at(off["oaT"], 4, T)
        cols = at(off["cols"], 40)
        bfg, ba2, ggla = cols[0:H_A, 0:1], cols[:, 4:8], cols[:, 8:16]
        dl = cols[:, 16:32]
        stat = at(off["stat"], 152)
        rs, mx, nm, ri = stat[:, 0:4], stat[:, 4:8], stat[:, 8:12], stat[:, 12:16]
        ss, ms, rstd = stat[:, 16:32], stat[:, 32:48], stat[:, 48:64]
        mxb, rsb = stat[:, 64:68], stat[:, 68:72]
        bnst = stat[:, 80:80 + 48].rearrange("p (a b) -> p a b", a=4)
        mv = stat[:, 130:138].rearrange("p (a b) -> p a b", a=4)
        lve, lrs = stat[:, 140:144], stat[:, 144:148]

        xs = at(off["xs"], 3, 1024)
        qT, kT, va = at(off["qT"], 4, T), at(off["kT"], 4, T), at(off["va"], NT, 512)
        cwT = at(off["cw"], 4, 44)
        cacheT = at(off["cacheT"], 44, 16)
        cvst = at(off["cvst"], 5632, parts=16)
        cwst = at(off["cwst"], 4, P, parts=44)
        lfp = at(off["lfp"], 16, H_A)
        wf, wfh, wfl = (k(n, off[o], KT, H_A) for k, n, o in ((named, "wf_raw", "wf"), (rounded, "wf_hi", "wfh"), (rounded, "wf_lo", "wf")))
        fz, fa = at(off["fz"], T, parts=H_A), at(off["fa"], T, parts=H_A)
        negC = at(off["negC"], T, parts=H_A)
        negCs = at(off["negCs"], 2176, parts=H_A)
        lfo = at(off["lfo"], NT, H_A)
        kst = at(off["kst"], 2, 512)
        cb, dg = at(off["cb"], 2, 1024), at(off["dg"], 2, 1024)
        S, PT = at(off["S"], 2, 1024), at(off["PT"], 2, 1024)
        oab = at(off["oab"], NP, P)
        qbd = at(off["qbd"], 2, 656)
        kp, vp = (at(off["kv"] + 4096 * i, 4, 1024) for i in range(2))
        kpT = at(off["kpT"], 2, 1024)
        sN, sP, sPT, om = at(off["sN"], 2, 128), at(off["sP"], 2, 384), at(off["sPT"], 2, 384), at(off["om"], 2, 512)

        qb, kb, zb, b16, qs = (at(off[n], T) for n in ("qb", "kb", "zb", "b", "qs"))
        X = at(off["X"], 2, T)
        ks = at(off["ks"], T)
        AT = at(off["AT"], T)
        vb, St = at(off["vb"], NT, DV), at(off["St"], 3, DV)
        S0 = at(off["S0"], DEC_B, DV)
        ktok, ksm = at(off["ktok"], NP, P), at(off["ksm"], DEC_B, P)
        qsm = at(off["qsm"], 1152)
        on = at(off["on"], 3, DV)
        a1T = at(off["a1T"], T, parts=RANK)
        wa2 = at(off["wa2"], 512, parts=RANK)
        wa1, wa1h, wa1l = (k(n, off[o], KT, RANK) for k, n, o in ((named, "wa1_raw", "wa1"), (rounded, "wa1_hi", "wa1h"), (rounded, "wa1_lo", "wa1")))
        sq = at(off["sq"], 256)
        obT = at(off["obT"], 2, T)
        oar, oah, oal = named("oa_raw", off["oal"], 4, T), rounded("oa_hi", off["oah"], 4, T), rounded("oa_lo", off["oal"], 4, T)
        obr, obl = named("ob_raw", off["obl"], KT, T), rounded("ob_lo", off["obl"], KT, T)
        obh = [rounded("ob_hi0", off["obh0"], 4, T), rounded("ob_hi1", off["obh1"], 4, T)]
        gate_a, gate_b = named("gate_a", off["gate_a"], KT, T), named("gate_b", off["gate_b"], KT, T)
        mh, ml = rounded("merged_hi", off["mh"], KT, T), rounded("merged_lo", off["ml"], KT, T)
        wor = [named(f"wo_raw{c}", off[f"wol{c}"], KT, 512) for c in range(2)]
        woh = [rounded(f"wo_hi{c}", off[f"woh{c}"], KT, 512) for c in range(2)]
        wol = [rounded(f"wo_lo{c}", off[f"wol{c}"], KT, 512) for c in range(2)]
        x1 = at(off["x1"], NT, D)
        x1h, x1l = rounded("x1_hi", off["x1h"], KT, T), rounded("x1_lo", off["x1l"], KT, T)
        g1, b1 = at(off["g1"], D), at(off["b1"], D)
        oa_out = nc.dram_tensor("branch_a", (P, 4, T), F32).ap()
        ob_out = nc.dram_tensor("branch_b", (P, H_B, 2, T), F32).ap()
        rawu = named("up_raw", off["ring"], 2, 2, KT * P).rearrange("p e v (k c) -> p e v k c", k=KT)
        wuh = rounded("up_hi", off["ringh"], 2, 2, KT * P).rearrange("p e v (k c) -> p e v k c", k=KT)
        wul = rounded("up_lo", off["ring"], 2, 2, KT * P).rearrange("p e v (k c) -> p e v k c", k=KT)
        rawd = named("down_raw", off["wdr"], 2, D)
        wdh, wdl = rounded("down_hi", off["wdh"], 2, D), rounded("down_lo", off["wdr"], 2, D)
        hh, hl = rounded("h_hi", off["hh"], 2, T), rounded("h_lo", off["hl"], 2, T)
        U, y = at(off["U"], 2, 1170), named("convolved_halves", off["y"], 2, 1170)
        cn, cno = at(off["cn"], 2, 18), at(off["cno"], 256, parts=18)
        rplg, rpl = named("plg_raw", off["plgr"], KT, D), named("pl_raw", off["plr"], 2, D)
        plgh, plgl = rounded("plg_hi", off["plgh"], KT, D), rounded("plg_lo", off["plgr"], KT, D)
        plh, pll = rounded("pl_hi", off["plh"], 2, D), rounded("pl_lo", off["plr"], 2, D)
        g2, b2, g3, b3 = (at(off[n], D) for n in ("g2", "b2", "g3", "b3"))
        pin = at(off["pin"], 2, PLE)
        pTh, pTl = rounded("p_hi", off["pTh"], 2, 2, P), rounded("p_lo", off["pTl"], 2, 2, P)
        x2h, x2l = rounded("x2_hi", off["x2h"], 2, KT, P), rounded("x2_lo", off["x2l"], 2, KT, P)
        sge, z3 = at(off["sge"], 2, D), at(off["z3"], 3, D)

        full = [sem(f"psum_full{s}") for s in range(4)]
        free = [sem(f"psum_free{s}") for s in range(4)]
        turn = {}

        def take(pe, key):
            n = len(turn)
            turn[key] = n
            if n >= 4:
                pe.wait_ge(free[n % 4], n // 4)
            return ps[:, n % 4, :]

        def filled(key):
            return full[turn[key] % 4]

        def drained(key):
            return free[turn[key] % 4]

        def count(key):
            return turn[key] // 4 + 1

        def product(eng, key):
            eng.wait_ge(filled(key), count(key))
            return ps[:, turn[key] % 4, :]

        def copied(eng, *keys):
            last = {}
            for k in keys:
                last[turn[k] % 4] = max(last.get(turn[k] % 4, 0), count(k))
            for s, v in last.items():
                eng.wait_ge(free[s], v)

        def past_pe(eng, *keys):
            last = {}
            for k in keys:
                last[turn[k] % 4] = max(last.get(turn[k] % 4, 0), count(k))
            for s, v in last.items():
                eng.wait_ge(full[s], v)

        bank = ps.rearrange("p s (a c) -> p (s a) c", a=2)
        up_full = [sem(f"up_full{s}") for s in range(4)]
        up_free = [sem(f"up_free{s}") for s in range(4)]
        dn_full = [sem(f"down_full{s}") for s in range(3)]
        dn_free = [sem(f"down_free{s}") for s in range(3)]
        cn_full, cn_free = sem("new_columns_full"), sem("new_columns_free")

        def up_use(j, d, v, g):
            n = 6 * d + 3 * v + g
            return n % 4, 3 * j + n // 4

        DOWN_AFTER = [range(0), range(0), range(0, 5), range(5, 11), range(11, 18), range(0)]

        def in_pairs(eng, step):
            step(0, 0)
            step(0, 1)
            with eng.Fori(0, NC_FF // 2 - 2) as j:
                step(j, 2)
                step(j, 3)
            step(0, NC_FF - 2)
            step(0, NC_FF - 1)

        def dn_use(j, d, w):
            n = 18 * d + w
            return n % 3, 12 * j + n // 3

        chunks = []

        def w_cols(w, c0, kt=KT):
            return w[0].rearrange("(k p) n -> p k n", p=P)[:, :, c0:c0 + P], kt

        for j in range(4):
            chunks.append((("qa", j), *w_cols(w_in, O_Q + j * P)))
        for j in range(4):
            chunks.append((("ka", j), *w_cols(w_in, O_K + j * P)))
        for j in range(4):
            chunks.append((("va", j), *w_cols(w_in, O_V + j * P)))
        for h in range(H_B):
            chunks.append((("qb", h), *w_cols(w_in, O_QB + h * P)))
            chunks.append((("kb", h), *w_cols(w_in, O_KB + h * P)))
            for c in range(2):
                chunks.append((("rb", h, c), *w_cols(w_in, O_RB + h * DV + c * P)))
            for c in range(2):
                chunks.append((("vb", h, c), *w_cols(w_in, O_VB + h * DV + c * P)))
        for j in range(KT):
            chunks.append((("ga", j), *w_cols(w_in, O_GA + j * P)))
            chunks.append((("gb", j), *w_cols(w_in, O_GB + j * P)))
        for j in range(KT):
            chunks.append((("ya", j), *w_cols(w_a_out, j * P, 4)))
        for j in range(KT):
            chunks.append((("yb", j), *w_cols(w_b_out, j * P)))
        for c in range(NC_FF):
            chunks.append((("uv", c), *w_cols(w_up, c * P)))
            chunks.append((("ug", c), *w_cols(w_up, D_FF + c * P)))
        UP_ROUND = sum(1 for c in chunks if c[0][0] not in ("uv", "ug")) // W_SLOTS
        w_index = {c[0]: n for n, c in enumerate(chunks)}
        w_last = {}
        w_in_sem = [sem(f"weights_in{s}") for s in range(W_SLOTS)]

        s_rh = sem("weights_hi_ready")
        s_rl = sem("weights_lo_ready")

        def weights(pe, name):
            n = w_index[name]
            pe.wait_ge(s_rl, n + 1)
            return ringh[:, n % W_SLOTS], ringl[:, n % W_SLOTS]

        FIRST_UP = UP_ROUND * W_SLOTS

        s_const = sem("const_in")
        s_const2 = sem("const2_in")
        s_small = sem("small_in")
        s_x = [sem(f"x_in{i}") for i in range(3)]
        s_cv = sem("conv_cache_in")
        s_lf = sem("logf_past_in")
        s_kv = [sem(f"kv_past_in{i}") for i in range(4)]
        s_b = sem("gla_small_in")
        s_s0 = sem("state_in")
        s_wo = [sem(f"wo_in{c}") for c in range(2)]
        s_g1 = sem("ln1_in")
        s_xin = [sem(f"x_again_in{i}") for i in range(NT)]
        s_ple = sem("embedding_weights_in")
        s_pin = [sem(f"p_in{i}") for i in range(2)]
        s_xh1 = sem("x_hi_ready")
        s_sm = sem("small_hi_ready")
        s_sl = sem("small_lo_ready")
        s_oas = sem("branch_a_stored")
        s_obs = sem("branch_b_stored")
        s_oai = sem("branch_a_in")
        s_obi = sem("branch_b_in")
        s_oh = sem("branch_hi_ready")
        s_ol2 = sem("branch_lo_ready")
        s_mr = sem("merged_sum_ready")
        s_mh = sem("merged_hi_ready")
        s_woh = sem("wo_hi_ready")
        s_wol = sem("wo_lo_ready")
        s_ok = [sem(f"k_stored{i}") for i in range(2)]
        s_ov = sem("v_stored")
        s_ol = sem("logf_stored")
        s_cols = sem("gla_columns_in")
        s_ost = sem("state_stored")
        s_ocn = sem("conv_stored")
        s_oy = [sem(f"y_stored{i}") for i in range(3)]

        s_dve = sem("dve_step")
        s_act = sem("act_step")
        s_pool = sem("pool_step")
        s_fz = sem("fgate_exp")
        s_lf8 = sem("logf_ready")
        s_negc = sem("negC_ready")
        s_dg = sem("diag_bias_ready")
        s_max = sem("row_max_ready")
        s_exp = sem("probs_ready")
        s_exs = sem("sample_probs_ready")
        s_qbd = sem("qbd_ready")
        s_smx = sem("sample_max_ready")
        s_lnz = sem("gate_log_ready")
        s_bsc = sem("cumsum_ready")
        s_kd = sem("k_decay_log_ready")
        s_ee = sem("decays_ready")
        s_qs = sem("qs_ready")
        s_ksr = sem("ks_ready")
        s_at0 = sem("AT_cleared")
        s_qsm = sem("qsm_ready")
        s_xl = sem("level_log_ready")
        s_xe = sem("level_exp_ready")
        s_xm = sem("level_ready")
        s_ssq = sem("square_sum_ready")
        s_rst = sem("rstd_ready")
        s_mt = sem("merged_lo_ready")
        s_var = sem("ln_var_ready")
        s_lve = sem("ln_var_eps_ready")
        s_msq = sem("mean_square_ready")
        s_lrs = sem("ln_rstd_ready")
        s_x1 = sem("x1_ready")
        s_u0 = sem("U_cleared")
        s_up = sem("cache_columns_ready")
        s_conv = sem("convolved")
        s_cv1 = sem("convolved_tap0")
        s_cv2 = sem("convolved_tap1")
        s_g2 = sem("ln23_in")
        s_gel = sem("gelu_ready")
        s_cg = sem("U_read")
        s_hm = sem("h_ready")
        s_hh = sem("h_hi_ready")
        s_hl = sem("h_lo_ready")
        s_wh = sem("up_hi_ready")
        s_wl = sem("up_lo_ready")
        s_dh = sem("down_hi_ready")
        s_dl = sem("down_lo_ready")
        s_wdi = [sem(f"down_in{i}") for i in range(2)]
        s_xh = sem("x1_hi_ready")
        s_xa = sem("x1_scaled")
        s_ph = sem("plg_hi_ready")
        s_pl = sem("plg_lo_ready")
        s_x2h = sem("x2_hi_ready")
        s_x2 = sem("x2_ready")
        s_y = sem("y_ready")

        block = ctx.enter_context(nc.Block())

        def split3(hi_w, lo_w, hi_x, lo_x):
            return [(hi_w, hi_x), (hi_w, lo_x), (lo_w, hi_x)]

        UNITS = [(h, i) for h in range(H_A) for i in reversed(range(NP))]

        @block.tensor
        def _(pe):
            mm, tr = pe.matmul, pe.transpose

            def chain(out, pairs):
                for n, (l, r) in enumerate(pairs):
                    m = mm(out, l, r, start=(n == 0), stop=(n == len(pairs) - 1))
                return m

            def split_chain(out, w, x, kt=KT):
                pairs = []
                for k in range(kt):
                    pairs += split3(w[0][:, k, :], w[1][:, k, :], x[0](k), x[1](k))
                return chain(out, pairs)

            def thirds(key, chunk, x, kt=KT, lhs=None):
                w = weights(pe, chunk) if lhs is None else lhs
                for g in range(3):
                    t = slice(g * THIRD, (g + 1) * THIRD)
                    o = take(pe, (*key, g))
                    split_chain(o[0:w[0].shape[-1], 0:THIRD], w, [lambda k, a=a: a(k)[:, t] for a in x], kt)\
                        .then_inc(filled((*key, g)), 1)
                if chunk is not None:
                    w_last[chunk] = (*key, 2)

            def pair_tile(o, chunk, n):
                s0 = w_index[chunk] % W_SLOTS
                t = slice(n * P, (n + 1) * P)
                pairs = []
                for k in range(KT):
                    pairs += split3(xh[:, k, t], xl[:, k, t], ringh[:, s0:s0 + 2, k, :], ringl[:, s0:s0 + 2, k, :])
                return chain(o[:, 0:2 * P], pairs)

            def turn_x(key, rounds):
                for n in range(NT):
                    pe.wait_ge(s_x[n % 3], 16 * (rounds * 3 + n // 3 + 1))
                    o = take(pe, (key, n))
                    for k in range(KT):
                        m = tr(o[:, k * P:(k + 1) * P], xs[:, n % 3, k * P:(k + 1) * P], ident)
                    m.then_inc(filled((key, n)), 1)

            x_parts = [lambda k, a=a: a[:, k, :] for a in (xh, xl)]

            pe.wait_ge(s_const, 16)
            turn_x("xT", 0)
            pe.wait_ge(s_cv, 32 + 16)
            o = take(pe, "cacheT")
            for c in range(44):
                m = tr(o[:, c * 16:(c + 1) * 16], cvst[:, c * P:(c + 1) * P], ident[0:16, 0:16])
            m.then_inc(filled("cacheT"), 1)
            o = take(pe, "cwT")
            for c in range(4):
                m = tr(o[:, c * 44:(c + 1) * 44], cwst[:, c, :], ident[0:44, 0:44])
            m.then_inc(filled("cwT"), 1)
            pe.wait_ge(s_lf, 16)
            for n in range(2):
                o = take(pe, ("lfp", n))
                for c in range(8):
                    m = tr(o[0:H_A, c * P:(c + 1) * P], lfp[:, n * 8 + c, :], ident)
                m.then_inc(filled(("lfp", n)), 1)
            copied(pe, *[("xT", n) for n in range(NT)])
            pe.wait_ge(s_sl, 1)
            thirds(("f",), None, x_parts, lhs=(wfh, wfl))
            for j in range(4):
                thirds(("qa", j), ("qa", j), x_parts)
            for j in range(4):
                thirds(("ka", j), ("ka", j), x_parts)
            for q in range(2):
                weights(pe, ("va", 2 * q + 1))
                for n in range(NT):
                    o = take(pe, ("va", q, n))
                    pair_tile(o, ("va", 2 * q), n).then_inc(filled(("va", q, n)), 1)
                w_last[("va", 2 * q)] = w_last[("va", 2 * q + 1)] = ("va", q, NT - 1)
            pe.wait_ge(s_lf8, 1)
            o = take(pe, "lfT")
            for n in range(NT):
                m = tr(o[:, n * H_A:(n + 1) * H_A], fz[:, n * P:(n + 1) * P], ident[0:H_A, 0:H_A])
            m.then_inc(filled("lfT"), 1)
            copied(pe, *[("ka", j, g) for j in range(4) for g in range(3)])
            for n in range(NT):
                o = take(pe, ("kt", n))
                for j in range(4):
                    m = tr(o[:, j * P:(j + 1) * P], kT[:, j, n * P:(n + 1) * P], ident)
                m.then_inc(filled(("kt", n)), 1)

            def bias_rows(h):
                if h == 0:
                    pe.wait_ge(s_negc, 1)
                    pe.wait_ge(s_const2, 16)
                o = take(pe, ("cb", h))
                for c in range(2):
                    m = mm(o[:, c * 512:(c + 1) * 512], hsel[:, h * P:(h + 1) * P], negC[:, c * 512:(c + 1) * 512],
                           start=True, stop=True)
                m.then_inc(filled(("cb", h)), 1)

            def scores(u):
                h, i = UNITS[u]
                r = (h % 2) * DH
                o = take(pe, ("s", u))
                n = (i + 1) * P
                for c in range(0, n, 512):
                    e = min(n, c + 512)
                    m = mm(o[:, c:e], qT[r:r + DH, h // 2, i * P:(i + 1) * P], kT[r:r + DH, h // 2, c:e],
                           start=True, stop=True)
                m.then_inc(filled(("s", u)), 1)

            def turn_probs(u):
                h, i = UNITS[u]
                pe.wait_ge(s_exp, u + 1)
                o = take(pe, ("pt", u))
                for c in range(i + 1):
                    m = tr(o[:, c * P:(c + 1) * P], S[:, u % 2, c * P:(c + 1) * P], ident)
                m.then_inc(filled(("pt", u)), 1)

            def probs_v(u):
                h, i = UNITS[u]
                copied(pe, ("pt", u))
                o = take(pe, ("pv", u))
                chain(o[:, 0:DH], [(PT[:, u % 2, c * P:(c + 1) * P], va[:, c, h * DH:(h + 1) * DH])
                                   for c in range(i + 1)]).then_inc(filled(("pv", u)), 1)
                if h % 2 == 1 and i == 0:
                    copied(pe, *[("pv", v) for v in range(u - 15, u + 1)])
                    o = take(pe, ("oT", h // 2))
                    for c in range(NP):
                        m = tr(o[:, c * P:(c + 1) * P], oab[:, c, :], ident)
                    m.then_inc(filled(("oT", h // 2)), 1)

            copied(pe, ("qa", 3, 0), ("qa", 3, 1), ("qa", 3, 2), *[("va", q, n) for q in range(2) for n in range(NT)])
            bias_rows(0)
            NU = len(UNITS)
            for u in range(NU + 2):
                if u < NU:
                    if u % 8 == 6 and UNITS[u][0] + 1 < H_A:
                        bias_rows(UNITS[u][0] + 1)
                    scores(u)
                if 1 <= u <= NU:
                    turn_probs(u - 1)
                if u >= 2:
                    probs_v(u - 2)

            def past_keys(b):
                pe.wait_ge(s_kv[b % 4], 32 * (b // 4 + 1))
                o = take(pe, ("kpT", b))
                for s in range(2):
                    for j in range(4):
                        m = tr(o[:, j * 256 + s * P:j * 256 + (s + 1) * P], kp[:, b % 4, s * 512 + j * P:s * 512 + (j + 1) * P], ident)
                m.then_inc(filled(("kpT", b)), 1)

            def sample_scores(b):
                pe.wait_ge(s_qbd, b + 1)
                copied(pe, ("kpT", b))
                o = take(pe, ("ss", b))
                chain(o[:, 0:256], [(qbd[:, b % 2, j * P:(j + 1) * P], kpT[:, b % 2, j * 256:(j + 1) * 256]) for j in range(4)]
                      + [(hs16, negCs[:, b * 256:(b + 1) * 256])])
                chain(o[:, 256:384], [(qbd[:, b % 2, j * P:(j + 1) * P], kT[:, j, SEQ:T]) for j in range(4)]
                      + [(hs16, negCs[:, 2048:2176])]).then_inc(filled(("ss", b)), 1)

            def sample_turn(b):
                pe.wait_ge(s_exs, b + 1)
                o = take(pe, ("spt", b))
                for c in range(3):
                    m = tr(o[:, c * P:(c + 1) * P], sP[:, b % 2, c * P:(c + 1) * P], ident)
                m.then_inc(filled(("spt", b)), 1)

            def sample_v(b):
                copied(pe, ("spt", b))
                o = take(pe, ("spv", b))
                v = [vp[:, b % 4, 0:512], vp[:, b % 4, 512:1024], va[:, NP, :]]
                chain(o[:, 0:512], [(sPT[:, b % 2, c * P:(c + 1) * P], v[c]) for c in range(3)]).then_inc(filled(("spv", b)), 1)

            def sample_out(b):
                copied(pe, ("spv", b))
                o = take(pe, ("soT", b))
                for j in range(4):
                    m = mm(o[:, j * 16:(j + 1) * 16], om[:, b % 2, j * P:(j + 1) * P], tsel, start=True, stop=True)
                m.then_inc(filled(("soT", b)), 1)

            past_keys(0)
            for b in range(DEC_B + 3):
                if b + 1 < DEC_B:
                    past_keys(b + 1)
                if b >= 3:
                    sample_out(b - 3)
                if b < DEC_B:
                    sample_scores(b)
                if 1 <= b <= DEC_B:
                    sample_turn(b - 1)
                if 2 <= b <= DEC_B + 1:
                    sample_v(b - 2)

            turn_x("xT2", 1)
            copied(pe, *[("xT2", n) for n in range(NT)])
            pe.wait_ge(s_b, 16 * 3)
            pe.wait_ge(s_sl, 2)
            thirds(("a1",), None, x_parts, lhs=(wa1h, wa1l))
            copied(pe, ("a1", 0), ("a1", 1), ("a1", 2))
            for h in range(H_B):
                thirds(("qb", h), ("qb", h), x_parts)
                thirds(("kb", h), ("kb", h), x_parts)
                for g in range(3):
                    o = take(pe, ("la", h, g))
                    mm(o[:, 0:THIRD], wa2[:, h * P:(h + 1) * P], a1T[:, g * THIRD:(g + 1) * THIRD],
                       start=True, stop=True).then_inc(filled(("la", h, g)), 1)
                thirds(("rb", h, 0), ("rb", h, 0), x_parts)
                thirds(("rb", h, 1), ("rb", h, 1), x_parts)
                pe.wait_ge(s_ksr, h + 1)
                o = take(pe, ("kst", h, 0))
                for n in range(NP):
                    m = tr(o[:, n * P:(n + 1) * P], ks[:, n * P:(n + 1) * P], ident)
                m.then_inc(filled(("kst", h, 0)), 1)
                o = take(pe, ("kst", h, 1))
                tr(o[:, 0:P], ks[:, SEQ:T], ident).then_inc(filled(("kst", h, 1)), 1)

                def level(l):
                    if l < 7:
                        pe.wait_ge(s_xm, 7 * h + l + 1)
                        a = c = X[:, l % 2, :]
                    else:
                        a, c = kb, qb
                    o = take(pe, ("lv", h, l, 0))
                    for n in range(NP):
                        t = slice(n * P, (n + 1) * P)
                        m = mm(o[:, t], a[:, t], c[:, t], start=True, stop=True)
                    m.then_inc(filled(("lv", h, l, 0)), 1)
                    if l >= 3:
                        o = take(pe, ("lv", h, l, 1))
                        mm(o[:, 0:P], a[:, SEQ:T], c[:, SEQ:T], start=True, stop=True)\
                            .then_inc(filled(("lv", h, l, 1)), 1)

                weights(pe, ("vb", h, 1))
                for n in range(NT):
                    o = take(pe, ("vb", h, n))
                    pair_tile(o, ("vb", h, 0), n).then_inc(filled(("vb", h, n)), 1)
                    if n < 8:
                        level(n)
                w_last[("vb", h, 0)] = w_last[("vb", h, 1)] = ("vb", h, NT - 1)
                copied(pe, ("kst", h, 0), ("kst", h, 1), *[("lv", h, 7, g) for g in range(2)],
                       *[("lv", h, l, 0) for l in range(8)], *[("vb", h, n) for n in range(NT)])
                pe.wait_ge(s_qs, h + 1)

                def turn_out(n):
                    copied(pe, ("o", h, n))
                    o = take(pe, ("ot", h, n))
                    for c in range(2):
                        m = tr(o[:, c * P:(c + 1) * P], on[:, n % 3, c * P:(c + 1) * P], ident)
                    m.then_inc(filled(("ot", h, n)), 1)

                for n in range(NP):
                    o = take(pe, ("u", h, n))
                    mm(o[:, 0:DV], ktok[:, n, :], vb[:, n, :], start=True, stop=True).then_inc(filled(("u", h, n)), 1)
                    t = slice(n * P, (n + 1) * P)
                    pairs = [(AT[:, t], vb[:, n, :])]
                    if n > 0:
                        copied(pe, ("u", h, n - 1))
                        pairs.append((qs[:, t], St[:, n % 3, :]))
                    o = take(pe, ("o", h, n))
                    chain(o[:, 0:DV], pairs).then_inc(filled(("o", h, n)), 1)
                    if n >= 2:
                        turn_out(n - 2)
                pe.wait_ge(s_s0, 16 * (h + 1))
                pe.wait_ge(s_qsm, h + 1)
                o = take(pe, ("o", h, NP))
                chain(o[:, 0:DV], [(AT[:, SEQ:T], vb[:, NP, :])]
                      + [(qsm[:, b * P:(b + 1) * P], S0[:, b, :]) for b in range(DEC_B)])\
                    .then_inc(filled(("o", h, NP)), 1)
                turn_out(NP - 2)
                for c in range(4):
                    o = take(pe, ("us", h, c))
                    for b in range(2):
                        m = mm(o[:, b * DV:(b + 1) * DV], ksm[:, 2 * c + b, :], vb[:, NP, :], start=True, stop=True)
                    m.then_inc(filled(("us", h, c)), 1)
                    if c < 2:
                        turn_out(NP - 1 + c)

            for j in range(KT):
                thirds(("ga", j), ("ga", j), x_parts)
                thirds(("gb", j), ("gb", j), x_parts)
            pe.wait_ge(s_ol2, 4)
            for j in range(KT):
                thirds(("ya", j), ("ya", j), [lambda k, a=a: a[:, k, :] for a in (oah, oal)], kt=4)
            pe.wait_ge(s_ol2, 4 + KT)
            for j in range(KT):
                thirds(("yb", j), ("yb", j), [lambda k: obh[k // 4][:, k % 4, :], lambda k: obl[:, k, :]])

            def turn_x1(n):
                pe.wait_ge(s_x1, n + 1)
                o = take(pe, ("x1T", n))
                for k in range(KT):
                    m = tr(o[:, k * P:(k + 1) * P], x1[:, n, k * P:(k + 1) * P], ident)
                m.then_inc(filled(("x1T", n)), 1)

            for c in range(2):
                pe.wait_ge(s_wol, 4 * c + 4)
                for n in range(NT):
                    if c == 0 and n % 3 == 0:
                        pe.wait_ge(s_mt, 3 * (KT - 1) + n // 3 + 1)
                    t = slice(n * P, (n + 1) * P)
                    o = take(pe, ("wo", c, n))
                    pairs = []
                    for k in range(KT):
                        pairs += split3(mh[:, k, t], ml[:, k, t], woh[c][:, k, :], wol[c][:, k, :])
                    chain(o[:, 0:512], pairs).then_inc(filled(("wo", c, n)), 1)
                    if c == 1 and n >= 2:
                        turn_x1(n - 2)
            turn_x1(NT - 2)
            turn_x1(NT - 1)
            copied(pe, *[("x1T", n) for n in range(NT)])

            pe.wait_ge(s_xh, NT)
            copied(pe, *[("wo", 1, n) for n in range(NT)])

            def up(j, d, v, g):
                if g == 0:
                    pe.wait_ge(s_wl, 4 * j + 2 * d + v + 1)
                b, n = up_use(j, d, v, g)
                t = slice(g * THIRD, (g + 1) * THIRD)
                if 6 * d + 3 * v + g >= 4:
                    pe.wait_ge(up_free[b], n)
                pairs = []
                for k in range(KT):
                    pairs += split3(wuh[:, d % 2, v, k, :], wul[:, d % 2, v, k, :], x1h[:, k, t], x1l[:, k, t])
                chain(bank[:, b, 0:THIRD], pairs).then_inc(up_full[b], 1)

            def new_columns(j, d):
                pe.wait_ge(s_cg, 4 * j + 2 * d + 4)
                if d:
                    pe.wait_ge(cn_free, 2 * j + d)
                for v in range(2):
                    m = tr(bank[0:18, 7, v * P:(v + 1) * P], cn[:, v, :], ident)
                m.then_inc(cn_full, 1)

            def down(j, d, half_tiles):
                if half_tiles and half_tiles[0] == 0:
                    pe.wait_ge(s_hl, 2 * j + d + 1)
                    pe.wait_ge(s_dl, 2 * j + d + 1)
                for w in half_tiles:
                    b, n = dn_use(j, d, w)
                    t, c = slice(w // 2 * P, (w // 2 + 1) * P), slice(w % 2 * 512, (w % 2 + 1) * 512)
                    if 18 * d + w >= 3:
                        pe.wait_ge(dn_free[b], n)
                    e = d % 2
                    chain(bank[:, 4 + b, :], split3(hh[:, e, t], hl[:, e, t], wdh[:, e, c], wdl[:, e, c]))\
                        .then_inc(dn_full[b], 1)

            def chunk(j, d):
                for g in range(6):
                    up(j, d, g // 3, g % 3)
                    if d and g == 2:
                        new_columns(j, d - 1)
                    if d:
                        down(j, d - 1, DOWN_AFTER[g])

            in_pairs(pe, chunk)
            new_columns(0, NC_FF - 1)
            down(0, NC_FF - 1, range(2 * NT))

            for b in range(4):
                pe.wait_ge(up_free[b], 6 * NC_FF // 4)
            for b in range(3):
                pe.wait_ge(dn_free[b], 6 * NC_FF)
            pe.wait_ge(cn_free, NC_FF)

            def embed_turn(n):
                pe.wait_ge(s_x2, n + 1)
                o = take(pe, ("x2T", n))
                for k in range(KT):
                    m = tr(o[:, k * P:(k + 1) * P], x1[:, n, k * P:(k + 1) * P], ident)
                m.then_inc(filled(("x2T", n)), 1)
                pe.wait_ge(s_pin[n % 2], 16 * (n // 2 + 1))
                o = take(pe, ("pT", n))
                for k in range(2):
                    m = tr(o[:, k * P:(k + 1) * P], pin[:, n % 2, k * P:(k + 1) * P], ident)
                m.then_inc(filled(("pT", n)), 1)

            def embed(n):
                if n == 0:
                    pe.wait_ge(s_pl, KT + 2)
                copied(pe, ("x2T", n), ("pT", n))
                for name, w, a, kt in (("pg", (plgh, plgl), (x2h, x2l), KT), ("pp", (plh, pll), (pTh, pTl), 2)):
                    o = take(pe, (name, n))
                    for c in range(2):
                        cc = slice(c * 512, (c + 1) * 512)
                        pairs = []
                        for k in range(kt):
                            pairs += split3(a[0][:, n % 2, k, :], a[1][:, n % 2, k, :], w[0][:, k, cc], w[1][:, k, cc])
                        m = chain(o[:, cc], pairs)
                    m.then_inc(filled((name, n)), 1)

            embed_turn(0)
            for n in range(NT):
                if n + 1 < NT:
                    embed_turn(n + 1)
                embed(n)

        @block.scalar
        def _(act):
            steps = [0]

            def link(ins):
                steps[0] += 1
                ins.then_inc(s_act, 1)
                act.wait_ge(s_act, steps[0])

            def copy(out, in_, scale=1.0):
                return act.activation(out, in_, ACT.Copy, scale=scale)

            def split_hi(*names):
                for n in names:
                    if n < FIRST_UP:
                        if n >= W_SLOTS:
                            past_pe(act, w_last[chunks[n - W_SLOTS][0]])
                        act.wait_ge(w_in_sem[n % W_SLOTS], 16 * (n // W_SLOTS + 1))
                        kt = chunks[n][2]
                        copy(ringh[:, n % W_SLOTS, 0:kt], ring[:, n % W_SLOTS, 0:kt]).then_inc(s_rh, 1)

            def x_hi(key):
                for n in range(NT):
                    o = product(act, (key, n))
                    copy(xh[:, :, n * P:(n + 1) * P], o.rearrange("p (k t) -> p k t", k=KT)).then_inc(s_xh1, 1)

            x_hi("xT")
            o = product(act, "cacheT")
            copy(cacheT, o[:, 0:704].rearrange("p (c r) -> p c r", c=44)).then_inc(drained("cacheT"), 1)
            act.wait_ge(s_small, 32)
            past_pe(act, ("xT", NT - 1), "cacheT", "cwT")
            copy(wfh, wf).then_inc(s_sm, 1)
            split_hi(0, 1, 2)
            past_pe(act, ("lfp", 1))
            for g in range(3):
                o = product(act, ("f", g))
                act.activation(fz[:, g * THIRD:(g + 1) * THIRD], o[0:H_A, 0:THIRD], ACT.Identity, bias=bfg)\
                    .then_inc(drained(("f", g)), 1)
            copied(act, ("f", 0), ("f", 1), ("f", 2))
            link(act.activation(fa, fz, ACT.Abs))
            link(act.activation(fa, fa, ACT.Exp, scale=-1.0))
            act.activation(fa, fa, ACT.Ln, bias=one[0:H_A, :]).then_inc(s_fz, 1)
            for j in range(4):
                for g in range(3):
                    o = product(act, ("qa", j, g))
                    copy(qT[:, j, g * THIRD:(g + 1) * THIRD], o[:, 0:THIRD], DH ** -0.5).then_inc(drained(("qa", j, g)), 1)
                split_hi(j + 3)
            for j in range(4):
                split_hi(j + 7)
            for q in range(2):
                for n in range(NT):
                    o = product(act, ("va", q, n))
                    copy(va[:, n, q * 256:(q + 1) * 256], o[:, 0:256]).then_inc(drained(("va", q, n)), 1)
                split_hi(2 * q + 11, 2 * q + 12)

            def bias_rows(h):
                if h == 0:
                    copied(act, ("kt", NT - 1), ("kt", NT - 2))
                if h >= 2:
                    act.wait_ge(s_max, NP * (h - 1))
                    act.wait_ge(s_dg, h - 1)
                o = product(act, ("cb", h))
                copy(cb[:, h % 2, :], o).then_inc(drained(("cb", h)), 1)

            def probs(u):
                h, i = UNITS[u]
                act.wait_ge(s_max, u + 1)
                n = (i + 1) * P
                act.activation(S[:, u % 2, 0:n], S[:, u % 2, 0:n], ACT.Exp, bias=nm[:, u % 4:u % 4 + 1],
                               accum_out=rs[:, u % 4:u % 4 + 1]).then_inc(s_exp, 1)

            def copy_probs(u):
                if u % 2 == 1:
                    h, i = UNITS[u]
                    o = product(act, ("pt", u))
                    if u >= 2:
                        past_pe(act, ("pv", u - 2))
                    copy(PT[:, u % 2, 0:(i + 1) * P], o[:, 0:(i + 1) * P]).then_inc(drained(("pt", u)), 1)

            NU = len(UNITS)
            bias_rows(0)
            for u in range(NU + 2):
                if u < NU:
                    if u % 8 == 6 and UNITS[u][0] + 1 < H_A:
                        bias_rows(UNITS[u][0] + 1)
                    if u >= 4:
                        copied(act, ("pv", u - 4))
                    probs(u)
                if 1 <= u <= NU:
                    copy_probs(u - 1)
                if u >= 2:
                    h, i = UNITS[u - 2]
                    if h % 2 == 1 and i == 0:
                        o = product(act, ("oT", h // 2))
                        copy(oaT[:, h // 2, 0:SEQ], o).then_inc(drained(("oT", h // 2)), 1)

            def past_turned(b):
                o = product(act, ("kpT", b))
                if b >= 2:
                    past_pe(act, ("ss", b - 2))
                copy(kpT[:, b % 2, :], o).then_inc(drained(("kpT", b)), 1)

            past_pe(act, ("pv", NU - 1), ("oT", 3))
            past_turned(0)
            for b in range(DEC_B + 1):
                if b + 1 < DEC_B:
                    past_turned(b + 1)
                if b >= 1:
                    o = product(act, ("spt", b - 1))
                    if b >= 3:
                        past_pe(act, ("spv", b - 3))
                    copy(sPT[:, (b - 1) % 2, :], o[:, 0:384]).then_inc(drained(("spt", b - 1)), 1)
                if b < DEC_B:
                    act.wait_ge(s_smx, b + 1)
                    if b >= 2:
                        past_pe(act, ("spt", b - 2))
                    o = product(act, ("ss", b))
                    act.activation(sP[:, b % 2, 256:384], sN[:, b % 2, :], ACT.Exp, bias=nm[:, b % 2:b % 2 + 1],
                                   accum_out=rsb[:, b % 2:b % 2 + 1])
                    act.activation(sP[:, b % 2, 0:256], o[:, 0:256], ACT.Exp, bias=nm[:, b % 2:b % 2 + 1],
                                   accum_out=rs[:, b % 2:b % 2 + 1]).then_inc(s_exs, 1)

            copied(act, *[("soT", b) for b in range(DEC_B)], *[("spv", b) for b in range(DEC_B)])
            x_hi("xT2")
            act.wait_ge(s_b, 48)
            copy(wa1h, wa1).then_inc(s_sm, 1)

            act.wait_ge(s_ov, 32)
            act.wait_ge(s_ol, 32)
            act.wait_ge(s_qbd, DEC_B)
            act.wait_ge(s_cols, 32)
            act.wait_ge(s_oas, 16)
            for g in range(3):
                o = product(act, ("a1", g))
                copy(a1T[:, g * THIRD:(g + 1) * THIRD], o[0:RANK, 0:THIRD]).then_inc(drained(("a1", g)), 1)
            for h in range(H_B):
                for g in range(3):
                    o = product(act, ("qb", h, g))
                    copy(qb[:, g * THIRD:(g + 1) * THIRD], o[:, 0:THIRD], DK ** -0.5).then_inc(drained(("qb", h, g)), 1)
                m = 12 + 6 * h
                split_hi(m + 3)
                for g in range(3):
                    o = product(act, ("la", h, g))
                    act.activation(zb[:, g * THIRD:(g + 1) * THIRD], o[:, 0:THIRD], ACT.Identity, bias=ba2[:, h:h + 1])\
                        .then_inc(drained(("la", h, g)), 1)
                split_hi(m + 4)
                copied(act, *[("la", h, g) for g in range(3)])
                if h:
                    past_pe(act, ("lv", h - 1, 6, 1))
                link(act.activation(X[:, 0, :], zb, ACT.Abs))
                link(act.activation(X[:, 0, :], X[:, 0, :], ACT.Exp, scale=-1.0))
                act.activation(X[:, 0, :], X[:, 0, :], ACT.Ln, bias=one).then_inc(s_lnz, 1)
                act.wait_ge(s_bsc, h + 1)
                link(act.activation(X[:, 1, :], b16, ACT.Exp, scale=1.0 / TAU))
                if h:
                    copied(act, ("u", h - 1, NP - 1), *[("us", h - 1, c) for c in range(4)])
                act.wait_ge(s_kd, h + 1)
                link(act.activation(ks, ks, ACT.Exp, scale=1.0 / TAU))
                link(act.activation(dl[:, 0:8], b16[:, 0:SEQ].rearrange("p (n t) -> p n t", t=P)[:, :, P - 1], ACT.Exp,
                                    scale=1.0 / TAU))
                act.activation(dl[:, 8:16], b16[:, SEQ:T].rearrange("p (n t) -> p n t", t=DEC_T)[:, :, DEC_T - 1], ACT.Exp,
                               scale=1.0 / TAU).then_inc(s_ee, 1)
                for c in range(2):
                    if h:
                        act.wait_ge(s_obs, 16 * h)
                    for g in range(3):
                        o = product(act, ("rb", h, c, g))
                        act.activation(obT[:, c, g * THIRD:(g + 1) * THIRD], o[:, 0:THIRD], ACT.Silu)\
                            .then_inc(drained(("rb", h, c, g)), 1)
                    split_hi(m + 5 + c)
                for n in range(NT):
                    if n < 7:
                        act.wait_ge(s_xl, 7 * h + n + 1)
                        t = SEQ if HALVES[n] > 8 else T
                        act.activation(X[:, n % 2, 0:t], X[:, n % 2, 0:t], ACT.Exp, scale=1.0 / TAU).then_inc(s_xe, 1)
                    o = product(act, ("vb", h, n))
                    copy(vb[:, n, :], o[:, 0:DV]).then_inc(drained(("vb", h, n)), 1)
                split_hi(m + 7, m + 8)
                for n in range(NT):
                    o = product(act, ("o", h, n))
                    if n:
                        act.wait_ge(s_ssq, NT * h + n)
                    act.activation(sq, o[:, 0:DV], ACT.Square, accum_out=ss[:, n:n + 1]).then_inc(s_ssq, 1)
                    act.wait_ge(s_rst, NT * h + n + 1)
                    if n >= 3:
                        past_pe(act, ("ot", h, n - 3))
                    act.activation(on[:, n % 3, :], o[:, 0:DV], ACT.Copy, scale=rstd[:, n:n + 1])\
                        .then_inc(drained(("o", h, n)), 1)

            act.wait_ge(s_ost, 32 * H_B)
            for j in range(KT):
                for q, (name, gate) in enumerate((("ga", gate_a), ("gb", gate_b))):
                    for g in range(3):
                        o = product(act, (name, j, g))
                        act.activation(gate[:, j, g * THIRD:(g + 1) * THIRD], o[:, 0:THIRD], ACT.Sigmoid)\
                            .then_inc(drained((name, j, g)), 1)
                    split_hi(w_index[(name, j)] + 3)
            act.wait_ge(s_oai, 16)
            past_pe(act, ("gb", KT - 1, 2))
            for k in range(4):
                copy(oah[:, k, :], oar[:, k, :]).then_inc(s_oh, 1)
            for j in range(KT):
                past_pe(act, ("ya", j, 2))
                split_hi(w_index[("ya", j)] + 3)
                if j == 3:
                    act.wait_ge(s_obi, 64)
                if j >= 4:
                    copy(obh[0][:, j - 4, :], obr[:, j - 4, :]).then_inc(s_oh, 1)
            for k in range(4):
                copy(obh[1][:, k, :], obr[:, k + 4, :]).then_inc(s_oh, 1)
            for j in range(KT):
                for g in range(3):
                    n = 3 * j + g
                    act.wait_ge(s_mr, n + 1)
                    t = slice(g * THIRD, (g + 1) * THIRD)
                    copy(mh[:, j, t], gate_a[:, j, t]).then_inc(s_mh, 1)
                split_hi(w_index[("yb", j)] + 3)
                if j >= 4:
                    i = w_index[("yb", j)] % W_SLOTS
                    act.wait_ge(s_wo[0], 16)
                    past_pe(act, w_last[("yb", j)])
                    copy(woh[0][:, 2 * i:2 * i + 2, :], wor[0][:, 2 * i:2 * i + 2, :]).then_inc(s_woh, 1)
            act.wait_ge(s_wo[1], 16)
            for i in range(4):
                copy(woh[1][:, 2 * i:2 * i + 2, :], wor[1][:, 2 * i:2 * i + 2, :]).then_inc(s_woh, 1)
            for n in range(NT):
                o = product(act, ("x1T", n))
                copy(x1h[:, :, n * P:(n + 1) * P], o.rearrange("p (k t) -> p k t", k=KT)).then_inc(s_xh, 1)
                copy(x1[:, n, :], x1[:, n, :], ALPHA).then_inc(s_xa, 1)

            def up_hi(j, d, v):
                act.wait_ge(w_in_sem[2 * (d % 2) + v], 16 * UP_ROUND + 16 * j + 16 * (d // 2 + 1))
                copy(wuh[:, d % 2, v], rawu[:, d % 2, v]).then_inc(s_wh, 1)

            def new_columns(j, d):
                act.wait_ge(cn_full, 2 * j + d + 1)
                if d:
                    act.wait_ge(s_ocn, 64 * j + 32 * d)
                copy(cno, bank[0:18, 7, 0:256]).then_inc(cn_free, 1)

            def halves(j, d):
                more = d != NC_FF - 1
                for v in range(2):
                    act.wait_ge(s_cg, 4 * j + 2 * d + v + 1)
                    u = U[:, v, :]
                    for g in range(3):
                        b, n = up_use(j, d, v, g)
                        act.wait_ge(up_full[b], n + 1)
                        if g < 2:
                            copy(u[:, 2 + g * THIRD:2 + (g + 1) * THIRD], bank[:, b, 0:THIRD]).then_inc(up_free[b], 1)
                        else:
                            copy(u[:, 2 + 2 * THIRD:2 + SEQ], bank[:, b, 0:SEQ - 2 * THIRD])
                            copy(u[:, 2 + SEQ:146 + SEQ].rearrange("p (b t) -> p b t", t=18)[:, :, 2:18],
                                 bank[:, b, SEQ - 2 * THIRD:THIRD].rearrange("p (b t) -> p b t", t=16)).then_inc(up_free[b], 1)
                    if v == 0:
                        if more:
                            up_hi(j, d + 1, 0)
                            up_hi(j, d + 1, 1)
                        if d:
                            new_columns(j, d - 1)
                        act.wait_ge(s_wdi[d % 2], 16 * j + 16 * (d // 2 + 1))
                        copy(wdh[:, d % 2, :], rawd[:, d % 2, :]).then_inc(s_dh, 1)
                act.wait_ge(s_conv, 4 * j + 2 * d + 2)
                act.activation(y[:, 1, 0:1168], y[:, 1, 0:1168], ACT.Gelu_apprx_tanh).then_inc(s_gel, 1)
                act.wait_ge(s_hm, 2 * j + d + 1)
                copy(hh[:, d % 2, 0:SEQ], y[:, 0, 0:SEQ])
                copy(hh[:, d % 2, SEQ:T].rearrange("p (b t) -> p b t", t=DEC_T),
                     y[:, 0, SEQ + 2:SEQ + 146].rearrange("p (b t) -> p b t", t=18)[:, :, 0:DEC_T]).then_inc(s_hh, 1)

            past_pe(act, ("wo", 1, NT - 1))
            for v in range(2):
                up_hi(0, 0, v)
            in_pairs(act, halves)
            new_columns(0, NC_FF - 1)

            def ple_hi(k, w, h):
                act.wait_ge(s_ple, 32)
                copy(h[:, k, :], w[:, k, :]).then_inc(s_ph, 1)

            for b in range(4):
                act.wait_ge(up_full[b], 6 * NC_FF // 4)
            for k in range(KT):
                ple_hi(k, rplg, plgh)
            for k in range(2):
                ple_hi(k, rpl, plh)

            def turn_in(n):
                o = product(act, ("x2T", n))
                if n >= 2:
                    past_pe(act, ("pg", n - 2))
                copy(x2h[:, n % 2], o.rearrange("p (k t) -> p k t", k=KT)).then_inc(s_x2h, 1)
                o = product(act, ("pT", n))
                if n >= 2:
                    past_pe(act, ("pp", n - 2))
                copy(pTh[:, n % 2], o[:, 0:256].rearrange("p (k t) -> p k t", k=2)).then_inc(s_x2h, 1)

            turn_in(0)
            for n in range(NT):
                if n + 1 < NT:
                    turn_in(n + 1)
                o = product(act, ("pg", n))
                if n >= 2:
                    copied(act, ("pp", n - 2))
                act.activation(sge[:, n % 2, :], o, ACT.Sigmoid).then_inc(drained(("pg", n)), 1)

        @block.vector
        def _(dve):
            steps = [0]

            def link(ins):
                steps[0] += 1
                ins.then_inc(s_dve, 1)
                dve.wait_ge(s_dve, steps[0])

            def stt(out, in0, scalar, in1, op0, op1):
                return dve.scalar_tensor_tensor(out=out, in0=in0, scalar=scalar, in1=in1, op0=op0, op1=op1)

            def rows(ap, n, w):
                return ap.rearrange("p (n w) -> p n w", w=w)[:, 0:n]

            def split_lo(*names):
                for n in names:
                    if n < FIRST_UP:
                        dve.wait_ge(s_rh, n + 1)
                        i, kt = n % W_SLOTS, chunks[n][2]
                        dve.tensor_tensor(ringl[:, i, 0:kt], ring[:, i, 0:kt], ringh[:, i, 0:kt].bitcast(F32), ALU.subtract)\
                            .then_inc(s_rl, 1)

            def x_lo(key, rounds):
                for n in range(NT):
                    o = product(dve, (key, n))
                    dve.wait_ge(s_xh1, NT * rounds + n + 1)
                    t = slice(n * P, (n + 1) * P)
                    dve.tensor_tensor(xl[:, :, t], o.rearrange("p (k t) -> p k t", k=KT), xh[:, :, t].bitcast(F32),
                                      ALU.subtract).then_inc(drained((key, n)), 1)

            x_lo("xT", 0)
            o = product(dve, "cwT")
            dve.tensor_copy(cwT, o[:, 0:176].rearrange("p (a c) -> p a c", a=4)).then_inc(drained("cwT"), 1)
            for n in range(2):
                o = product(dve, ("lfp", n))
                for c in range(4):
                    b = 4 * n + c
                    ins = dve.tensor_tensor_scan(negCs[:, b * 256:(b + 1) * 256], one[0:H_A, :].to_broadcast([H_A, 256]),
                                                 o[0:H_A, c * 256:(c + 1) * 256], 0.0, ALU.mult, ALU.subtract)
                ins.then_inc(drained(("lfp", n)), 1)
            dve.wait_ge(s_sm, 1)
            dve.tensor_tensor(wfl, wf, wfh.bitcast(F32), ALU.subtract).then_inc(s_sl, 1)
            split_lo(0, 1, 2)
            dve.wait_ge(s_fz, 1)
            stt(fz, fz, 0.0, fa, ALU.min, ALU.subtract).then_inc(s_lf8, 1)
            dve.wait_ge(s_lf8, 1)
            copied(dve, ("lfp", 0), ("lfp", 1))
            for b in range(DEC_B):
                dve.tensor_tensor_scan(negCs[:, 2048 + b * 16:2048 + (b + 1) * 16], one[0:H_A, :].to_broadcast([H_A, 16]),
                                       fz[:, SEQ + b * 16:SEQ + (b + 1) * 16], negCs[:, b * 256 + 255:b * 256 + 256],
                                       ALU.mult, ALU.subtract)
            dve.tensor_tensor_scan(negC[:, 0:SEQ], one[0:H_A, :].to_broadcast([H_A, SEQ]), fz[:, 0:SEQ], 0.0,
                                   ALU.mult, ALU.subtract).then_inc(s_negc, 1)
            split_lo(3, 4, 5, 6)
            for j in range(4):
                for g in range(3):
                    o = product(dve, ("ka", j, g))
                    dve.tensor_copy(kT[:, j, g * THIRD:(g + 1) * THIRD], o[:, 0:THIRD]).then_inc(drained(("ka", j, g)), 1)
                split_lo(j + 7)
            split_lo(11, 12, 13, 14)
            o = product(dve, "lfT")
            dve.tensor_copy(lfo, o[:, 0:72].rearrange("p (n h) -> p n h", n=NT)).then_inc(drained("lfT"), 1)
            for n in range(NT):
                o = product(dve, ("kt", n))
                if n >= 2:
                    dve.wait_ge(s_ok[n % 2], 16 * (n // 2))
                dve.tensor_copy(kst[:, n % 2, :], o[:, 0:512]).then_inc(drained(("kt", n)), 1)

            def row_max(u):
                h, i = UNITS[u]
                n = i * P
                o = product(dve, ("s", u))
                if i == NP - 1:
                    copied(dve, ("cb", h))
                    dve.wait_ge(s_dg, h + 1)
                if u >= 2:
                    past_pe(dve, ("pt", u - 2))
                m, v = mx[:, u % 4:u % 4 + 1], nm[:, u % 4:u % 4 + 1]
                init = -3e38
                if i:
                    link(dve.tensor_tensor_reduce(S[:, u % 2, 0:n], o[:, 0:n], cb[:, h % 2, 0:n], 1.0, -3e38, ALU.add,
                                                  ALU.max, m))
                    init = m
                dve.tensor_tensor_reduce(S[:, u % 2, n:n + P], o[:, n:n + P], dg[:, h % 2, n:n + P], 1.0, init,
                                         ALU.add, ALU.max, m).then_inc(drained(("s", u)), 1)
                copied(dve, ("s", u))
                dve.tensor_scalar(v, m, -1.0, None, ALU.mult).then_inc(s_max, 1)

            def copy_probs(u):
                if u % 2 == 0:
                    h, i = UNITS[u]
                    o = product(dve, ("pt", u))
                    if u >= 2:
                        past_pe(dve, ("pv", u - 2))
                    dve.tensor_copy(PT[:, u % 2, 0:(i + 1) * P], o[:, 0:(i + 1) * P]).then_inc(drained(("pt", u)), 1)

            def norm_out(u):
                h, i = UNITS[u]
                dve.wait_ge(s_exp, u + 1)
                link(dve.reciprocal(ri[:, u % 4:u % 4 + 1], rs[:, u % 4:u % 4 + 1]))
                if h >= 2 and h % 2 == 0 and i == NP - 1:
                    past_pe(dve, ("oT", h // 2 - 1))
                o = product(dve, ("pv", u))
                dve.tensor_scalar(oab[:, i, (h % 2) * DH:(h % 2 + 1) * DH], o[:, 0:DH], ri[:, u % 4:u % 4 + 1], None,
                                  ALU.mult).then_inc(drained(("pv", u)), 1)

            NU = len(UNITS)
            dve.wait_ge(s_ok[0], 16 * 5)
            dve.wait_ge(s_ok[1], 16 * 4)
            for u in range(NU + 2):
                if u < NU:
                    row_max(u)
                if 1 <= u <= NU:
                    copy_probs(u - 1)
                if u >= 2:
                    norm_out(u - 2)

            past_pe(dve, ("oT", 3))
            for b in range(DEC_B + 3):
                if b >= 3:
                    o = product(dve, ("soT", b - 3))
                    t = SEQ + 16 * (b - 3)
                    dve.tensor_copy(oaT[:, :, t:t + 16], o[:, 0:64].rearrange("p (j t) -> p j t", j=4))\
                        .then_inc(drained(("soT", b - 3)), 1)
                if b < DEC_B:
                    o = product(dve, ("ss", b))
                    q, qi = slice(b % 2, b % 2 + 1), slice(b % 4, b % 4 + 1)
                    if b >= 2:
                        dve.wait_ge(s_exs, b - 1)
                    link(dve.tensor_tensor_reduce(sN[:, b % 2, :], o[:, 256:384], win[:, 112 - 16 * b:240 - 16 * b], 1.0,
                                                  -3e38, ALU.add, ALU.max, mxb[:, q]))
                    link(dve.tensor_reduce(mx[:, q], o[:, 0:256], AX.X, ALU.max))
                    stt(nm[:, q], mx[:, q], mxb[:, q], neg1, ALU.max, ALU.mult).then_inc(s_smx, 1)
                if 2 <= b <= DEC_B + 1:
                    o = product(dve, ("spv", b - 2))
                    if b >= 4:
                        past_pe(dve, ("soT", b - 4))
                    q = slice((b - 2) % 4, (b - 2) % 4 + 1)
                    stt(om[:, b % 2, :], o[:, 0:512], ri[:, q], omask, ALU.mult, ALU.mult)\
                        .then_inc(drained(("spv", b - 2)), 1)
                if b < DEC_B:
                    q = slice(b % 2, b % 2 + 1)
                    dve.wait_ge(s_exs, b + 1)
                    dve.tensor_tensor(ri[:, qi], rs[:, q], rsb[:, q], ALU.add).then_inc(drained(("ss", b)), 1)
                    copied(dve, ("ss", b))
                    link(dve.reciprocal(ri[:, qi], ri[:, qi]))

            copied(dve, *[("soT", b) for b in range(DEC_B)])
            x_lo("xT2", 1)
            dve.wait_ge(s_sm, 2)
            dve.tensor_tensor(wa1l, wa1, wa1h.bitcast(F32), ALU.subtract).then_inc(s_sl, 1)
            dve.wait_ge(s_qbd, DEC_B)
            dve.wait_ge(s_b, 16 * 3)
            dve.wait_ge(s_cols, 32)
            dve.wait_ge(s_oas, 16)
            for h in range(H_B):
                m = 12 + 6 * h
                split_lo(m + 3)
                for g in range(3):
                    o = product(dve, ("kb", h, g))
                    dve.tensor_copy(kb[:, g * THIRD:(g + 1) * THIRD], o[:, 0:THIRD]).then_inc(drained(("kb", h, g)), 1)
                split_lo(m + 4)
                dve.wait_ge(s_lnz, h + 1)
                link(stt(zb, zb, 0.0, X[:, 0, :], ALU.min, ALU.subtract))
                dve.tensor_tensor_scan(b16, scanm, zb, 0.0, ALU.mult, ALU.add).then_inc(s_bsc, 1)
                dve.wait_ge(s_bsc, h + 1)
                if h:
                    past_pe(dve, ("kst", h - 1, 1))
                bp, bs = rows(b16[:, 0:SEQ], NP, P), rows(b16[:, SEQ:T], DEC_B, DEC_T)
                kp_, ks_ = rows(ks[:, 0:SEQ], NP, P), rows(ks[:, SEQ:T], DEC_B, DEC_T)
                dve.tensor_tensor(kp_, bp[:, :, P - 1:P].to_broadcast([P, NP, P]), bp, ALU.subtract)
                dve.tensor_tensor(ks_, bs[:, :, DEC_T - 1:DEC_T].to_broadcast([P, DEC_B, DEC_T]), bs, ALU.subtract)\
                    .then_inc(s_kd, 1)
                dve.wait_ge(s_ee, h + 1)
                dve.tensor_tensor(qs, qb, X[:, 1, :], ALU.mult).then_inc(s_qs, 1)
                dve.tensor_tensor(ks, ks, kb, ALU.mult).then_inc(s_ksr, 1)
                dve.wait_ge(s_qs, h + 1)
                split_lo(m + 5)

                def level_log(l):
                    if l >= 2:
                        past_pe(dve, ("lv", h, l - 2, 0))
                        if l - 2 >= 3:
                            past_pe(dve, ("lv", h, l - 2, 1))
                    hf = HALVES[l]
                    t = SEQ if hf > 8 else T
                    xv = X[:, l % 2, 0:t].rearrange("p (n a j) -> p n a j", a=2, j=hf)
                    bv = b16[:, 0:t].rearrange("p (n a j) -> p n a j", a=2, j=hf)
                    ref = bv[:, :, 0, hf - 1:hf].to_broadcast([P, t // (2 * hf), hf])
                    dve.tensor_tensor(xv[:, :, 0, :], ref, bv[:, :, 0, :], ALU.subtract)
                    dve.tensor_tensor(xv[:, :, 1, :], bv[:, :, 1, :], ref, ALU.subtract).then_inc(s_xl, 1)

                def level_scale(l):
                    hf = HALVES[l]
                    t = SEQ if hf > 8 else T
                    dve.wait_ge(s_xe, 7 * h + l + 1)
                    v = [a[:, 0:t].rearrange("p (n a j) -> p n a j", a=2, j=hf) for a in (X[:, l % 2, :], kb, qb)]
                    dve.tensor_tensor(v[0][:, :, 0, :], v[0][:, :, 0, :], v[1][:, :, 0, :], ALU.mult)
                    dve.tensor_tensor(v[0][:, :, 1, :], v[0][:, :, 1, :], v[2][:, :, 1, :], ALU.mult).then_inc(s_xm, 1)

                def level_take(l):
                    mask = levm[:, l * P:(l + 1) * P] if l < 7 else ident.bitcast(U32)
                    o = product(dve, ("lv", h, l, 0))
                    if l:
                        copied(dve, ("lv", h, l - 1, 0))
                    dve.copy_predicated(rows(AT[:, 0:SEQ], NP, P), mask.rearrange("p (a t) -> p a t", a=1).to_broadcast([P, NP, P]),
                                        rows(o, NP, P)).then_inc(drained(("lv", h, l, 0)), 1)
                    if l >= 3:
                        o = product(dve, ("lv", h, l, 1))
                        if l > 3:
                            copied(dve, ("lv", h, l - 1, 1))
                        dve.copy_predicated(AT[:, SEQ:T], mask, o[:, 0:P]).then_inc(drained(("lv", h, l, 1)), 1)

                level_log(0)
                o = product(dve, ("kst", h, 0))
                dve.tensor_copy(ktok, rows(o, NP, P)).then_inc(drained(("kst", h, 0)), 1)
                o = product(dve, ("kst", h, 1))
                dve.tensor_tensor(ksm, o[:, 0:P].rearrange("p (a t) -> p a t", a=1).to_broadcast([P, DEC_B, P]),
                                  bmask.rearrange("p (b a) -> p b a", a=1).to_broadcast([P, DEC_B, P]), ALU.mult)\
                    .then_inc(drained(("kst", h, 1)), 1)
                dve.wait_ge(s_at0, h + 1)
                for l in range(8):
                    if l + 1 < 7:
                        level_log(l + 1)
                    if l < 7:
                        level_scale(l)
                    level_take(l)
                    if l == 1:
                        split_lo(m + 6)

                def out_turned(n):
                    o = product(dve, ("ot", h, n))
                    for c in range(2):
                        v = obT[:, c, n * P:(n + 1) * P]
                        ins = stt(v, o[:, c * P:(c + 1) * P], ggla[:, 2 * h + c:2 * h + c + 1], v, ALU.mult, ALU.mult)
                    ins.then_inc(drained(("ot", h, n)), 1)

                for n in range(NP):
                    o = product(dve, ("u", h, n))
                    if n >= 2:
                        past_pe(dve, ("o", h, n - 2))
                    if n == 1 and h:
                        dve.wait_ge(s_ost, 32 * h)
                    if n == 0:
                        ins = dve.tensor_copy(St[:, 1, :], o[:, 0:DV])
                    else:
                        copied(dve, ("u", h, n - 1))
                        ins = stt(St[:, (n + 1) % 3, :], St[:, n % 3, :], dl[:, n:n + 1], o[:, 0:DV], ALU.mult, ALU.add)
                    ins.then_inc(drained(("u", h, n)), 1)
                    if n >= 2:
                        out_turned(n - 2)
                    if n == 3:
                        split_lo(m + 7, m + 8)
                out_turned(NP - 2)
                past_pe(dve, ("o", h, NP))
                for c in range(4):
                    o = product(dve, ("us", h, c))
                    for b in range(2):
                        v = S0[:, 2 * c + b, :]
                        ins = stt(v, v, dl[:, 8 + 2 * c + b:9 + 2 * c + b], o[:, b * DV:(b + 1) * DV], ALU.mult, ALU.add)
                    ins.then_inc(drained(("us", h, c)), 1)
                    if c < 2:
                        out_turned(NP - 1 + c)

            for j in range(KT):
                split_lo(w_index[("ga", j)] + 3, w_index[("gb", j)] + 3)
            def branch_lo(i, lo, raw, hi):
                dve.wait_ge(s_oh, i + 1)
                dve.tensor_tensor(lo, raw, hi.bitcast(F32), ALU.subtract).then_inc(s_ol2, 1)

            for k in range(4):
                branch_lo(k, oal[:, k, :], oar[:, k, :], oah[:, k, :])
            for j in range(KT):
                for g in range(3):
                    o = product(dve, ("ya", j, g))
                    copied(dve, ("ga", j, g))
                    v = gate_a[:, j, g * THIRD:(g + 1) * THIRD]
                    dve.tensor_tensor(v, o[:, 0:THIRD], v, ALU.mult).then_inc(drained(("ya", j, g)), 1)
                split_lo(w_index[("ya", j)] + 3)
                if j >= 4:
                    branch_lo(j, obl[:, j - 4, :], obr[:, j - 4, :], obh[0][:, j - 4, :])
            for k in range(4):
                branch_lo(8 + k, obl[:, 4 + k, :], obr[:, 4 + k, :], obh[1][:, k, :])

            def merged_lo(n):
                j, t = n // 3, slice(n % 3 * THIRD, (n % 3 + 1) * THIRD)
                dve.wait_ge(s_mh, n + 1)
                dve.tensor_tensor(ml[:, j, t], gate_a[:, j, t], mh[:, j, t].bitcast(F32), ALU.subtract).then_inc(s_mt, 1)

            def wo_lo(q, c, i):
                dve.wait_ge(s_woh, q + 1)
                k = slice(2 * i, 2 * i + 2)
                dve.tensor_tensor(wol[c][:, k, :], wor[c][:, k, :], woh[c][:, k, :].bitcast(F32), ALU.subtract).then_inc(s_wol, 1)

            for j in range(KT):
                for g in range(3):
                    o = product(dve, ("yb", j, g))
                    copied(dve, ("gb", j, g))
                    v = gate_b[:, j, g * THIRD:(g + 1) * THIRD]
                    dve.tensor_tensor(v, o[:, 0:THIRD], v, ALU.mult).then_inc(drained(("yb", j, g)), 1)
                    if 3 * j + g >= 1:
                        merged_lo(3 * j + g - 1)
                split_lo(w_index[("yb", j)] + 3)
                if j >= 5:
                    wo_lo(j - 5, 0, w_index[("yb", j - 1)] % W_SLOTS)
            merged_lo(3 * KT - 1)
            wo_lo(3, 0, w_index[("yb", KT - 1)] % W_SLOTS)

            norms = [0]

            def stats(z):
                q = norms[0] % 4
                for c in range(2):
                    ins = dve.bn_stats(bnst[:, q, c * 6:(c + 1) * 6], z[:, c * 512:(c + 1) * 512])
                link(ins)
                dve.bn_aggr(mv[:, q, :], bnst[:, q, :]).then_inc(s_var, 1)
                norms[0] += 1

            def normed(z, out, gain, bias):
                q = (norms[0] - 1) % 4
                dve.wait_ge(s_lrs, norms[0])
                link(dve.tensor_scalar(z, z, mv[:, q, 0:1], lrs[:, q:q + 1], ALU.subtract, ALU.mult))
                link(dve.tensor_tensor(z, z, gain, ALU.mult))
                return dve.tensor_tensor(out, z, bias, ALU.add)

            def x1_lo(n):
                dve.wait_ge(s_xh, n + 1)
                o = product(dve, ("x1T", n))
                t = slice(n * P, (n + 1) * P)
                dve.tensor_tensor(x1l[:, :, t], o.rearrange("p (k t) -> p k t", k=KT), x1h[:, :, t].bitcast(F32),
                                  ALU.subtract).then_inc(drained(("x1T", n)), 1)

            def add_x(c, n):
                o = product(dve, ("wo", c, n))
                z = x1[:, n, c * 512:(c + 1) * 512]
                stt(z, z, ALPHA, o[:, 0:512], ALU.mult, ALU.add).then_inc(drained(("wo", c, n)), 1)

            for n in range(NT):
                dve.wait_ge(s_xin[n], 16)
                add_x(0, n)
                if n >= 5:
                    wo_lo(4 + n - 5, 1, n - 5)
            dve.wait_ge(s_g1, 32)
            for n in range(NT):
                add_x(1, n)
                copied(dve, ("wo", 1, n))
                z = x1[:, n, :]
                stats(z)
                normed(z, z, g1, b1).then_inc(s_x1, 1)
                if n >= 2:
                    x1_lo(n - 2)
            x1_lo(NT - 2)
            x1_lo(NT - 1)

            def up_lo(j, d, v):
                dve.wait_ge(s_wh, 4 * j + 2 * d + v + 1)
                dve.tensor_tensor(wul[:, d % 2, v], rawu[:, d % 2, v], wuh[:, d % 2, v].bitcast(F32), ALU.subtract)\
                    .then_inc(s_wl, 1)

            def convolve(j, d, v):
                c = 2 * j + d
                for g in range(3):
                    b, n = up_use(j, d, v, g)
                    dve.wait_ge(up_free[b], n + 1)
                dve.wait_ge(s_up, 4 * j + 2 * d + v + 1)
                u, yv = U[:, v, :], y[:, v, 0:1168]
                w = [cwT[:, a, bass.ds(c + v * NC_FF, 1)] for a in range(4)]
                dve.tensor_scalar(yv, u[:, 0:1168], w[0], w[3], ALU.mult, ALU.add).then_inc(s_cv1, 1)
                dve.wait_ge(s_cv1, 4 * j + 2 * d + v + 1)
                stt(yv, u[:, 1:1169], w[1], yv, ALU.mult, ALU.add).then_inc(s_cv2, 1)
                dve.wait_ge(s_cv2, 4 * j + 2 * d + v + 1)
                stt(yv, u[:, 2:1170], w[2], yv, ALU.mult, ALU.add).then_inc(s_conv, 1)

            def add_down(j, d, half_tiles):
                for w in half_tiles:
                    b, m = dn_use(j, d, w)
                    dve.wait_ge(dn_full[b], m + 1)
                    z = x1[:, w // 2, (w % 2) * 512:(w % 2 + 1) * 512]
                    dve.tensor_tensor(z, z, bank[:, 4 + b, :], ALU.add).then_inc(dn_free[b], 1)

            def halves(j, d):
                def before(g):
                    if d:
                        add_down(j, d - 1, DOWN_AFTER[g])

                if d:
                    dve.wait_ge(s_hl, 2 * j + d)
                before(2)
                convolve(j, d, 0)
                before(3)
                if d != NC_FF - 1:
                    up_lo(j, d + 1, 0)
                    up_lo(j, d + 1, 1)
                before(4)
                dve.wait_ge(s_dh, 2 * j + d + 1)
                dve.tensor_tensor(wdl[:, d % 2, :], rawd[:, d % 2, :], wdh[:, d % 2, :].bitcast(F32), ALU.subtract)\
                    .then_inc(s_dl, 1)
                convolve(j, d, 1)
                dve.wait_ge(s_gel, 2 * j + d + 1)
                dve.tensor_tensor(y[:, 0, 0:1168], y[:, 0, 0:1168], y[:, 1, 0:1168], ALU.mult).then_inc(s_hm, 1)
                dve.wait_ge(s_hh, 2 * j + d + 1)
                e = d % 2
                dve.tensor_tensor(hl[:, e, 0:SEQ], y[:, 0, 0:SEQ], hh[:, e, 0:SEQ].bitcast(F32), ALU.subtract)
                dve.tensor_tensor(rows(hl[:, e, SEQ:T], DEC_B, DEC_T), rows(y[:, 0, SEQ + 2:SEQ + 146], DEC_B, 18)[:, :, 0:DEC_T],
                                  rows(hh[:, e, SEQ:T].bitcast(F32), DEC_B, DEC_T), ALU.subtract).then_inc(s_hl, 1)

            dve.wait_ge(s_xa, NT)
            for v in range(2):
                up_lo(0, 0, v)
            in_pairs(dve, halves)

            def ple_lo(k, i, w, h, l):
                dve.wait_ge(s_ph, i + 1)
                dve.tensor_tensor(l[:, k, :], w[:, k, :], h[:, k, :].bitcast(F32), ALU.subtract).then_inc(s_pl, 1)

            def second(n):
                z = x1[:, n, :]
                stats(z)
                normed(z, z, g2, b2).then_inc(s_x2, 1)

            def turn_lo(n):
                dve.wait_ge(s_x2h, 2 * n + 2)
                o = product(dve, ("x2T", n))
                dve.tensor_tensor(x2l[:, n % 2], o.rearrange("p (k t) -> p k t", k=KT), x2h[:, n % 2].bitcast(F32),
                                  ALU.subtract).then_inc(drained(("x2T", n)), 1)
                o = product(dve, ("pT", n))
                dve.tensor_tensor(pTl[:, n % 2], o[:, 0:256].rearrange("p (k t) -> p k t", k=2), pTh[:, n % 2].bitcast(F32),
                                  ALU.subtract).then_inc(drained(("pT", n)), 1)

            add_down(0, NC_FF - 1, range(2 * NT))
            dve.wait_ge(s_g2, 64)
            for b in range(3):
                dve.wait_ge(dn_free[b], 6 * NC_FF)
            second(0)
            for k in range(KT):
                ple_lo(k, k, rplg, plgh, plgl)
            for k in range(2):
                ple_lo(k, KT + k, rpl, plh, pll)
            second(1)
            turn_lo(0)
            dve.wait_ge(s_ocn, 32 * NC_FF)
            for n in range(NT):
                if n + 2 < NT:
                    second(n + 2)
                if n + 1 < NT:
                    turn_lo(n + 1)
                copied(dve, ("pg", n))
                o = product(dve, ("pp", n))
                if n >= 3:
                    dve.wait_ge(s_oy[n % 3], 16 * (n // 3))
                z = z3[:, n % 3, :]
                dve.tensor_tensor(z, o, sge[:, n % 2, :], ALU.mult).then_inc(drained(("pp", n)), 1)
                copied(dve, ("pp", n))
                link(stt(z, x1[:, n, :], ALPHA, z, ALU.mult, ALU.add))
                stats(z)
                normed(z, z, g3, b3).then_inc(s_y, 1)

        @block.gpsimd
        def _(pool):
            copied(pool, *[("va", q, n) for q in range(2) for n in range(NT)])
            rows_p, rows_s = (lambda ap: ap[0, 0].rearrange("t h d -> t (h d)")), (lambda ap: ap[0].rearrange("b t h d -> (b t) (h d)"))
            pool.dma_start(rows_p(fv_p).rearrange("(n p) c -> p n c", p=P), va[:, 0:NP, :]).then_inc(s_ov, 16)
            pool.dma_start(rows_s(fv_s), va[:, NP, :]).then_inc(s_ov, 16)
            copied(pool, "lfT")
            with nc.allow_non_contiguous_dma(reason="8 log-forgets of a token in a row"):
                pool.dma_start(fl_p[0, 0].rearrange("(n p) h -> p n h", p=P), lfo[:, 0:NP, :]).then_inc(s_ol, 16)
                pool.dma_start(fl_s[0].rearrange("b t h -> (b t) h"), lfo[:, NP, :]).then_inc(s_ol, 16)
            for n in range(NT):
                copied(pool, ("kt", n))
                dst = rows_p(fk_p)[n * P:(n + 1) * P, :] if n < NP else rows_s(fk_s)
                pool.dma_start(dst, kst[:, n % 2, :]).then_inc(s_ok[n % 2], 16)

            for h in range(H_A):
                copied(pool, ("cb", h))
                if h >= 2:
                    pool.wait_ge(s_max, NP * (h - 1))
                pool.tensor_tensor(dg[:, h % 2, :].rearrange("p (n t) -> p n t", t=P), cb[:, h % 2, :].rearrange("p (n t) -> p n t", t=P),
                                   causal.rearrange("p (a t) -> p a t", a=1).to_broadcast([P, NP, P]), ALU.add).then_inc(s_dg, 1)

            NU = len(UNITS)
            copied(pool, ("pv", NU - 1), ("pv", NU - 2), ("oT", 3))
            pool.memset(at(off["qbd"], 1312), 0.0).then_inc(s_pool, 1)
            pool.wait_ge(s_pool, 1)
            for b in range(DEC_B):
                if b >= 2:
                    past_pe(pool, ("ss", b - 2))
                for hh in range(2):
                    v = qbd[hh * DH:(hh + 1) * DH, b % 2, hh * 16:hh * 16 + 640].rearrange("p (j x) -> p j x", x=160)[:, :, 0:16]
                    ins = pool.tensor_copy(v, qT[hh * DH:(hh + 1) * DH, :, SEQ + 16 * b:SEQ + 16 * (b + 1)])
                ins.then_inc(s_qbd, 1)

            pool.wait_ge(s_ov, 32)
            copied(pool, ("soT", DEC_B - 1), ("soT", DEC_B - 2), ("spv", DEC_B - 1))
            pool.dma_start(oa_out, oaT).then_inc(s_oas, 16)
            past_pe(pool, ("xT2", NT - 1))
            pool.memset(qsm, 0.0).then_inc(s_pool, 1)
            for h in range(H_B):
                if h:
                    pool.wait_ge(s_ost, 32 * h)
                pool.dma_start(S0, state_gla[0].rearrange("b h c v -> h c b v")[h]).then_inc(s_s0, 16)
                pool.memset(AT, 0.0).then_inc(s_at0, 1)
                if h == 0:
                    pool.wait_ge(s_pool, 2)
                pool.wait_ge(s_qs, h + 1)
                pool.tensor_copy(qsm.rearrange("p (b x) -> p b x", x=P + DEC_T)[:, :, 0:DEC_T],
                                 qs[:, SEQ:T].rearrange("p (b t) -> p b t", t=DEC_T)).then_inc(s_qsm, 1)
                for n in range(NT):
                    pool.wait_ge(s_ssq, NT * h + n + 1)
                    pool.tensor_scalar(ms[:, n:n + 1], ss[:, n:n + 1], 1.0 / DV, LN_EPS, ALU.mult, ALU.add).then_inc(s_msq, 1)
                    pool.wait_ge(s_msq, NT * h + n + 1)
                    pool.tensor_tensor(rstd[:, n:n + 1], ms[:, n:n + 1], nhalf, ALU.pow).then_inc(s_rst, 1)
                copied(pool, ("u", h, NP - 1))
                pool.dma_start(st_p[0, 0, h], St[:, NP % 3, :]).then_inc(s_ost, 16)
                copied(pool, *[("us", h, c) for c in range(4)])
                pool.dma_start(st_s[0].rearrange("b h c v -> h c b v")[h], S0).then_inc(s_ost, 16)
                copied(pool, *[("ot", h, n) for n in range(NT)])
                pool.dma_start(ob_out[:, h], obT).then_inc(s_obs, 16)

            for j in range(KT):
                for g in range(3):
                    t = slice(g * THIRD, (g + 1) * THIRD)
                    copied(pool, ("ya", j, g), ("yb", j, g))
                    pool.tensor_tensor(gate_a[:, j, t], gate_a[:, j, t], gate_b[:, j, t], ALU.add).then_inc(s_mr, 1)

            norms = [0]

            def row_rstd():
                i = norms[0]
                q = i % 4
                norms[0] += 1
                pool.wait_ge(s_var, i + 1)
                pool.tensor_scalar(lve[:, q:q + 1], mv[:, q, 1:2], LN_EPS, None, ALU.add).then_inc(s_lve, 1)
                pool.wait_ge(s_lve, i + 1)
                pool.tensor_tensor(lrs[:, q:q + 1], lve[:, q:q + 1], nhalf, ALU.pow).then_inc(s_lrs, 1)

            for n in range(NT):
                row_rstd()

            past_pe(pool, ("wo", 1, NT - 1))
            pool.wait_ge(s_x1, NT)
            pool.memset(U[:, :, 0:2], 0.0).then_inc(s_cg, 2)

            def cached(j, d, v):
                pool.wait_ge(s_cg, 4 * j + 2 * d + v + 1)
                u = U[:, v, SEQ + 2:SEQ + 146].rearrange("p (b t) -> p b t", t=18)
                src = cacheT.rearrange("p c (b r) -> p c b r", r=2)[:, bass.ds(2 * j + d + v * NC_FF, 1), :, :]
                pool.tensor_copy(u[:, :, 0:2], src.rearrange("p a b r -> p (a b) r")).then_inc(s_up, 1)

            def gather(j, d, v):
                if v == 0 and d:
                    pool.wait_ge(cn_free, 2 * j + d)
                pool.wait_ge(s_conv, 4 * j + 2 * d + v + 1)
                u = U[:, v, :]
                pool.tensor_tensor(cn[:, v, 0:2], u[:, SEQ:SEQ + 2], one.to_broadcast([P, 2]), ALU.mult)
                pool.tensor_copy(cn[:, v, 2:18].rearrange("p (b r) -> p b r", r=2),
                                 u[:, SEQ + 2:SEQ + 146].rearrange("p (b t) -> p b t", t=18)[:, :, 16:18]).then_inc(s_cg, 1)

            def store_new(j, d):
                pool.wait_ge(cn_free, 2 * j + d + 1)
                src = cno.rearrange("r (v p) -> r v p", v=2)
                for r0, r1, dst in ((0, 2, cv_p[0, 0]), (2, 18, cv_s[0].rearrange("b r c -> (b r) c"))):
                    pool.dma_start(dst.rearrange("r (v c) -> r v c", v=2)[:, :, bass.ds((2 * j + d) * P, P)], src[r0:r1])\
                        .then_inc(s_ocn, 16)

            def columns(j, d):
                cached(j, d, 0)
                cached(j, d, 1)
                if d:
                    store_new(j, d - 1)
                gather(j, d, 0)
                gather(j, d, 1)

            in_pairs(pool, columns)
            store_new(0, NC_FF - 1)

            row_rstd()
            row_rstd()
            for n in range(NT):
                if n + 2 < NT:
                    row_rstd()
                row_rstd()
                pool.wait_ge(s_y, n + 1)
                dst = y_p[0, n * P:(n + 1) * P, :] if n < NP else y_s.rearrange("b t d -> (b t) d")
                pool.dma_start(dst, z3[:, n % 3, :]).then_inc(s_oy[n % 3], 16)
            for i in range(3):
                pool.wait_ge(s_oy[i], 16 * 3)
            pool.wait_ge(s_ocn, 32 * NC_FF)
            for i in range(2):
                pool.wait_ge(s_ok[i], 16 * (5 - i))
            pool.wait_ge(s_ost, 32 * H_B)
            pool.wait_ge(s_ov, 32)
            pool.wait_ge(s_ol, 32)

        @block.sync
        def _(sp):
            def load(n):
                name, src, kt = chunks[n]
                if n >= W_SLOTS:
                    past_pe(sp, w_last[chunks[n - W_SLOTS][0]])
                s = n % W_SLOTS
                slot = ring[:, s, 0:kt, :] if n < w_index[("uv", 0)] else rawu[:, s // 2, s % 2]
                sp.dma_start(slot, src).then_inc(w_in_sem[s], 16)

            def tokens(p_, s_, n):
                return p_[n * P:(n + 1) * P, :] if n < NP else s_.rearrange("b t d -> (b t) d")

            def bcast(v, dst, s):
                sp.dma_start(dst, v.partition_broadcast(P)).then_inc(s, 16)

            sp.dma_start(keep, consts[:, 0:C_KEEP]).then_inc(s_const, 16)
            for n in range(3):
                sp.dma_start(xs[:, n, :], tokens(x_prompt[0], x_sample, n)).then_inc(s_x[n % 3], 16)
            with nc.allow_non_contiguous_dma(reason="small columns"):
                sp.dma_start(bfg, b_fgate.rearrange("o h -> h o")).then_inc(s_small, 16)
                sp.dma_start(wf, w_in[0].rearrange("(k p) n -> p k n", p=P)[:, :, O_F:O_F + H_A]).then_inc(s_small, 16)
                sp.dma_start(cvst, cache_ffn_conv[0].rearrange("b r c -> (b r) c")).then_inc(s_cv, 16)
                sp.dma_start(cwst[:, 0:3, :], conv_w[0].rearrange("j (c p) -> c j p", p=P)).then_inc(s_cv, 16)
                sp.dma_start(cwst[:, 3, :], conv_b[0].rearrange("(c p) -> c p", p=P)).then_inc(s_cv, 16)
                sp.dma_start(lfp.rearrange("p (b n) h -> p b n h", n=2), cache_fox_logf[0].rearrange("b (n p) h -> p b n h", p=P)).then_inc(s_lf, 16)
            for n in range(3, NT):
                past_pe(sp, ("xT", n - 3))
                sp.dma_start(xs[:, n % 3, :], tokens(x_prompt[0], x_sample, n)).then_inc(s_x[n % 3], 16)
            for n in range(4):
                load(n)
            sp.dma_start(hc, consts[:, C_HSEL:C_SCAN]).then_inc(s_const2, 16)
            with nc.allow_non_contiguous_dma(reason="small columns"):
                sp.dma_start(ba2, b_a2[0].rearrange("(c p) -> p c", p=P)).then_inc(s_cols, 16)
                sp.dma_start(ggla, g_gla[0].rearrange("(c p) -> p c", p=P)).then_inc(s_cols, 16)
            for n in range(4, 16):
                load(n)
            NU = len(UNITS)
            sp.wait_ge(s_rl, 12)
            past_pe(sp, ("va", 1, NT - 1))
            copied(sp, ("va", 1, NT - 1))
            for b in range(DEC_B):
                if b == 4:
                    copied(sp, ("pv", NU - 1), ("pv", NU - 2), ("oT", 3))
                    sp.wait_ge(s_ov, 32)
                    for n in range(3):
                        sp.dma_start(xs[:, n, :], tokens(x_prompt[0], x_sample, n)).then_inc(s_x[n], 16)
                if b >= 4:
                    past_pe(sp, ("spv", b - 4))
                for dst, src in ((kp, cache_fox_k), (vp, cache_fox_v)):
                    sp.dma_start(dst[:, b % 4, :].rearrange("p (n c) -> p n c", n=2),
                                 src[0, b].rearrange("(n p) h d -> p n (h d)", p=P)).then_inc(s_kv[b % 4], 16)
            copied(sp, ("soT", DEC_B - 1), ("soT", DEC_B - 2), ("spv", DEC_B - 1))
            sp.dma_start(wa2, w_a2[0]).then_inc(s_b, 16)
            with nc.allow_non_contiguous_dma(reason="16 columns"):
                sp.dma_start(wa1, w_in[0].rearrange("(k p) n -> p k n", p=P)[:, :, O_A1:O_A1 + RANK]).then_inc(s_b, 16)
            sp.dma_start(scanm, consts[:, C_SCAN:C_ALL]).then_inc(s_b, 16)
            for n in range(3, NT):
                past_pe(sp, ("xT2", n - 3))
                sp.dma_start(xs[:, n % 3, :], tokens(x_prompt[0], x_sample, n)).then_inc(s_x[n % 3], 16)
            for n in range(16, FIRST_UP):
                load(n)
                if n == w_index[("gb", KT - 1)]:
                    sp.wait_ge(s_obs, 16 * H_B)
                    sp.dma_start(oar, oa_out).then_inc(s_oai, 16)
                if n == w_index[("ya", 3)]:
                    past_pe(sp, ("gb", KT - 1, 2))
                    for h in range(H_B):
                        sp.dma_start(obr[:, 2 * h:2 * h + 2, :], ob_out[:, h]).then_inc(s_obi, 16)
            wo_cols = w_o[0].rearrange("(k p) n -> p k n", p=P)
            past_pe(sp, ("ya", KT - 1, 2))
            sp.dma_start(wor[0], wo_cols[:, :, 0:512]).then_inc(s_wo[0], 16)
            past_pe(sp, ("yb", KT - 1, 2))
            for n in range(NT):
                sp.dma_start(x1[:, n, :], tokens(x_prompt[0], x_sample, n)).then_inc(s_xin[n], 16)
            sp.dma_start(wor[1], wo_cols[:, :, 512:1024]).then_inc(s_wo[1], 16)
            bcast(ln1_g[0], g1, s_g1)
            bcast(ln1_b[0], b1, s_g1)
            for n in range(FIRST_UP, FIRST_UP + W_SLOTS):
                load(n)
            def load_up(j, d):
                for v in range(2):
                    b, n = up_use(j, d - 2, v, 2)
                    sp.wait_ge(up_full[b], n + 1)
                    sp.dma_start(rawu[:, d % 2, v], w_up[0].rearrange("(k p) n -> p k n", p=P)
                                 [:, :, bass.ds((2 * j + d) * P + v * D_FF, P)]).then_inc(w_in_sem[2 * (d % 2) + v], 16)

            def load_down(j, d, wait=True):
                if wait:
                    b, n = dn_use(j, d - 2, 2 * NT - 1)
                    sp.wait_ge(dn_full[b], n + 1)
                sp.dma_start(rawd[:, d % 2, :], w_down[0, bass.ds((2 * j + d) * P, P), :]).then_inc(s_wdi[d % 2], 16)

            past_pe(sp, ("wo", 1, NT - 1))
            load_down(0, 0, wait=False)
            load_down(0, 1, wait=False)
            load_up(0, 2)
            with sp.Fori(0, NC_FF // 2 - 2) as j:
                for d in (1, 2):
                    load_up(j, d + 2)
                    load_down(j, d + 1)
            load_up(0, NC_FF - 1)
            load_down(0, NC_FF - 2)
            load_down(0, NC_FF - 1)
            for b in range(4):
                sp.wait_ge(up_full[b], 6 * NC_FF // 4)
            for n in range(2):
                sp.dma_start(pin[:, n, :], tokens(p_prompt[0, 0], p_sample[0], n)).then_inc(s_pin[n], 16)
            for v, dst in ((ln2_g, g2), (ln2_b, b2), (ln3_g, g3), (ln3_b, b3)):
                bcast(v[0], dst, s_g2)
            sp.dma_start(rplg, w_plg[0].rearrange("(k p) n -> p k n", p=P)).then_inc(s_ple, 16)
            for b in range(3):
                sp.wait_ge(dn_full[b], 6 * NC_FF)
            sp.dma_start(rpl, w_pl[0].rearrange("(k p) n -> p k n", p=P)).then_inc(s_ple, 16)
            for n in range(2, NT):
                past_pe(sp, ("pT", n - 2))
                sp.dma_start(pin[:, n % 2, :], tokens(p_prompt[0, 0], p_sample[0], n)).then_inc(s_pin[n % 2], 16)


_INS = ["x_prompt", "x_sample", "cache_fox_k", "cache_fox_v", "cache_fox_logf", "state_gla", "cache_ffn_conv",
        "p_prompt", "p_sample", "w_in", "b_fgate", "w_a2", "b_a2", "g_gla", "w_a_out", "w_b_out", "w_o", "ln1_g",
        "ln1_b", "w_up", "conv_w", "conv_b", "w_down", "ln2_g", "ln2_b", "w_pl", "w_plg", "ln3_g", "ln3_b"]
_OUTS = [(1, SEQ, D), (DEC_B, DEC_T, D),
         (1, 1, SEQ, H_A, DH), (1, 1, SEQ, H_A, DH), (1, 1, SEQ, H_A), (1, 1, H_B, DK, DV), (1, 1, 2, 2 * D_FF),
         (1, DEC_B, DEC_T, H_A, DH), (1, DEC_B, DEC_T, H_A, DH), (1, DEC_B, DEC_T, H_A), (1, DEC_B, H_B, DK, DV),
         (1, DEC_B, 2, 2 * D_FF)]


def kernel(**inputs):
    import concourse.bacc as bacc
    from concourse.bass_utils import run_bass_kernel_spmd

    nc = bacc.Bacc("TRN2", target_bir_lowering=False, num_devices=1)
    arrays, args = {}, []
    for name in _INS:
        a = np.ascontiguousarray(inputs[name])
        arrays[f"in_{name}"] = a
        args.append(nc.dram_tensor(f"in_{name}", a.shape, F32, kind="ExternalInput").ap())
    arrays["in_consts"] = shape_constants()
    args.append(nc.dram_tensor("in_consts", arrays["in_consts"].shape, F32, kind="ExternalInput").ap())
    for i, shape in enumerate(_OUTS):
        args.append(nc.dram_tensor(f"out_{i}", shape, F32, kind="ExternalOutput").ap())
    build(nc, *args)
    r = run_bass_kernel_spmd(nc, [arrays], core_ids=[0])
    return tuple(r.results[0][f"out_{i}"] for i in range(len(_OUTS)))
```

```python
from contextlib import ExitStack

import numpy as np

import concourse.bass as bass
from concourse import mybir

F32 = mybir.dt.float32
F32R = mybir.dt.float32r
U32 = mybir.dt.uint32
ALU = mybir.AluOpType
ACT = mybir.ActivationFunctionType
AX = mybir.AxisListType

P = 128
D = 1024
KT = D // P
SEQ, DEC_B, DEC_T = 1024, 8, 16
PAST = 256
T = SEQ + DEC_B * DEC_T
NP = SEQ // P
NT = T // P
THIRD = T // 3
H_A, DH = 8, 64
H_B, DK, DV = 4, 128, 256
RANK, TAU = 16, 16
D_FF, PLE = 2816, 256
NC_FF = D_FF // P
LN_EPS = 1e-5
ALPHA = 2.0 ** 0.25
NEG = -1e30
O_Q, O_K, O_V, O_F = 0, 512, 1024, 1536
O_QB, O_KB, O_VB, O_RB = 1544, 2056, 2568, 3592
O_A1, O_GA, O_GB = 4616, 4632, 5656
HALVES = [64, 32, 16, 8, 4, 2, 1]
W_SLOTS = 4

C_ID = 0
C_LEV = C_ID + P
C_CAUSAL = C_LEV + 7 * P
C_NEG1 = C_CAUSAL + P
C_NHALF = C_NEG1 + 1
C_BM = C_NHALF + 1
C_ONE = C_BM + DEC_B
C_KEEP = C_ONE + 1
C_HSEL = C_KEEP + 5
C_OMASK = C_HSEL + H_A * P
C_WIN = C_OMASK + H_A * DH
C_HS16 = C_WIN + 240
C_TSEL = C_HS16 + P
C_SCAN = C_TSEL + DEC_T
C_ALL = C_SCAN + T


def shape_constants():
    c = np.zeros((P, C_ALL), np.float32)
    i = np.arange(P)
    c[:, C_ID:C_ID + P] = np.eye(P)
    for n, h in enumerate(HALVES):
        s, t = i[:, None], i[None, :]
        c[:, C_LEV + n * P:C_LEV + (n + 1) * P] = (s // (2 * h) == t // (2 * h)) & (s % (2 * h) < h) & (t % (2 * h) >= h)
    c[:, C_CAUSAL:C_CAUSAL + P] = np.where(i[None, :] > i[:, None], NEG, 0.0)
    c[:, C_NEG1] = -1.0
    c[:, C_NHALF] = -0.5
    c[:, C_BM:C_BM + DEC_B] = i[:, None] // DEC_T == np.arange(DEC_B)[None, :]
    c[:, C_ONE] = 1.0
    for h in range(H_A):
        c[h, C_HSEL + h * P:C_HSEL + (h + 1) * P] = 1.0
        c[h, C_HS16 + h * DEC_T:C_HS16 + (h + 1) * DEC_T] = 1.0
        c[h * DEC_T:(h + 1) * DEC_T, C_OMASK + h * DH:C_OMASK + (h + 1) * DH] = 1.0
    x = np.arange(240)[None, :] - 112
    c[:, C_WIN:C_WIN + 240] = np.where((x >= 0) & (x <= i[:, None] % DEC_T), 0.0, NEG)
    c[:, C_TSEL:C_TSEL + DEC_T] = i[:, None] % DEC_T == np.arange(DEC_T)[None, :]
    t = np.arange(T)
    c[:, C_SCAN:] = np.where(np.where(t < SEQ, t % P, t % DEC_T) == 0, 0.0, 1.0)
    return c


def build(nc, x_prompt, x_sample, cache_fox_k, cache_fox_v, cache_fox_logf, state_gla, cache_ffn_conv,
          p_prompt, p_sample, w_in, b_fgate, w_a2, b_a2, g_gla, w_a_out, w_b_out, w_o, ln1_g, ln1_b,
          w_up, conv_w, conv_b, w_down, ln2_g, ln2_b, w_pl, w_plg, ln3_g, ln3_b, consts,
          y_p, y_s, fk_p, fv_p, fl_p, st_p, cv_p, fk_s, fv_s, fl_s, st_s, cv_s):
    ctx = ExitStack()
    with ctx:
        def sem(name):
            return ctx.enter_context(nc.semaphore(name))

        M_ALL = 53200
        W_FA = 48
        SB_BASE = (nc.sbuf_base + 31) // 32 * 32
        sb = ctx.enter_context(nc.sbuf_tensor("sb", [P, M_ALL], F32))
        ps = ctx.enter_context(nc.psum_tensor("ps", [P, 4, 1024], F32))

        def at(off, *dims, parts=P):
            n = int(np.prod(dims))
            assert off + n <= M_ALL, (off, n)
            v = sb[0:parts, off:off + n]
            if len(dims) == 2:
                v = v.rearrange("p (a b) -> p a b", a=dims[0])
            if len(dims) == 3:
                v = v.rearrange("p (a b c) -> p a b c", a=dims[0], b=dims[1])
            return v

        off = {}

        def place(base, *items):
            for name, n in items:
                off[name] = base
                base += n
            return base

        e = place(0, ("keep", C_KEEP + 5), ("cw", 176), ("cacheT", 704), ("cols", 40), ("stat", 152))
        e = place(e, ("ring", W_SLOTS * 1024), ("ringh", W_SLOTS * 1024))
        e = place(e, ("R1", 9216), ("R2", 9216), ("R3", 9216), ("R4", 9216))
        off["R5"] = e
        place(off["R1"], ("xh", 9216), ("xl", 9216))
        place(off["R3"], ("oaT", 4608), ("qT", 4608), ("kT", 4608), ("va", 4608))
        place(off["oaT"], ("fz", 1152), ("fa", 1152), ("kst", 2048), ("lfp", 128))
        place(off["qT"], ("cvst", 5632), ("cwst", 512))
        off["xs"] = off["cwst"] + 512
        off["wf"] = off["va"] + 4096
        e = place(off["R5"], ("hsel", C_SCAN - C_HSEL), ("negC", 1152), ("negCs", 2048 + 128), ("lfo", 72), ("wfh", KT * W_FA))
        assert e <= M_ALL, e
        place(off["R1"], ("cb", 2048), ("dg", 2048), ("S", 2048), ("PT", 2048), ("S2", 1024))
        place(off["R1"], ("qbd", 1312), ("kpT", 2048), ("sN", 256), ("sP", 768), ("sPT", 768), ("om", 1024))
        place(off["R2"], ("kp", 4096), ("vp", 4096))
        off["qO"] = off["vp"]
        e = place(off["R3"], ("qb", 1152), ("kb", 1152), ("zb", 1152), ("b", 1152), ("X", 2 * 1152),
                  ("ks", 1152), ("AT", 1152), ("vb", 2304), ("St", 768), ("S0", 2048), ("ktok", 1024),
                  ("ksm", 1024), ("qsm", 1152), ("on", 768), ("scan", 1152), ("a1T", 1152), ("wa2", 512),
                  ("sq", 256), ("obT", 2304))
        off["qs"] = off["zb"]
        assert e <= M_ALL, e
        off["gate_a"], off["gate_b"] = off["R3"], off["R4"]
        off["oal"], off["oah"] = off["R5"], off["R1"]
        off["obl"] = off["R2"]
        off["obh0"], off["obh1"] = off["R1"] + 4608, off["R1"]
        off["mh"], off["ml"] = off["gate_b"], off["gate_a"]
        off["x1"] = off["R1"]
        place(off["R5"], ("wol0", 4096), ("g1", 1024))
        off["woh0"] = off["ringh"]
        place(off["R2"], ("wol1", 4096), ("woh1", 4096), ("b1", 1024))
        off["x1h"], off["x1l"] = off["mh"], off["ml"]
        place(off["R2"], ("hh", 2304), ("hl", 2304), ("wdr", 2048), ("wdh", 2048))
        e = place(off["R5"], ("U", 2344), ("y", 2344), ("cn", 72), ("cno", 256))
        assert e <= M_ALL, e
        off["plgr"], off["plgh"] = off["x1h"], off["x1l"]
        off["plr"], off["plh"] = off["hh"], off["hh"] + 2048
        place(off["wdr"], ("x2h", 2048), ("x2l", 2048))
        place(off["ring"], ("pin", 512), ("pTh", 512), ("pTl", 512), ("g2", 1024), ("b2", 1024), ("g3", 1024),
              ("b3", 1024))
        place(off["R5"], ("z3", 3072), ("sge", 2048))

        def named(name, base, *dims, kind=F32):
            t = nc.alloc_sbuf_tensor_at(name, [P, int(np.prod(dims))], kind, offset=SB_BASE + 4 * base)
            v = t[:, :]
            if len(dims) == 2:
                v = v.rearrange("p (a b) -> p a b", a=dims[0])
            if len(dims) == 3:
                v = v.rearrange("p (a b c) -> p a b c", a=dims[0], b=dims[1])
            return v

        def rounded(name, base, *dims):
            return named(name, base, *dims, kind=F32R)

        keep = at(off["keep"], C_KEEP)
        ident = keep[:, C_ID:C_ID + P]
        levm = keep[:, C_LEV:C_LEV + 7 * P].bitcast(U32)
        causal = keep[:, C_CAUSAL:C_CAUSAL + P]
        neg1, nhalf, one = keep[:, C_NEG1:C_NEG1 + 1], keep[:, C_NHALF:C_NHALF + 1], keep[:, C_ONE:C_ONE + 1]
        bmask = keep[:, C_BM:C_BM + DEC_B]
        hc = at(off["hsel"], C_SCAN - C_HSEL)
        hsel = hc[:, 0:H_A * P]
        omask = hc[:, C_OMASK - C_HSEL:C_OMASK - C_HSEL + 512]
        win = hc[:, C_WIN - C_HSEL:C_WIN - C_HSEL + 240]
        hs16 = hc[:, C_HS16 - C_HSEL:C_HS16 - C_HSEL + P]
        tsel = hc[:, C_TSEL - C_HSEL:C_TSEL - C_HSEL + DEC_T]
        scanm = at(off["scan"], T)

        xh, xl = rounded("x_hi", off["xh"], KT, T), rounded("x_lo", off["xl"], KT, T)
        ring, ringh, ringl = (v.rearrange("p s (k c) -> p s k c", k=KT) for v in (
            named("ring_raw", off["ring"], W_SLOTS, KT * P), rounded("ring_hi", off["ringh"], W_SLOTS, KT * P),
            rounded("ring_lo", off["ring"], W_SLOTS, KT * P)))
        oaT = at(off["oaT"], 4, T)
        cols = at(off["cols"], 40)
        bfg, ba2, ggla = cols[0:H_A, 0:1], cols[:, 4:8], cols[:, 8:16]
        dl = cols[:, 16:32]
        stat = at(off["stat"], 152)
        rs, mx, nm, ri = stat[:, 0:4], stat[:, 4:8], stat[:, 8:12], stat[:, 12:16]
        ss, ms, rstd = stat[:, 16:32], stat[:, 32:48], stat[:, 48:64]
        mxb, rsb = stat[:, 64:68], stat[:, 68:72]
        bnst = stat[:, 80:80 + 48].rearrange("p (a b) -> p a b", a=4)
        mv = stat[:, 130:138].rearrange("p (a b) -> p a b", a=4)
        lve, lrs = stat[:, 140:144], stat[:, 144:148]

        X_BUFS = 7
        PLG_POOL = 7
        xs = at(off["xs"], X_BUFS, 1024)
        xs2 = [at(off["va"] + 1024 * i, 1024) for i in range(4)] + [at(off["kT"] + T * i, 1024) for i in range(4)] \
            + [at(off["qT"], 1024)]
        qT, kT, va = at(off["qT"], 4, T), at(off["kT"], 4, T), at(off["va"], NT, 512)
        cwT = at(off["cw"], 4, 44)
        cacheT = at(off["cacheT"], 44, 16)
        cvst = at(off["cvst"], 5632, parts=16)
        cwst = at(off["cwst"], 4, P, parts=44)
        lfp = at(off["lfp"], 16, H_A)
        wf, wfh, wfl = (k(n, off[o], KT, W_FA) for k, n, o in ((named, "wf_raw", "wf"), (rounded, "wf_hi", "wfh"), (rounded, "wf_lo", "wf")))
        fz, fa = at(off["fz"], T, parts=H_A), at(off["fa"], T, parts=H_A)
        negC = at(off["negC"], T)
        negCs = at(off["negCs"], 2176)
        lfo = at(off["lfo"], NT, H_A)
        kst = at(off["kst"], 4, 512)
        cb, dg = at(off["cb"], 2, 1024), at(off["dg"], 2, 1024)
        S, PT = [at(o, 1024) for o in (off["S"], off["S"] + 1024, off["S2"])], at(off["PT"], 2, 1024)
        qO = at(off["qO"], 4, SEQ)
        qbd = at(off["qbd"], 2, 656)
        kp, vp = at(off["kp"], 4, 1024), at(off["vp"], 4, 1024)
        kpT = at(off["kpT"], 2, 1024)
        sN, sP, sPT, om = at(off["sN"], 2, 128), at(off["sP"], 2, 384), at(off["sPT"], 2, 384), at(off["om"], 2, 512)

        qb, kb, zb, b16, qs = (at(off[n], T) for n in ("qb", "kb", "zb", "b", "qs"))
        X = at(off["X"], 2, T)
        ks = at(off["ks"], T)
        AT = at(off["AT"], T)
        vb, St = at(off["vb"], NT, DV), at(off["St"], 3, DV)
        S0 = at(off["S0"], DEC_B, DV)
        ktok, ksm = at(off["ktok"], NP, P), at(off["ksm"], DEC_B, P)
        qsm = at(off["qsm"], 1152)
        on = at(off["on"], 3, DV)
        a1T = at(off["a1T"], T)[32:32 + RANK]
        a1s = at(off["negCs"], T)[32:32 + RANK]
        wa2 = at(off["wa2"], 512)[32:32 + RANK]
        sq = at(off["sq"], 256)
        obT = at(off["obT"], 2, T)
        oar, oah, oal = named("oa_raw", off["oal"], 4, T), rounded("oa_hi", off["oah"], 4, T), rounded("oa_lo", off["oal"], 4, T)
        obr, obl = named("ob_raw", off["obl"], KT, T), rounded("ob_lo", off["obl"], KT, T)
        obh = [rounded("ob_hi0", off["obh0"], 4, T), rounded("ob_hi1", off["obh1"], 4, T)]
        gate_a, gate_b = named("gate_a", off["gate_a"], KT, T), named("gate_b", off["gate_b"], KT, T)
        mh, ml = rounded("merged_hi", off["mh"], KT, T), rounded("merged_lo", off["ml"], KT, T)
        wor = [named(f"wo_raw{c}", off[f"wol{c}"], KT, 512) for c in range(2)]
        woh = [rounded(f"wo_hi{c}", off[f"woh{c}"], KT, 512) for c in range(2)]
        wol = [rounded(f"wo_lo{c}", off[f"wol{c}"], KT, 512) for c in range(2)]
        x1 = at(off["x1"], NT, D)
        x1h, x1l = rounded("x1_hi", off["x1h"], KT, T), rounded("x1_lo", off["x1l"], KT, T)
        g1, b1 = at(off["g1"], D), at(off["b1"], D)
        oa_out = nc.dram_tensor("branch_a", (P, 4, T), F32).ap()
        ob_out = nc.dram_tensor("branch_b", (P, H_B, 2, T), F32).ap()
        rawu = named("up_raw", off["ring"], 2, 2, KT * P).rearrange("p e v (k c) -> p e v k c", k=KT)
        wuh = rounded("up_hi", off["ringh"], 2, 2, KT * P).rearrange("p e v (k c) -> p e v k c", k=KT)
        wul = rounded("up_lo", off["ring"], 2, 2, KT * P).rearrange("p e v (k c) -> p e v k c", k=KT)
        rawd = named("down_raw", off["wdr"], 2, D)
        wdh, wdl = rounded("down_hi", off["wdh"], 2, D), rounded("down_lo", off["wdr"], 2, D)
        hh, hl = rounded("h_hi", off["hh"], 2, T), rounded("h_lo", off["hl"], 2, T)
        U, y = at(off["U"], 2, 1170), named("convolved_halves", off["y"], 2, 1170)
        cn, cno = at(off["cn"], 2, 18), at(off["cno"], 256, parts=18)
        rplg, rpl = named("plg_raw", off["plgr"], KT, D), named("pl_raw", off["plr"], 2, D)
        plgh, plgl = rounded("plg_hi", off["plgh"], KT, D), rounded("plg_lo", off["plgr"], KT, D)
        plh, pll = rounded("pl_hi", off["plh"], 2, D), rounded("pl_lo", off["plr"], 2, D)
        g2, b2, g3, b3 = (at(off[n], D) for n in ("g2", "b2", "g3", "b3"))
        pin = at(off["pin"], 2, PLE)
        pTh, pTl = rounded("p_hi", off["pTh"], 2, 2, P), rounded("p_lo", off["pTl"], 2, 2, P)
        x2h, x2l = rounded("x2_hi", off["x2h"], 2, KT, P), rounded("x2_lo", off["x2l"], 2, KT, P)
        sge, z3 = at(off["sge"], 2, D), at(off["z3"], 3, D)

        full = [sem(f"psum_full{s}") for s in range(4)]
        free = [sem(f"psum_free{s}") for s in range(4)]
        turn = {}

        def take(pe, key):
            n = len(turn)
            turn[key] = n
            if n >= 4:
                pe.wait_ge(free[n % 4], n // 4)
            return ps[:, n % 4, :]

        def filled(key):
            return full[turn[key] % 4]

        def drained(key):
            return free[turn[key] % 4]

        def count(key):
            return turn[key] // 4 + 1

        def product(eng, key):
            eng.wait_ge(filled(key), count(key))
            return ps[:, turn[key] % 4, :]

        def copied(eng, *keys):
            last = {}
            for k in keys:
                last[turn[k] % 4] = max(last.get(turn[k] % 4, 0), count(k))
            for s, v in last.items():
                eng.wait_ge(free[s], v)

        def past_pe(eng, *keys):
            last = {}
            for k in keys:
                last[turn[k] % 4] = max(last.get(turn[k] % 4, 0), count(k))
            for s, v in last.items():
                eng.wait_ge(full[s], v)

        bank = ps.rearrange("p s (a c) -> p (s a) c", a=2)
        up_full = [sem(f"up_full{s}") for s in range(4)]
        up_free = [sem(f"up_free{s}") for s in range(4)]
        dn_full = [sem(f"down_full{s}") for s in range(3)]
        dn_free = [sem(f"down_free{s}") for s in range(3)]
        cn_full, cn_free = sem("new_columns_full"), sem("new_columns_free")

        def up_use(j, d, v, g):
            n = 6 * d + 3 * v + g
            return n % 4, 3 * j + n // 4

        DOWN_AFTER = [range(0), range(0), range(0, 5), range(5, 11), range(11, 18), range(0)]

        def in_pairs(eng, step):
            step(0, 0)
            step(0, 1)
            with eng.Fori(0, NC_FF // 2 - 2) as j:
                step(j, 2)
                step(j, 3)
            step(0, NC_FF - 2)
            step(0, NC_FF - 1)

        def dn_use(j, d, w):
            n = 18 * d + w
            return n % 3, 12 * j + n // 3

        chunks = []

        def w_cols(w, c0, kt=KT):
            return w[0].rearrange("(k p) n -> p k n", p=P)[:, :, c0:c0 + P], kt

        for j in range(4):
            chunks.append((("qa", j), *w_cols(w_in, O_Q + j * P)))
        for j in range(4):
            chunks.append((("ka", j), *w_cols(w_in, O_K + j * P)))
        for j in range(4):
            chunks.append((("va", j), *w_cols(w_in, O_V + j * P)))
        for h in range(H_B):
            chunks.append((("qb", h), *w_cols(w_in, O_QB + h * P)))
            chunks.append((("kb", h), *w_cols(w_in, O_KB + h * P)))
            for c in range(2):
                chunks.append((("rb", h, c), *w_cols(w_in, O_RB + h * DV + c * P)))
            for c in range(2):
                chunks.append((("vb", h, c), *w_cols(w_in, O_VB + h * DV + c * P)))
        for j in range(KT):
            chunks.append((("ga", j), *w_cols(w_in, O_GA + j * P)))
            chunks.append((("gb", j), *w_cols(w_in, O_GB + j * P)))
        for j in range(KT):
            chunks.append((("ya", j), *w_cols(w_a_out, j * P, 4)))
        for j in range(KT):
            chunks.append((("yb", j), *w_cols(w_b_out, j * P)))
        for c in range(2):
            chunks.append((("uv", c), *w_cols(w_up, c * P)))
            chunks.append((("ug", c), *w_cols(w_up, D_FF + c * P)))
        UP_ROUND = sum(1 for c in chunks if c[0][0] not in ("uv", "ug")) // W_SLOTS
        w_index = {c[0]: n for n, c in enumerate(chunks)}
        w_last = {}
        w_in_sem = [sem(f"weights_in{s}") for s in range(W_SLOTS)]

        s_rh = sem("weights_hi_ready")
        s_rl = sem("weights_lo_ready")

        def weights(pe, name):
            n = w_index[name]
            pe.wait_ge(s_rl, n + 1)
            return ringh[:, n % W_SLOTS], ringl[:, n % W_SLOTS]

        FIRST_UP = UP_ROUND * W_SLOTS

        s_const = sem("const_in")
        s_const2 = sem("const2_in")
        s_small = sem("small_in")
        s_ident = sem("identity_in")
        s_xt = [sem(f"x_in{n}") for n in range(NT)]
        s_cv = sem("conv_cache_in")
        s_lf = sem("logf_past_in")
        s_kp, s_vp = ([sem(f"{n}_past_in{i}") for i in range(4)] for n in "kv")
        s_b = sem("gla_small_in")
        s_s0 = sem("state_in")
        s_wo = [sem(f"wo_in{c}") for c in range(2)]
        s_g1 = sem("ln1_in")

        s_plg = [sem(f"embedding_gate_in{k}") for k in range(KT)]
        s_ple = sem("embedding_weights_in")
        s_pin = [sem(f"p_in{i}") for i in range(2)]
        s_xh1 = sem("x_hi_ready")
        s_sm = sem("small_hi_ready")
        s_sl = sem("small_lo_ready")
        s_oas = sem("branch_a_stored")
        s_obs = sem("branch_b_stored")
        s_oai = sem("branch_a_in")
        s_obi = sem("branch_b_in")
        s_oh = sem("branch_hi_ready")
        s_ol2 = sem("branch_lo_ready")
        s_mr = sem("merged_sum_ready")
        s_mh = sem("merged_hi_ready")
        s_woh = sem("wo_hi_ready")
        s_wol = sem("wo_lo_ready")
        s_ok = [sem(f"k_stored{i}") for i in range(4)]
        s_ov = sem("v_stored")
        s_ol = sem("logf_stored")
        s_cols = sem("gla_columns_in")
        s_ost = sem("state_stored")
        s_ocn = sem("conv_stored")
        s_oy = [sem(f"y_stored{i}") for i in range(3)]

        s_dve = sem("dve_step")
        s_act = sem("act_step")
        s_pool = sem("pool_step")
        s_fz = sem("fgate_exp")
        s_lf8 = sem("logf_ready")
        s_negc = sem("negC_ready")
        s_nc0 = sem("negC_cleared")
        s_a1 = sem("decay_rank_ready")
        s_qz = sem("q_cleared")
        s_qo = sem("q_odd_ready")
        s_nrm = sem("probs_normed")
        s_dg = sem("diag_bias_ready")
        s_max = sem("row_max_ready")
        s_exp = sem("probs_ready")
        s_exs = sem("sample_probs_ready")
        s_qbd = sem("qbd_ready")
        s_smx = sem("sample_max_ready")
        s_lnz = sem("gate_log_ready")
        s_bsc = sem("cumsum_ready")
        s_kd = sem("k_decay_log_ready")
        s_ee = sem("decays_ready")
        s_qs = sem("qs_ready")
        s_ksr = sem("ks_ready")
        s_at0 = sem("AT_cleared")
        s_qsm = sem("qsm_ready")
        s_xl = sem("level_log_ready")
        s_xe = sem("level_exp_ready")
        s_xm = sem("level_ready")
        s_ssq = sem("square_sum_ready")
        s_rst = sem("rstd_ready")
        s_mt = sem("merged_lo_ready")
        s_var = sem("ln_var_ready")
        s_lve = sem("ln_var_eps_ready")
        s_msq = sem("mean_square_ready")
        s_lrs = sem("ln_rstd_ready")
        s_x1 = sem("x1_ready")
        s_up = sem("cache_columns_ready")
        s_conv = sem("convolved")
        s_cv1 = sem("convolved_tap0")
        s_cv2 = sem("convolved_tap1")
        s_g2 = sem("ln23_in")
        s_gel = sem("gelu_ready")
        s_cg = sem("U_read")
        s_hm = sem("h_ready")
        s_hh = sem("h_hi_ready")
        s_hl = sem("h_lo_ready")
        s_wh = sem("up_hi_ready")
        s_wl = sem("up_lo_ready")
        s_dh = sem("down_hi_ready")
        s_dl = sem("down_lo_ready")
        s_wdi = [sem(f"down_in{i}") for i in range(2)]
        s_xh = sem("x1_hi_ready")
        s_xa = sem("x1_scaled")
        s_ph = sem("plg_hi_ready")
        s_pl = sem("plg_lo_ready")
        s_x2h = sem("x2_hi_ready")
        s_x2 = sem("x2_ready")
        s_y = sem("y_ready")

        block = ctx.enter_context(nc.Block())

        def split3(hi_w, lo_w, hi_x, lo_x):
            return [(hi_w, hi_x), (hi_w, lo_x), (lo_w, hi_x)]

        UNITS = [(h, i) for h in range(H_A) for i in reversed(range(NP))]

        @block.tensor
        def _(pe):
            mm, tr = pe.matmul, pe.transpose

            def chain(out, pairs):
                for n, (l, r) in enumerate(pairs):
                    m = mm(out, l, r, start=(n == 0), stop=(n == len(pairs) - 1))
                return m

            def split_chain(out, w, x, kt=KT):
                pairs = []
                for k in range(kt):
                    pairs += split3(w[0][:, k, :], w[1][:, k, :], x[0](k), x[1](k))
                return chain(out, pairs)

            def thirds(key, chunk, x, kt=KT, lhs=None, first=None):
                w = weights(pe, chunk) if lhs is None else lhs
                for g in range(3):
                    if first is not None and key[-1] == 0:
                        pe.wait_ge(s_ol2, first + 4 * g)
                    t = slice(g * THIRD, (g + 1) * THIRD)
                    o = take(pe, (*key, g))
                    split_chain(o[0:w[0].shape[-1], 0:THIRD], w, [lambda k, a=a: a(k)[:, t] for a in x], kt)\
                        .then_inc(filled((*key, g)), 1)
                if chunk is not None:
                    w_last[chunk] = (*key, 2)

            def pair_tile(o, chunk, n):
                s0 = w_index[chunk] % W_SLOTS
                t = slice(n * P, (n + 1) * P)
                pairs = []
                for k in range(KT):
                    pairs += split3(xh[:, k, t], xl[:, k, t], ringh[:, s0:s0 + 2, k, :], ringl[:, s0:s0 + 2, k, :])
                return chain(o[:, 0:2 * P], pairs)

            def turn_x(key, n, x):
                o = take(pe, (key, n))
                for k in range(KT):
                    m = tr(o[:, k * P:(k + 1) * P], x[:, k * P:(k + 1) * P], ident)
                m.then_inc(filled((key, n)), 1)

            x_parts = [lambda k, a=a: a[:, k, :] for a in (xh, xl)]

            pe.wait_ge(s_ident, 16)
            for n in range(NT):
                pe.wait_ge(s_xt[n], 16)
                turn_x("xT", n, xs[:, n % X_BUFS, :])
            pe.wait_ge(s_cv, 32 + 16)
            o = take(pe, "cacheT")
            for c in range(44):
                m = tr(o[:, c * 16:(c + 1) * 16], cvst[:, c * P:(c + 1) * P], ident[0:16, 0:16])
            m.then_inc(filled("cacheT"), 1)
            o = take(pe, "cwT")
            for c in range(4):
                m = tr(o[:, c * 44:(c + 1) * 44], cwst[:, c, :], ident[0:44, 0:44])
            m.then_inc(filled("cwT"), 1)
            pe.wait_ge(s_lf, 16)
            for n in range(2):
                o = take(pe, ("lfp", n))
                for c in range(8):
                    m = tr(o[0:H_A, c * P:(c + 1) * P], lfp[:, n * 8 + c, :], ident)
                m.then_inc(filled(("lfp", n)), 1)
            copied(pe, *[("xT", n) for n in range(NT)])
            pe.wait_ge(s_sl, 1)
            thirds(("f",), None, x_parts, lhs=(wfh, wfl))
            for j in range(4):
                thirds(("qa", j), ("qa", j), x_parts)
            for j in range(4):
                thirds(("ka", j), ("ka", j), x_parts)
            for q in range(2):
                weights(pe, ("va", 2 * q + 1))
                for n in range(NT):
                    o = take(pe, ("va", q, n))
                    pair_tile(o, ("va", 2 * q), n).then_inc(filled(("va", q, n)), 1)
                w_last[("va", 2 * q)] = w_last[("va", 2 * q + 1)] = ("va", q, NT - 1)
            pe.wait_ge(s_lf8, 1)
            o = take(pe, "lfT")
            for n in range(NT):
                m = tr(o[:, n * H_A:(n + 1) * H_A], fz[:, n * P:(n + 1) * P], ident[0:H_A, 0:H_A])
            m.then_inc(filled("lfT"), 1)
            copied(pe, *[("ka", j, g) for j in range(4) for g in range(3)])
            for n in range(NT):
                o = take(pe, ("kt", n))
                for j in range(4):
                    m = tr(o[:, j * P:(j + 1) * P], kT[:, j, n * P:(n + 1) * P], ident)
                m.then_inc(filled(("kt", n)), 1)

            def bias_rows(h):
                if h == 0:
                    pe.wait_ge(s_negc, 1)
                    pe.wait_ge(s_const2, 16)
                o = take(pe, ("cb", h))
                for c in range(2):
                    m = mm(o[:, c * 512:(c + 1) * 512], hsel[:, h * P:(h + 1) * P], negC[:, c * 512:(c + 1) * 512],
                           start=True, stop=True)
                m.then_inc(filled(("cb", h)), 1)

            def scores(u):
                h, i = UNITS[u]
                if h % 2 == 0 and i == NP - 1:
                    pe.wait_ge(s_qz, h + 2)
                    pe.wait_ge(s_qo, h // 2 + 1)
                q = (qT, qO)[h % 2]
                o = take(pe, ("s", u))
                n = (i + 1) * P
                for c in range(0, n, 512):
                    e = min(n, c + 512)
                    m = mm(o[:, c:e], q[:, h // 2, i * P:(i + 1) * P], kT[:, h // 2, c:e],
                           start=True, stop=True)
                m.then_inc(filled(("s", u)), 1)

            def turn_probs(u):
                h, i = UNITS[u]
                pe.wait_ge(s_nrm, u + 1)
                o = take(pe, ("pt", u))
                for c in range(i + 1):
                    m = tr(o[:, c * P:(c + 1) * P], S[u % 3][:, c * P:(c + 1) * P], ident)
                m.then_inc(filled(("pt", u)), 1)

            def probs_v(u):
                h, i = UNITS[u]
                copied(pe, ("pt", u))
                o = take(pe, ("pv", u))
                r = h % 2 * DH
                chain(o[r:r + DH, 0:P], [(va[:, c, h * DH:(h + 1) * DH], PT[:, u % 2, c * P:(c + 1) * P])
                                         for c in range(i + 1)]).then_inc(filled(("pv", u)), 1)

            copied(pe, ("qa", 3, 0), ("qa", 3, 1), ("qa", 3, 2), *[("va", q, n) for q in range(2) for n in range(NT)])
            bias_rows(0)
            NU = len(UNITS)
            for u in range(NU + 4):
                if u >= 4:
                    probs_v(u - 4)
                if u < NU:
                    if u % 8 == 6 and UNITS[u][0] + 1 < H_A:
                        bias_rows(UNITS[u][0] + 1)
                    scores(u)
                if 2 <= u <= NU + 1:
                    turn_probs(u - 2)

            def past_keys(b):
                pe.wait_ge(s_kp[b % 4], 16 * (b // 4 + 1))
                o = take(pe, ("kpT", b))
                for s in range(2):
                    for j in range(4):
                        m = tr(o[:, j * 256 + s * P:j * 256 + (s + 1) * P], kp[:, b % 4, s * 512 + j * P:s * 512 + (j + 1) * P], ident)
                m.then_inc(filled(("kpT", b)), 1)

            def sample_scores(b):
                pe.wait_ge(s_qbd, b + 1)
                copied(pe, ("kpT", b))
                o = take(pe, ("ss", b))
                chain(o[:, 0:256], [(qbd[:, b % 2, j * P:(j + 1) * P], kpT[:, b % 2, j * 256:(j + 1) * 256]) for j in range(4)]
                      + [(hs16[0:32], negCs[0:32, b * 256:(b + 1) * 256])])
                chain(o[:, 256:384], [(qbd[:, b % 2, j * P:(j + 1) * P], kT[:, j, SEQ:T]) for j in range(4)]
                      + [(hs16[0:32], negCs[0:32, 2048:2176])]).then_inc(filled(("ss", b)), 1)

            def sample_turn(b):
                pe.wait_ge(s_exs, b + 1)
                o = take(pe, ("spt", b))
                for c in range(3):
                    m = tr(o[:, c * P:(c + 1) * P], sP[:, b % 2, c * P:(c + 1) * P], ident)
                m.then_inc(filled(("spt", b)), 1)

            def sample_v(b):
                pe.wait_ge(s_vp[b % 4], 16 * (b // 4 + 1))
                copied(pe, ("spt", b))
                o = take(pe, ("spv", b))
                v = [vp[:, b % 4, 0:512], vp[:, b % 4, 512:1024], va[:, NP, :]]
                chain(o[:, 0:512], [(sPT[:, b % 2, c * P:(c + 1) * P], v[c]) for c in range(3)]).then_inc(filled(("spv", b)), 1)

            def sample_out(b):
                copied(pe, ("spv", b))
                o = take(pe, ("soT", b))
                for j in range(4):
                    m = mm(o[:, j * 16:(j + 1) * 16], om[:, b % 2, j * P:(j + 1) * P], tsel, start=True, stop=True)
                m.then_inc(filled(("soT", b)), 1)

            past_keys(0)
            for b in range(DEC_B + 3):
                if b + 1 < DEC_B:
                    past_keys(b + 1)
                if b >= 3:
                    sample_out(b - 3)
                if b < DEC_B:
                    sample_scores(b)
                if 1 <= b <= DEC_B:
                    sample_turn(b - 1)
                if 2 <= b <= DEC_B + 1:
                    sample_v(b - 2)

            for n in range(NT):
                pe.wait_ge(s_xt[n], 32)
                turn_x("xT2", n, xs2[n])
            copied(pe, *[("xT2", n) for n in range(NT)])
            pe.wait_ge(s_b, 16 * 2)
            pe.wait_ge(s_a1, 1)
            for h in range(H_B):
                thirds(("qb", h), ("qb", h), x_parts)
                thirds(("kb", h), ("kb", h), x_parts)
                for g in range(3):
                    o = take(pe, ("la", h, g))
                    mm(o[:, 0:THIRD], wa2[:, h * P:(h + 1) * P], a1T[:, g * THIRD:(g + 1) * THIRD],
                       start=True, stop=True).then_inc(filled(("la", h, g)), 1)
                thirds(("rb", h, 0), ("rb", h, 0), x_parts)
                thirds(("rb", h, 1), ("rb", h, 1), x_parts)
                pe.wait_ge(s_ksr, h + 1)
                o = take(pe, ("kst", h, 0))
                for n in range(NP):
                    m = tr(o[:, n * P:(n + 1) * P], ks[:, n * P:(n + 1) * P], ident)
                m.then_inc(filled(("kst", h, 0)), 1)
                o = take(pe, ("kst", h, 1))
                tr(o[:, 0:P], ks[:, SEQ:T], ident).then_inc(filled(("kst", h, 1)), 1)

                def level(l):
                    if l < 7:
                        pe.wait_ge(s_xm, 7 * h + l + 1)
                        a = c = X[:, l % 2, :]
                    else:
                        a, c = kb, qb
                    o = take(pe, ("lv", h, l, 0))
                    for n in range(NP):
                        t = slice(n * P, (n + 1) * P)
                        m = mm(o[:, t], a[:, t], c[:, t], start=True, stop=True)
                    m.then_inc(filled(("lv", h, l, 0)), 1)
                    if l >= 3:
                        o = take(pe, ("lv", h, l, 1))
                        mm(o[:, 0:P], a[:, SEQ:T], c[:, SEQ:T], start=True, stop=True)\
                            .then_inc(filled(("lv", h, l, 1)), 1)

                weights(pe, ("vb", h, 1))
                for n in range(NT):
                    o = take(pe, ("vb", h, n))
                    pair_tile(o, ("vb", h, 0), n).then_inc(filled(("vb", h, n)), 1)
                    if n < 8:
                        level(n)
                w_last[("vb", h, 0)] = w_last[("vb", h, 1)] = ("vb", h, NT - 1)
                copied(pe, ("kst", h, 0), ("kst", h, 1), *[("lv", h, 7, g) for g in range(2)],
                       *[("lv", h, l, 0) for l in range(8)], *[("vb", h, n) for n in range(NT)])
                pe.wait_ge(s_qs, h + 1)

                def turn_out(n):
                    copied(pe, ("o", h, n))
                    o = take(pe, ("ot", h, n))
                    for c in range(2):
                        m = tr(o[:, c * P:(c + 1) * P], on[:, n % 3, c * P:(c + 1) * P], ident)
                    m.then_inc(filled(("ot", h, n)), 1)

                for n in range(NP):
                    o = take(pe, ("u", h, n))
                    mm(o[:, 0:DV], ktok[:, n, :], vb[:, n, :], start=True, stop=True).then_inc(filled(("u", h, n)), 1)
                    t = slice(n * P, (n + 1) * P)
                    pairs = [(AT[:, t], vb[:, n, :])]
                    if n > 0:
                        copied(pe, ("u", h, n - 1))
                        pairs.append((qs[:, t], St[:, n % 3, :]))
                    o = take(pe, ("o", h, n))
                    chain(o[:, 0:DV], pairs).then_inc(filled(("o", h, n)), 1)
                    if n >= 2:
                        turn_out(n - 2)
                pe.wait_ge(s_s0, 16 * (h + 1))
                pe.wait_ge(s_qsm, h + 1)
                o = take(pe, ("o", h, NP))
                chain(o[:, 0:DV], [(AT[:, SEQ:T], vb[:, NP, :])]
                      + [(qsm[:, b * P:(b + 1) * P], S0[:, b, :]) for b in range(DEC_B)])\
                    .then_inc(filled(("o", h, NP)), 1)
                turn_out(NP - 2)
                for c in range(4):
                    o = take(pe, ("us", h, c))
                    for b in range(2):
                        m = mm(o[:, b * DV:(b + 1) * DV], ksm[:, 2 * c + b, :], vb[:, NP, :], start=True, stop=True)
                    m.then_inc(filled(("us", h, c)), 1)
                    if c < 2:
                        turn_out(NP - 1 + c)

            for j in range(KT):
                thirds(("ga", j), ("ga", j), x_parts)
                thirds(("gb", j), ("gb", j), x_parts)
            for j in range(KT):
                thirds(("ya", j), ("ya", j), [lambda k, a=a: a[:, k, :] for a in (oah, oal)], kt=4, first=4)
            for j in range(KT):
                thirds(("yb", j), ("yb", j), [lambda k: obh[k // 4][:, k % 4, :], lambda k: obl[:, k, :]],
                       first=20)

            def turn_x1(n):
                pe.wait_ge(s_x1, n + 1)
                o = take(pe, ("x1T", n))
                for k in range(KT):
                    m = tr(o[:, k * P:(k + 1) * P], x1[:, n, k * P:(k + 1) * P], ident)
                m.then_inc(filled(("x1T", n)), 1)

            for c in range(2):
                for n in range(NT):
                    if c == 0 and n % 3 == 0:
                        pe.wait_ge(s_mt, 3 * (KT - 1) + n // 3 + 1)
                    t = slice(n * P, (n + 1) * P)
                    o = take(pe, ("wo", c, n))
                    for k in range(KT):
                        if n == 0 and k % 2 == 0:
                            pe.wait_ge(s_wol, 4 * c + k // 2 + 1)
                        for i, (a, b) in enumerate(split3(mh[:, k, t], ml[:, k, t], woh[c][:, k, :], wol[c][:, k, :])):
                            m = mm(o[:, 0:512], a, b, start=(k == i == 0), stop=(k == KT - 1 and i == 2))
                    m.then_inc(filled(("wo", c, n)), 1)
                    if c == 1 and n >= 2:
                        turn_x1(n - 2)
            turn_x1(NT - 2)
            turn_x1(NT - 1)
            last_turn = turn[("x1T", NT - 1)] % 4
            assert last_turn != 0, "its banks are the first to go up"
            copied(pe, *[("wo", 1, n) for n in range(NT)], *[("x1T", n) for n in range(NT - 1)])

            def up(j, d, v, g):
                if g == 0:
                    pe.wait_ge(s_wl, 4 * j + 2 * d + v + 1)
                if d == v == 0:
                    pe.wait_ge(s_xh, 3 * g + 3)
                    copied(pe, *[("x1T", n) for n in range(3 * g, 3 * g + 3)])
                b, n = up_use(j, d, v, g)
                t = slice(g * THIRD, (g + 1) * THIRD)
                if 6 * d + 3 * v + g >= 4:
                    pe.wait_ge(up_free[b], n)
                pairs = []
                for k in range(KT):
                    pairs += split3(wuh[:, d % 2, v, k, :], wul[:, d % 2, v, k, :], x1h[:, k, t], x1l[:, k, t])
                chain(bank[:, b, 0:THIRD], pairs).then_inc(up_full[b], 1)

            def new_columns(j, d):
                pe.wait_ge(s_cg, 4 * j + 2 * d + 4)
                if d:
                    pe.wait_ge(cn_free, 2 * j + d)
                for v in range(2):
                    m = tr(bank[0:18, 7, v * P:(v + 1) * P], cn[:, v, :], ident)
                m.then_inc(cn_full, 1)

            def down(j, d, half_tiles):
                if half_tiles and half_tiles[0] == 0:
                    pe.wait_ge(s_hl, 2 * j + d + 1)
                    pe.wait_ge(s_dl, 2 * j + d + 1)
                for w in half_tiles:
                    b, n = dn_use(j, d, w)
                    t, c = slice(w // 2 * P, (w // 2 + 1) * P), slice(w % 2 * 512, (w % 2 + 1) * 512)
                    if 18 * d + w >= 3:
                        pe.wait_ge(dn_free[b], n)
                    e = d % 2
                    chain(bank[:, 4 + b, :], split3(hh[:, e, t], hl[:, e, t], wdh[:, e, c], wdl[:, e, c]))\
                        .then_inc(dn_full[b], 1)

            def chunk(j, d):
                for g in range(6):
                    up(j, d, g // 3, g % 3)
                    if d and g == 2:
                        new_columns(j, d - 1)
                    if d:
                        down(j, d - 1, DOWN_AFTER[g])

            in_pairs(pe, chunk)
            new_columns(0, NC_FF - 1)
            down(0, NC_FF - 1, range(2 * NT))

            for b in range(4):
                pe.wait_ge(up_free[b], 6 * NC_FF // 4)
            for b in range(3):
                pe.wait_ge(dn_free[b], 6 * NC_FF)
            pe.wait_ge(cn_free, NC_FF)

            def embed_turn(n):
                pe.wait_ge(s_x2, n + 1)
                o = take(pe, ("x2T", n))
                for k in range(KT):
                    m = tr(o[:, k * P:(k + 1) * P], x1[:, n, k * P:(k + 1) * P], ident)
                m.then_inc(filled(("x2T", n)), 1)
                pe.wait_ge(s_pin[n % 2], 16 * (n // 2 + 1))
                o = take(pe, ("pT", n))
                for k in range(2):
                    m = tr(o[:, k * P:(k + 1) * P], pin[:, n % 2, k * P:(k + 1) * P], ident)
                m.then_inc(filled(("pT", n)), 1)

            def embed(n):
                if n == 0:
                    pe.wait_ge(s_pl, KT + 2)
                copied(pe, ("x2T", n), ("pT", n))
                for name, w, a, kt in (("pg", (plgh, plgl), (x2h, x2l), KT), ("pp", (plh, pll), (pTh, pTl), 2)):
                    o = take(pe, (name, n))
                    for c in range(2):
                        cc = slice(c * 512, (c + 1) * 512)
                        pairs = []
                        for k in range(kt):
                            pairs += split3(a[0][:, n % 2, k, :], a[1][:, n % 2, k, :], w[0][:, k, cc], w[1][:, k, cc])
                        m = chain(o[:, cc], pairs)
                    m.then_inc(filled((name, n)), 1)

            embed_turn(0)
            for n in range(NT):
                if n + 1 < NT:
                    embed_turn(n + 1)
                embed(n)

        @block.scalar
        def _(act):
            steps = [0]

            def link(ins):
                steps[0] += 1
                ins.then_inc(s_act, 1)
                act.wait_ge(s_act, steps[0])

            def copy(out, in_, scale=1.0):
                return act.activation(out, in_, ACT.Copy, scale=scale)

            def split_hi(*names):
                for n in names:
                    if n < FIRST_UP:
                        if n >= W_SLOTS:
                            past_pe(act, w_last[chunks[n - W_SLOTS][0]])
                        act.wait_ge(w_in_sem[n % W_SLOTS], 16 * (n // W_SLOTS + 1))
                        kt = chunks[n][2]
                        copy(ringh[:, n % W_SLOTS, 0:kt], ring[:, n % W_SLOTS, 0:kt]).then_inc(s_rh, 1)

            def x_hi(key):
                for n in range(NT):
                    o = product(act, (key, n))
                    copy(xh[:, :, n * P:(n + 1) * P], o.rearrange("p (k t) -> p k t", k=KT)).then_inc(s_xh1, 1)

            act.wait_ge(s_const, 16)
            x_hi("xT")
            o = product(act, "cacheT")
            copy(cacheT, o[:, 0:704].rearrange("p (c r) -> p c r", c=44)).then_inc(drained("cacheT"), 1)
            act.wait_ge(s_small, 48)
            past_pe(act, ("xT", NT - 1), "cacheT", "cwT")
            act.wait_ge(s_nc0, 3)
            copy(wfh, wf).then_inc(s_sm, 1)
            split_hi(0, 1, 2)
            past_pe(act, ("lfp", 1))
            for g in range(3):
                o = product(act, ("f", g))
                act.activation(fz[:, g * THIRD:(g + 1) * THIRD], o[0:H_A, 0:THIRD], ACT.Identity, bias=bfg)
                copy(a1s[:, g * THIRD:(g + 1) * THIRD], o[32:32 + RANK, 0:THIRD]).then_inc(drained(("f", g)), 1)
            copied(act, ("f", 0), ("f", 1), ("f", 2))
            link(act.activation(fa, fz, ACT.Abs))
            link(act.activation(fa, fa, ACT.Exp, scale=-1.0))
            act.activation(fa, fa, ACT.Ln, bias=one[0:H_A, :]).then_inc(s_fz, 1)
            for j in range(4):
                for g in range(3):
                    o = product(act, ("qa", j, g))
                    copy(qT[:, j, g * THIRD:(g + 1) * THIRD], o[:, 0:THIRD], DH ** -0.5).then_inc(drained(("qa", j, g)), 1)
                split_hi(j + 3)
            for j in range(4):
                split_hi(j + 7)
            for q in range(2):
                for n in range(NT):
                    o = product(act, ("va", q, n))
                    copy(va[:, n, q * 256:(q + 1) * 256], o[:, 0:256]).then_inc(drained(("va", q, n)), 1)
                if q == 0:
                    split_hi(11, 12)

            def bias_rows(h):
                if h == 0:
                    copied(act, ("kt", NT - 1), ("kt", NT - 2))
                if h >= 2:
                    act.wait_ge(s_max, NP * (h - 1))
                    act.wait_ge(s_dg, h - 1)
                o = product(act, ("cb", h))
                copy(cb[:, h % 2, :], o).then_inc(drained(("cb", h)), 1)

            def probs(u):
                h, i = UNITS[u]
                act.wait_ge(s_max, u + 1)
                n = (i + 1) * P
                act.activation(S[u % 3][:, 0:n], S[u % 3][:, 0:n], ACT.Exp, bias=nm[:, u % 4:u % 4 + 1],
                               accum_out=rs[:, u % 4:u % 4 + 1]).then_inc(s_exp, 1)

            def copy_probs(u):
                if u % 2 == 1:
                    h, i = UNITS[u]
                    o = product(act, ("pt", u))
                    if u >= 2:
                        past_pe(act, ("pv", u - 2))
                    copy(PT[:, u % 2, 0:(i + 1) * P], o[:, 0:(i + 1) * P]).then_inc(drained(("pt", u)), 1)

            NU = len(UNITS)
            past_pe(act, ("va", 1, NT - 1))
            for j in range(4):
                copy(qO[DH:P, j, :], qT[DH:P, j, 0:SEQ]).then_inc(s_qo, 1)
            bias_rows(0)
            for u in range(NU + 4):
                if u >= 4:
                    h, i = UNITS[u - 4]
                    r = h % 2 * DH
                    o = product(act, ("pv", u - 4))
                    if h == 4 and i == NP - 1:
                        for q in range(4):
                            act.wait_ge(s_ok[q], 16 * (NT // 4 + (q < NT % 4)))
                    copy(oaT[r:r + DH, h // 2, i * P:(i + 1) * P], o[r:r + DH, 0:P]).then_inc(drained(("pv", u - 4)), 1)
                if u < NU:
                    if u % 8 == 6 and UNITS[u][0] + 1 < H_A:
                        bias_rows(UNITS[u][0] + 1)
                    if u >= 4:
                        act.wait_ge(s_nrm, u - 3)
                    probs(u)
                if 2 <= u <= NU + 1:
                    copy_probs(u - 2)

            split_hi(13, 14)

            def past_turned(b):
                o = product(act, ("kpT", b))
                if b >= 2:
                    past_pe(act, ("ss", b - 2))
                copy(kpT[:, b % 2, :], o).then_inc(drained(("kpT", b)), 1)

            past_pe(act, ("pv", NU - 1))
            past_turned(0)
            for b in range(DEC_B + 1):
                if b + 1 < DEC_B:
                    past_turned(b + 1)
                if b >= 1:
                    o = product(act, ("spt", b - 1))
                    if b >= 3:
                        past_pe(act, ("spv", b - 3))
                    copy(sPT[:, (b - 1) % 2, :], o[:, 0:384]).then_inc(drained(("spt", b - 1)), 1)
                if b < DEC_B:
                    act.wait_ge(s_smx, b + 1)
                    if b >= 2:
                        past_pe(act, ("spt", b - 2))
                    o = product(act, ("ss", b))
                    act.activation(sP[:, b % 2, 256:384], sN[:, b % 2, :], ACT.Exp, bias=nm[:, b % 2:b % 2 + 1],
                                   accum_out=rsb[:, b % 2:b % 2 + 1])
                    act.activation(sP[:, b % 2, 0:256], o[:, 0:256], ACT.Exp, bias=nm[:, b % 2:b % 2 + 1],
                                   accum_out=rs[:, b % 2:b % 2 + 1]).then_inc(s_exs, 1)

            copied(act, *[("soT", b) for b in range(DEC_B)], *[("spv", b) for b in range(DEC_B)])
            x_hi("xT2")
            copy(a1T, a1s).then_inc(s_a1, 1)

            act.wait_ge(s_ov, 32)
            act.wait_ge(s_ol, 32)
            act.wait_ge(s_qbd, DEC_B)
            act.wait_ge(s_cols, 32)
            act.wait_ge(s_oas, 16)
            for h in range(H_B):
                for g in range(3):
                    o = product(act, ("qb", h, g))
                    copy(qb[:, g * THIRD:(g + 1) * THIRD], o[:, 0:THIRD], DK ** -0.5).then_inc(drained(("qb", h, g)), 1)
                m = 12 + 6 * h
                split_hi(m + 3)
                for g in range(3):
                    o = product(act, ("la", h, g))
                    act.activation(zb[:, g * THIRD:(g + 1) * THIRD], o[:, 0:THIRD], ACT.Identity, bias=ba2[:, h:h + 1])\
                        .then_inc(drained(("la", h, g)), 1)
                split_hi(m + 4)
                copied(act, *[("la", h, g) for g in range(3)])
                if h:
                    past_pe(act, ("lv", h - 1, 6, 1))
                link(act.activation(X[:, 0, :], zb, ACT.Abs))
                link(act.activation(X[:, 0, :], X[:, 0, :], ACT.Exp, scale=-1.0))
                act.activation(X[:, 0, :], X[:, 0, :], ACT.Ln, bias=one).then_inc(s_lnz, 1)
                act.wait_ge(s_bsc, h + 1)
                link(act.activation(X[:, 1, :], b16, ACT.Exp, scale=1.0 / TAU))
                if h:
                    copied(act, ("u", h - 1, NP - 1), *[("us", h - 1, c) for c in range(4)])
                act.wait_ge(s_kd, h + 1)
                link(act.activation(ks, ks, ACT.Exp, scale=1.0 / TAU))
                link(act.activation(dl[:, 0:8], b16[:, 0:SEQ].rearrange("p (n t) -> p n t", t=P)[:, :, P - 1], ACT.Exp,
                                    scale=1.0 / TAU))
                act.activation(dl[:, 8:16], b16[:, SEQ:T].rearrange("p (n t) -> p n t", t=DEC_T)[:, :, DEC_T - 1], ACT.Exp,
                               scale=1.0 / TAU).then_inc(s_ee, 1)
                for c in range(2):
                    if h:
                        act.wait_ge(s_obs, 16 * h)
                    for g in range(3):
                        o = product(act, ("rb", h, c, g))
                        act.activation(obT[:, c, g * THIRD:(g + 1) * THIRD], o[:, 0:THIRD], ACT.Silu)\
                            .then_inc(drained(("rb", h, c, g)), 1)
                    split_hi(m + 5 + c)
                for n in range(NT):
                    if n < 7:
                        act.wait_ge(s_xl, 7 * h + n + 1)
                        t = SEQ if HALVES[n] > 8 else T
                        act.activation(X[:, n % 2, 0:t], X[:, n % 2, 0:t], ACT.Exp, scale=1.0 / TAU).then_inc(s_xe, 1)
                    o = product(act, ("vb", h, n))
                    copy(vb[:, n, :], o[:, 0:DV]).then_inc(drained(("vb", h, n)), 1)
                split_hi(m + 7, m + 8)
                for n in range(NT):
                    o = product(act, ("o", h, n))
                    if n:
                        act.wait_ge(s_ssq, NT * h + n)
                    act.activation(sq, o[:, 0:DV], ACT.Square, accum_out=ss[:, n:n + 1]).then_inc(s_ssq, 1)
                    act.wait_ge(s_rst, NT * h + n + 1)
                    if n >= 3:
                        past_pe(act, ("ot", h, n - 3))
                    act.activation(on[:, n % 3, :], o[:, 0:DV], ACT.Copy, scale=rstd[:, n:n + 1])\
                        .then_inc(drained(("o", h, n)), 1)

            act.wait_ge(s_ost, 32 * H_B)
            for j in range(KT):
                for q, (name, gate) in enumerate((("ga", gate_a), ("gb", gate_b))):
                    for g in range(3):
                        o = product(act, (name, j, g))
                        act.activation(gate[:, j, g * THIRD:(g + 1) * THIRD], o[:, 0:THIRD], ACT.Sigmoid)\
                            .then_inc(drained((name, j, g)), 1)
                    split_hi(w_index[(name, j)] + 3)
            act.wait_ge(s_oai, 16)
            past_pe(act, ("gb", KT - 1, 2))
            for g in range(3):
                for k in range(4):
                    t = slice(g * THIRD, (g + 1) * THIRD)
                    copy(oah[:, k, t], oar[:, k, t]).then_inc(s_oh, 1)
            for j in range(KT):
                past_pe(act, ("ya", j, 2))
                split_hi(w_index[("ya", j)] + 3)
                if j == 3:
                    act.wait_ge(s_obi, 64)
                if j >= 4:
                    copy(obh[0][:, j - 4, :], obr[:, j - 4, :]).then_inc(s_oh, 1)
            for g in range(3):
                for k in range(4):
                    t = slice(g * THIRD, (g + 1) * THIRD)
                    copy(obh[1][:, k, t], obr[:, k + 4, t]).then_inc(s_oh, 1)
            for j in range(KT):
                for g in range(3):
                    n = 3 * j + g
                    act.wait_ge(s_mr, n + 1)
                    t = slice(g * THIRD, (g + 1) * THIRD)
                    copy(mh[:, j, t], gate_a[:, j, t]).then_inc(s_mh, 1)
                split_hi(w_index[("yb", j)] + 3)
                if j >= 4:
                    i = w_index[("yb", j)] % W_SLOTS
                    act.wait_ge(s_wo[0], 16)
                    past_pe(act, w_last[("yb", j)])
                    copy(woh[0][:, 2 * i:2 * i + 2, :], wor[0][:, 2 * i:2 * i + 2, :]).then_inc(s_woh, 1)
            act.wait_ge(s_wo[1], 16)
            for i in range(4):
                copy(woh[1][:, 2 * i:2 * i + 2, :], wor[1][:, 2 * i:2 * i + 2, :]).then_inc(s_woh, 1)
            def up_hi(j, d, v):
                act.wait_ge(w_in_sem[2 * (d % 2) + v], 16 * UP_ROUND + 16 * j + 16 * (d // 2 + 1))
                copy(wuh[:, d % 2, v], rawu[:, d % 2, v]).then_inc(s_wh, 1)

            past_pe(act, ("wo", 0, NT - 1))
            for v in range(2):
                up_hi(0, 0, v)
            for n in range(NT):
                o = product(act, ("x1T", n))
                copy(x1h[:, :, n * P:(n + 1) * P], o.rearrange("p (k t) -> p k t", k=KT)).then_inc(s_xh, 1)
                copy(x1[:, n, :], x1[:, n, :], ALPHA).then_inc(s_xa, 1)

            def new_columns(j, d):
                act.wait_ge(cn_full, 2 * j + d + 1)
                if d:
                    act.wait_ge(s_ocn, 64 * j + 32 * d)
                copy(cno, bank[0:18, 7, 0:256]).then_inc(cn_free, 1)

            def halves(j, d):
                more = d != NC_FF - 1
                for v in range(2):
                    act.wait_ge(s_cg, 4 * j + 2 * d + v + 1)
                    u = U[:, v, :]
                    for g in range(3):
                        b, n = up_use(j, d, v, g)
                        act.wait_ge(up_full[b], n + 1)
                        if g < 2:
                            copy(u[:, 2 + g * THIRD:2 + (g + 1) * THIRD], bank[:, b, 0:THIRD]).then_inc(up_free[b], 1)
                        else:
                            copy(u[:, 2 + 2 * THIRD:2 + SEQ], bank[:, b, 0:SEQ - 2 * THIRD])
                            copy(u[:, 2 + SEQ:146 + SEQ].rearrange("p (b t) -> p b t", t=18)[:, :, 2:18],
                                 bank[:, b, SEQ - 2 * THIRD:THIRD].rearrange("p (b t) -> p b t", t=16)).then_inc(up_free[b], 1)
                    if v == 0:
                        if more:
                            up_hi(j, d + 1, 0)
                            up_hi(j, d + 1, 1)
                        if d:
                            new_columns(j, d - 1)
                        act.wait_ge(s_wdi[d % 2], 16 * j + 16 * (d // 2 + 1))
                        copy(wdh[:, d % 2, :], rawd[:, d % 2, :]).then_inc(s_dh, 1)
                act.wait_ge(s_conv, 4 * j + 2 * d + 2)
                act.activation(y[:, 1, 0:1168], y[:, 1, 0:1168], ACT.Gelu_apprx_tanh).then_inc(s_gel, 1)
                act.wait_ge(s_hm, 2 * j + d + 1)
                copy(hh[:, d % 2, 0:SEQ], y[:, 0, 0:SEQ])
                copy(hh[:, d % 2, SEQ:T].rearrange("p (b t) -> p b t", t=DEC_T),
                     y[:, 0, SEQ + 2:SEQ + 146].rearrange("p (b t) -> p b t", t=18)[:, :, 0:DEC_T]).then_inc(s_hh, 1)

            in_pairs(act, halves)
            new_columns(0, NC_FF - 1)

            def ple_hi(k, w, h):
                act.wait_ge(s_plg[k] if w is rplg else s_ple, 16)
                copy(h[:, k, :], w[:, k, :]).then_inc(s_ph, 1)

            for b in range(4):
                act.wait_ge(up_full[b], 6 * NC_FF // 4)
            for k in range(KT):
                ple_hi(k, rplg, plgh)
            for k in range(2):
                ple_hi(k, rpl, plh)

            def turn_in(n):
                o = product(act, ("x2T", n))
                if n >= 2:
                    past_pe(act, ("pg", n - 2))
                copy(x2h[:, n % 2], o.rearrange("p (k t) -> p k t", k=KT)).then_inc(s_x2h, 1)
                o = product(act, ("pT", n))
                if n >= 2:
                    past_pe(act, ("pp", n - 2))
                copy(pTh[:, n % 2], o[:, 0:256].rearrange("p (k t) -> p k t", k=2)).then_inc(s_x2h, 1)

            turn_in(0)
            for n in range(NT):
                if n + 1 < NT:
                    turn_in(n + 1)
                o = product(act, ("pg", n))
                if n >= 2:
                    copied(act, ("pp", n - 2))
                act.activation(sge[:, n % 2, :], o, ACT.Sigmoid).then_inc(drained(("pg", n)), 1)

        @block.vector
        def _(dve):
            steps = [0]

            def link(ins):
                steps[0] += 1
                ins.then_inc(s_dve, 1)
                dve.wait_ge(s_dve, steps[0])

            def stt(out, in0, scalar, in1, op0, op1):
                return dve.scalar_tensor_tensor(out=out, in0=in0, scalar=scalar, in1=in1, op0=op0, op1=op1)

            def rows(ap, n, w):
                return ap.rearrange("p (n w) -> p n w", w=w)[:, 0:n]

            def split_lo(*names):
                for n in names:
                    if n < FIRST_UP:
                        dve.wait_ge(s_rh, n + 1)
                        i, kt = n % W_SLOTS, chunks[n][2]
                        dve.tensor_tensor(ringl[:, i, 0:kt], ring[:, i, 0:kt], ringh[:, i, 0:kt].bitcast(F32), ALU.subtract)\
                            .then_inc(s_rl, 1)

            def x_lo(key, rounds):
                for n in range(NT):
                    o = product(dve, (key, n))
                    dve.wait_ge(s_xh1, NT * rounds + n + 1)
                    t = slice(n * P, (n + 1) * P)
                    dve.tensor_tensor(xl[:, :, t], o.rearrange("p (k t) -> p k t", k=KT), xh[:, :, t].bitcast(F32),
                                      ALU.subtract).then_inc(drained((key, n)), 1)

            dve.wait_ge(s_const, 16)
            x_lo("xT", 0)
            o = product(dve, "cwT")
            dve.tensor_copy(cwT, o[:, 0:176].rearrange("p (a c) -> p a c", a=4)).then_inc(drained("cwT"), 1)
            dve.wait_ge(s_nc0, 3)
            for n in range(2):
                o = product(dve, ("lfp", n))
                for c in range(4):
                    b = 4 * n + c
                    ins = dve.tensor_tensor_scan(negCs[0:H_A, b * 256:(b + 1) * 256], one[0:H_A, :].to_broadcast([H_A, 256]),
                                                 o[0:H_A, c * 256:(c + 1) * 256], 0.0, ALU.mult, ALU.subtract)
                ins.then_inc(drained(("lfp", n)), 1)
            dve.wait_ge(s_sm, 1)
            dve.tensor_tensor(wfl, wf, wfh.bitcast(F32), ALU.subtract).then_inc(s_sl, 1)
            split_lo(0, 1, 2)
            dve.wait_ge(s_fz, 1)
            stt(fz, fz, 0.0, fa, ALU.min, ALU.subtract).then_inc(s_lf8, 1)
            dve.wait_ge(s_lf8, 1)
            copied(dve, ("lfp", 0), ("lfp", 1))
            for b in range(DEC_B):
                dve.tensor_tensor_scan(negCs[0:H_A, 2048 + b * 16:2048 + (b + 1) * 16], one[0:H_A, :].to_broadcast([H_A, 16]),
                                       fz[:, SEQ + b * 16:SEQ + (b + 1) * 16], negCs[0:H_A, b * 256 + 255:b * 256 + 256],
                                       ALU.mult, ALU.subtract)
            dve.tensor_tensor_scan(negC[0:H_A, 0:SEQ], one[0:H_A, :].to_broadcast([H_A, SEQ]), fz[:, 0:SEQ], 0.0,
                                   ALU.mult, ALU.subtract).then_inc(s_negc, 1)
            split_lo(3, 4, 5, 6)
            for j in range(4):
                for g in range(3):
                    o = product(dve, ("ka", j, g))
                    dve.tensor_copy(kT[:, j, g * THIRD:(g + 1) * THIRD], o[:, 0:THIRD]).then_inc(drained(("ka", j, g)), 1)
                split_lo(j + 7)
            split_lo(11, 12)
            o = product(dve, "lfT")
            dve.tensor_copy(lfo, o[:, 0:72].rearrange("p (n h) -> p n h", n=NT)).then_inc(drained("lfT"), 1)
            for n in range(NT):
                o = product(dve, ("kt", n))
                if n >= 4:
                    dve.wait_ge(s_ok[n % 4], 16 * (n // 4))
                dve.tensor_copy(kst[:, n % 4, :], o[:, 0:512]).then_inc(drained(("kt", n)), 1)

            def row_max(u):
                h, i = UNITS[u]
                n = i * P
                o = product(dve, ("s", u))
                if i == NP - 1:
                    copied(dve, ("cb", h))
                    dve.wait_ge(s_dg, h + 1)
                if u >= 3:
                    past_pe(dve, ("pt", u - 3))
                m, v = mx[:, u % 4:u % 4 + 1], nm[:, u % 4:u % 4 + 1]
                init = -3e38
                if i:
                    link(dve.tensor_tensor_reduce(S[u % 3][:, 0:n], o[:, 0:n], cb[:, h % 2, 0:n], 1.0, -3e38, ALU.add,
                                                  ALU.max, m))
                    init = m
                dve.tensor_tensor_reduce(S[u % 3][:, n:n + P], o[:, n:n + P], dg[:, h % 2, n:n + P], 1.0, init,
                                         ALU.add, ALU.max, m).then_inc(drained(("s", u)), 1)
                copied(dve, ("s", u))
                dve.tensor_scalar(v, m, -1.0, None, ALU.mult).then_inc(s_max, 1)

            def copy_probs(u):
                if u % 2 == 0:
                    h, i = UNITS[u]
                    o = product(dve, ("pt", u))
                    if u >= 2:
                        past_pe(dve, ("pv", u - 2))
                    dve.tensor_copy(PT[:, u % 2, 0:(i + 1) * P], o[:, 0:(i + 1) * P]).then_inc(drained(("pt", u)), 1)

            def norm_probs(u):
                h, i = UNITS[u]
                dve.wait_ge(s_exp, u + 1)
                q, n = slice(u % 4, u % 4 + 1), (i + 1) * P
                link(dve.reciprocal(ri[:, q], rs[:, q]))
                dve.tensor_scalar(S[u % 3][:, 0:n], S[u % 3][:, 0:n], ri[:, q], None, ALU.mult).then_inc(s_nrm, 1)

            NU = len(UNITS)
            for u in range(NU + 3):
                if u < NU:
                    row_max(u)
                if 1 <= u <= NU:
                    norm_probs(u - 1)
                if 2 <= u <= NU + 1:
                    copy_probs(u - 2)

            split_lo(13, 14)
            past_pe(dve, ("pv", NU - 1), ("pv", NU - 2))
            for b in range(DEC_B + 3):
                if b >= 3:
                    o = product(dve, ("soT", b - 3))
                    t = SEQ + 16 * (b - 3)
                    dve.tensor_copy(oaT[:, :, t:t + 16], o[:, 0:64].rearrange("p (j t) -> p j t", j=4))\
                        .then_inc(drained(("soT", b - 3)), 1)
                if b < DEC_B:
                    o = product(dve, ("ss", b))
                    q, qi = slice(b % 2, b % 2 + 1), slice(b % 4, b % 4 + 1)
                    if b >= 2:
                        dve.wait_ge(s_exs, b - 1)
                    link(dve.tensor_tensor_reduce(sN[:, b % 2, :], o[:, 256:384], win[:, 112 - 16 * b:240 - 16 * b], 1.0,
                                                  -3e38, ALU.add, ALU.max, mxb[:, q]))
                    link(dve.tensor_reduce(mx[:, q], o[:, 0:256], AX.X, ALU.max))
                    stt(nm[:, q], mx[:, q], mxb[:, q], neg1, ALU.max, ALU.mult).then_inc(s_smx, 1)
                if 2 <= b <= DEC_B + 1:
                    o = product(dve, ("spv", b - 2))
                    if b >= 4:
                        past_pe(dve, ("soT", b - 4))
                    q = slice((b - 2) % 4, (b - 2) % 4 + 1)
                    stt(om[:, b % 2, :], o[:, 0:512], ri[:, q], omask, ALU.mult, ALU.mult)\
                        .then_inc(drained(("spv", b - 2)), 1)
                if b < DEC_B:
                    q = slice(b % 2, b % 2 + 1)
                    dve.wait_ge(s_exs, b + 1)
                    dve.tensor_tensor(ri[:, qi], rs[:, q], rsb[:, q], ALU.add).then_inc(drained(("ss", b)), 1)
                    copied(dve, ("ss", b))
                    link(dve.reciprocal(ri[:, qi], ri[:, qi]))

            copied(dve, *[("soT", b) for b in range(DEC_B)])
            x_lo("xT2", 1)
            dve.wait_ge(s_qbd, DEC_B)
            dve.wait_ge(s_b, 16 * 2)
            dve.wait_ge(s_cols, 32)
            dve.wait_ge(s_oas, 16)
            for h in range(H_B):
                m = 12 + 6 * h
                split_lo(m + 3)
                for g in range(3):
                    o = product(dve, ("kb", h, g))
                    dve.tensor_copy(kb[:, g * THIRD:(g + 1) * THIRD], o[:, 0:THIRD]).then_inc(drained(("kb", h, g)), 1)
                split_lo(m + 4)
                dve.wait_ge(s_lnz, h + 1)
                link(stt(zb, zb, 0.0, X[:, 0, :], ALU.min, ALU.subtract))
                dve.tensor_tensor_scan(b16, scanm, zb, 0.0, ALU.mult, ALU.add).then_inc(s_bsc, 1)
                dve.wait_ge(s_bsc, h + 1)
                if h:
                    past_pe(dve, ("kst", h - 1, 1))
                bp, bs = rows(b16[:, 0:SEQ], NP, P), rows(b16[:, SEQ:T], DEC_B, DEC_T)
                kp_, ks_ = rows(ks[:, 0:SEQ], NP, P), rows(ks[:, SEQ:T], DEC_B, DEC_T)
                dve.tensor_tensor(kp_, bp[:, :, P - 1:P].to_broadcast([P, NP, P]), bp, ALU.subtract)
                dve.tensor_tensor(ks_, bs[:, :, DEC_T - 1:DEC_T].to_broadcast([P, DEC_B, DEC_T]), bs, ALU.subtract)\
                    .then_inc(s_kd, 1)
                dve.wait_ge(s_ee, h + 1)
                dve.tensor_tensor(qs, qb, X[:, 1, :], ALU.mult).then_inc(s_qs, 1)
                dve.tensor_tensor(ks, ks, kb, ALU.mult).then_inc(s_ksr, 1)
                dve.wait_ge(s_qs, h + 1)
                split_lo(m + 5)

                def level_log(l):
                    if l >= 2:
                        past_pe(dve, ("lv", h, l - 2, 0))
                        if l - 2 >= 3:
                            past_pe(dve, ("lv", h, l - 2, 1))
                    hf = HALVES[l]
                    t = SEQ if hf > 8 else T
                    xv = X[:, l % 2, 0:t].rearrange("p (n a j) -> p n a j", a=2, j=hf)
                    bv = b16[:, 0:t].rearrange("p (n a j) -> p n a j", a=2, j=hf)
                    ref = bv[:, :, 0, hf - 1:hf].to_broadcast([P, t // (2 * hf), hf])
                    dve.tensor_tensor(xv[:, :, 0, :], ref, bv[:, :, 0, :], ALU.subtract)
                    dve.tensor_tensor(xv[:, :, 1, :], bv[:, :, 1, :], ref, ALU.subtract).then_inc(s_xl, 1)

                def level_scale(l):
                    hf = HALVES[l]
                    t = SEQ if hf > 8 else T
                    dve.wait_ge(s_xe, 7 * h + l + 1)
                    v = [a[:, 0:t].rearrange("p (n a j) -> p n a j", a=2, j=hf) for a in (X[:, l % 2, :], kb, qb)]
                    dve.tensor_tensor(v[0][:, :, 0, :], v[0][:, :, 0, :], v[1][:, :, 0, :], ALU.mult)
                    dve.tensor_tensor(v[0][:, :, 1, :], v[0][:, :, 1, :], v[2][:, :, 1, :], ALU.mult).then_inc(s_xm, 1)

                def level_take(l):
                    mask = levm[:, l * P:(l + 1) * P] if l < 7 else ident.bitcast(U32)
                    o = product(dve, ("lv", h, l, 0))
                    if l:
                        copied(dve, ("lv", h, l - 1, 0))
                    dve.copy_predicated(rows(AT[:, 0:SEQ], NP, P), mask.rearrange("p (a t) -> p a t", a=1).to_broadcast([P, NP, P]),
                                        rows(o, NP, P)).then_inc(drained(("lv", h, l, 0)), 1)
                    if l >= 3:
                        o = product(dve, ("lv", h, l, 1))
                        if l > 3:
                            copied(dve, ("lv", h, l - 1, 1))
                        dve.copy_predicated(AT[:, SEQ:T], mask, o[:, 0:P]).then_inc(drained(("lv", h, l, 1)), 1)

                level_log(0)
                level_log(1)
                o = product(dve, ("kst", h, 0))
                dve.tensor_copy(ktok, rows(o, NP, P)).then_inc(drained(("kst", h, 0)), 1)
                o = product(dve, ("kst", h, 1))
                dve.tensor_tensor(ksm, o[:, 0:P].rearrange("p (a t) -> p a t", a=1).to_broadcast([P, DEC_B, P]),
                                  bmask.rearrange("p (b a) -> p b a", a=1).to_broadcast([P, DEC_B, P]), ALU.mult)\
                    .then_inc(drained(("kst", h, 1)), 1)
                dve.wait_ge(s_at0, h + 1)
                level_scale(0)
                for l in range(8):
                    if l + 1 < 7:
                        level_scale(l + 1)
                    if l + 2 < 7:
                        level_log(l + 2)
                    level_take(l)
                    if l == 1:
                        split_lo(m + 6)

                def out_turned(n):
                    o = product(dve, ("ot", h, n))
                    for c in range(2):
                        v = obT[:, c, n * P:(n + 1) * P]
                        ins = stt(v, o[:, c * P:(c + 1) * P], ggla[:, 2 * h + c:2 * h + c + 1], v, ALU.mult, ALU.mult)
                    ins.then_inc(drained(("ot", h, n)), 1)

                for n in range(NP):
                    o = product(dve, ("u", h, n))
                    if n >= 2:
                        past_pe(dve, ("o", h, n - 2))
                    if n == 1 and h:
                        dve.wait_ge(s_ost, 32 * h)
                    if n == 0:
                        ins = dve.tensor_copy(St[:, 1, :], o[:, 0:DV])
                    else:
                        copied(dve, ("u", h, n - 1))
                        ins = stt(St[:, (n + 1) % 3, :], St[:, n % 3, :], dl[:, n:n + 1], o[:, 0:DV], ALU.mult, ALU.add)
                    ins.then_inc(drained(("u", h, n)), 1)
                    if n >= 2:
                        out_turned(n - 2)
                    if n == 3:
                        split_lo(m + 7, m + 8)
                out_turned(NP - 2)
                past_pe(dve, ("o", h, NP))
                for c in range(4):
                    o = product(dve, ("us", h, c))
                    for b in range(2):
                        v = S0[:, 2 * c + b, :]
                        ins = stt(v, v, dl[:, 8 + 2 * c + b:9 + 2 * c + b], o[:, b * DV:(b + 1) * DV], ALU.mult, ALU.add)
                    ins.then_inc(drained(("us", h, c)), 1)
                    if c < 2:
                        out_turned(NP - 1 + c)

            for j in range(KT):
                split_lo(w_index[("ga", j)] + 3, w_index[("gb", j)] + 3)
            def branch_lo(i, lo, raw, hi):
                dve.wait_ge(s_oh, i + 1)
                dve.tensor_tensor(lo, raw, hi.bitcast(F32), ALU.subtract).then_inc(s_ol2, 1)

            for g in range(3):
                for k in range(4):
                    t = slice(g * THIRD, (g + 1) * THIRD)
                    branch_lo(4 * g + k, oal[:, k, t], oar[:, k, t], oah[:, k, t])
            for j in range(KT):
                for g in range(3):
                    o = product(dve, ("ya", j, g))
                    copied(dve, ("ga", j, g))
                    v = gate_a[:, j, g * THIRD:(g + 1) * THIRD]
                    dve.tensor_tensor(v, o[:, 0:THIRD], v, ALU.mult).then_inc(drained(("ya", j, g)), 1)
                split_lo(w_index[("ya", j)] + 3)
                if j >= 4:
                    branch_lo(8 + j, obl[:, j - 4, :], obr[:, j - 4, :], obh[0][:, j - 4, :])
            for g in range(3):
                for k in range(4):
                    t = slice(g * THIRD, (g + 1) * THIRD)
                    branch_lo(16 + 4 * g + k, obl[:, 4 + k, t], obr[:, 4 + k, t], obh[1][:, k, t])

            def merged_lo(n):
                j, t = n // 3, slice(n % 3 * THIRD, (n % 3 + 1) * THIRD)
                dve.wait_ge(s_mh, n + 1)
                dve.tensor_tensor(ml[:, j, t], gate_a[:, j, t], mh[:, j, t].bitcast(F32), ALU.subtract).then_inc(s_mt, 1)

            def wo_lo(q, c, i):
                dve.wait_ge(s_woh, q + 1)
                k = slice(2 * i, 2 * i + 2)
                dve.tensor_tensor(wol[c][:, k, :], wor[c][:, k, :], woh[c][:, k, :].bitcast(F32), ALU.subtract).then_inc(s_wol, 1)

            for j in range(KT):
                for g in range(3):
                    o = product(dve, ("yb", j, g))
                    copied(dve, ("gb", j, g))
                    v = gate_b[:, j, g * THIRD:(g + 1) * THIRD]
                    dve.tensor_tensor(v, o[:, 0:THIRD], v, ALU.mult).then_inc(drained(("yb", j, g)), 1)
                    if 3 * j + g >= 1:
                        merged_lo(3 * j + g - 1)
                split_lo(w_index[("yb", j)] + 3)
                if j >= 5:
                    wo_lo(j - 5, 0, w_index[("yb", j - 1)] % W_SLOTS)
            merged_lo(3 * KT - 1)
            wo_lo(3, 0, w_index[("yb", KT - 1)] % W_SLOTS)

            norms = [0]

            def stats(z):
                q = norms[0] % 4
                for c in range(2):
                    ins = dve.bn_stats(bnst[:, q, c * 6:(c + 1) * 6], z[:, c * 512:(c + 1) * 512])
                link(ins)
                dve.bn_aggr(mv[:, q, :], bnst[:, q, :]).then_inc(s_var, 1)
                norms[0] += 1

            def normed(z, out, gain, bias):
                q = (norms[0] - 1) % 4
                dve.wait_ge(s_var, norms[0])
                link(stt(z, z, mv[:, q, 0:1], gain, ALU.subtract, ALU.mult))
                dve.wait_ge(s_lrs, norms[0])
                return stt(out, z, lrs[:, q:q + 1], bias, ALU.mult, ALU.add)

            def x1_lo(n):
                dve.wait_ge(s_xh, n + 1)
                o = product(dve, ("x1T", n))
                t = slice(n * P, (n + 1) * P)
                dve.tensor_tensor(x1l[:, :, t], o.rearrange("p (k t) -> p k t", k=KT), x1h[:, :, t].bitcast(F32),
                                  ALU.subtract).then_inc(drained(("x1T", n)), 1)

            def add_x(c, n):
                o = product(dve, ("wo", c, n))
                z = x1[:, n, c * 512:(c + 1) * 512]
                stt(z, z, ALPHA, o[:, 0:512], ALU.mult, ALU.add).then_inc(drained(("wo", c, n)), 1)

            for n in range(NT):
                dve.wait_ge(s_xt[n], 48)
                add_x(0, n)
                if n >= 5:
                    wo_lo(4 + n - 5, 1, n - 5)
            def up_lo(j, d, v):
                dve.wait_ge(s_wh, 4 * j + 2 * d + v + 1)
                dve.tensor_tensor(wul[:, d % 2, v], rawu[:, d % 2, v], wuh[:, d % 2, v].bitcast(F32), ALU.subtract)\
                    .then_inc(s_wl, 1)

            dve.wait_ge(s_g1, 32)
            for n in range(NT):
                if n == 3:
                    up_lo(0, 0, 0)
                    up_lo(0, 0, 1)
                add_x(1, n)
                copied(dve, ("wo", 1, n))
                z = x1[:, n, :]
                stats(z)
                normed(z, z, g1, b1).then_inc(s_x1, 1)
                if n >= 2:
                    x1_lo(n - 2)
            x1_lo(NT - 2)
            x1_lo(NT - 1)

            def convolve(j, d, v):
                c = 2 * j + d
                for g in range(3):
                    b, n = up_use(j, d, v, g)
                    dve.wait_ge(up_free[b], n + 1)
                dve.wait_ge(s_up, 4 * j + 2 * d + v + 1)
                u, yv = U[:, v, :], y[:, v, 0:1168]
                w = [cwT[:, a, bass.ds(c + v * NC_FF, 1)] for a in range(4)]
                dve.tensor_scalar(yv, u[:, 0:1168], w[0], w[3], ALU.mult, ALU.add).then_inc(s_cv1, 1)
                dve.wait_ge(s_cv1, 4 * j + 2 * d + v + 1)
                stt(yv, u[:, 1:1169], w[1], yv, ALU.mult, ALU.add).then_inc(s_cv2, 1)
                dve.wait_ge(s_cv2, 4 * j + 2 * d + v + 1)
                stt(yv, u[:, 2:1170], w[2], yv, ALU.mult, ALU.add).then_inc(s_conv, 1)

            def add_down(j, d, half_tiles):
                for w in half_tiles:
                    b, m = dn_use(j, d, w)
                    dve.wait_ge(dn_full[b], m + 1)
                    z = x1[:, w // 2, (w % 2) * 512:(w % 2 + 1) * 512]
                    dve.tensor_tensor(z, z, bank[:, 4 + b, :], ALU.add).then_inc(dn_free[b], 1)

            def halves(j, d):
                def before(g):
                    if d:
                        add_down(j, d - 1, DOWN_AFTER[g])

                if d:
                    dve.wait_ge(s_hl, 2 * j + d)
                before(2)
                convolve(j, d, 0)
                before(3)
                if d != NC_FF - 1:
                    up_lo(j, d + 1, 0)
                    up_lo(j, d + 1, 1)
                before(4)
                dve.wait_ge(s_dh, 2 * j + d + 1)
                dve.tensor_tensor(wdl[:, d % 2, :], rawd[:, d % 2, :], wdh[:, d % 2, :].bitcast(F32), ALU.subtract)\
                    .then_inc(s_dl, 1)
                convolve(j, d, 1)
                dve.wait_ge(s_gel, 2 * j + d + 1)
                dve.tensor_tensor(y[:, 0, 0:1168], y[:, 0, 0:1168], y[:, 1, 0:1168], ALU.mult).then_inc(s_hm, 1)
                dve.wait_ge(s_hh, 2 * j + d + 1)
                e = d % 2
                dve.tensor_tensor(hl[:, e, 0:SEQ], y[:, 0, 0:SEQ], hh[:, e, 0:SEQ].bitcast(F32), ALU.subtract)
                dve.tensor_tensor(rows(hl[:, e, SEQ:T], DEC_B, DEC_T), rows(y[:, 0, SEQ + 2:SEQ + 146], DEC_B, 18)[:, :, 0:DEC_T],
                                  rows(hh[:, e, SEQ:T].bitcast(F32), DEC_B, DEC_T), ALU.subtract).then_inc(s_hl, 1)

            dve.wait_ge(s_xa, NT)
            in_pairs(dve, halves)

            def ple_lo(k, i, w, h, l):
                dve.wait_ge(s_ph, i + 1)
                dve.tensor_tensor(l[:, k, :], w[:, k, :], h[:, k, :].bitcast(F32), ALU.subtract).then_inc(s_pl, 1)

            def second(n):
                z = x1[:, n, :]
                stats(z)
                normed(z, z, g2, b2).then_inc(s_x2, 1)

            def turn_lo(n):
                dve.wait_ge(s_x2h, 2 * n + 2)
                o = product(dve, ("x2T", n))
                dve.tensor_tensor(x2l[:, n % 2], o.rearrange("p (k t) -> p k t", k=KT), x2h[:, n % 2].bitcast(F32),
                                  ALU.subtract).then_inc(drained(("x2T", n)), 1)
                o = product(dve, ("pT", n))
                dve.tensor_tensor(pTl[:, n % 2], o[:, 0:256].rearrange("p (k t) -> p k t", k=2), pTh[:, n % 2].bitcast(F32),
                                  ALU.subtract).then_inc(drained(("pT", n)), 1)

            add_down(0, NC_FF - 1, range(2 * NT))
            dve.wait_ge(s_g2, 64)
            for b in range(3):
                dve.wait_ge(dn_free[b], 6 * NC_FF)
            second(0)
            for k in range(PLG_POOL, KT):
                ple_lo(k, k, rplg, plgh, plgl)
            turn_lo(0)
            for k in range(2):
                ple_lo(k, KT + k, rpl, plh, pll)
            second(1)
            dve.wait_ge(s_ocn, 32 * NC_FF)
            for n in range(NT):
                if n + 2 < NT:
                    second(n + 2)
                if n + 1 < NT:
                    turn_lo(n + 1)
                copied(dve, ("pg", n))
                o = product(dve, ("pp", n))
                if n >= 3:
                    dve.wait_ge(s_oy[n % 3], 16 * (n // 3))
                z = z3[:, n % 3, :]
                dve.tensor_tensor(z, o, sge[:, n % 2, :], ALU.mult).then_inc(drained(("pp", n)), 1)
                copied(dve, ("pp", n))
                link(stt(z, x1[:, n, :], ALPHA, z, ALU.mult, ALU.add))
                stats(z)
                normed(z, z, g3, b3).then_inc(s_y, 1)

        @block.gpsimd
        def _(pool):
            pool.memset(negC, 0.0).then_inc(s_nc0, 1)
            pool.memset(negCs, 0.0).then_inc(s_nc0, 1)
            pool.memset(wf[:, :, H_A:32], 0.0).then_inc(s_nc0, 1)
            past_pe(pool, ("va", 1, NT - 1))
            copied(pool, *[("qa", j, g) for j in range(4) for g in range(3)])
            def clear_q(j):
                pool.memset(qO[0:DH, j, :], 0.0).then_inc(s_qz, 1)
                pool.wait_ge(s_qo, j + 1)
                pool.memset(qT[DH:P, j, 0:SEQ], 0.0).then_inc(s_qz, 1)

            for h in range(H_A):
                if h % 2 == 0:
                    if h:
                        pool.wait_ge(s_dg, h)
                    clear_q(h // 2)
                    pool.wait_ge(s_qz, h + 2)
                copied(pool, ("cb", h))
                if h >= 2:
                    pool.wait_ge(s_max, NP * (h - 1))
                pool.tensor_tensor(dg[:, h % 2, :].rearrange("p (n t) -> p n t", t=P), cb[:, h % 2, :].rearrange("p (n t) -> p n t", t=P),
                                   causal.rearrange("p (a t) -> p a t", a=1).to_broadcast([P, NP, P]), ALU.add).then_inc(s_dg, 1)

            NU = len(UNITS)
            copied(pool, *[("pv", u) for u in range(NU - 4, NU)])
            pool.memset(at(off["qbd"], 1312), 0.0).then_inc(s_pool, 1)
            pool.wait_ge(s_pool, 1)
            for b in range(DEC_B):
                if b >= 2:
                    past_pe(pool, ("ss", b - 2))
                for hh in range(2):
                    v = qbd[hh * DH:(hh + 1) * DH, b % 2, hh * 16:hh * 16 + 640].rearrange("p (j x) -> p j x", x=160)[:, :, 0:16]
                    ins = pool.tensor_copy(v, qT[hh * DH:(hh + 1) * DH, :, SEQ + 16 * b:SEQ + 16 * (b + 1)])
                ins.then_inc(s_qbd, 1)

            pool.wait_ge(s_ov, 32)
            copied(pool, ("soT", DEC_B - 1), ("soT", DEC_B - 2), ("spv", DEC_B - 1))
            pool.dma_start(oa_out, oaT).then_inc(s_oas, 16)
            past_pe(pool, ("xT2", NT - 1))
            pool.memset(qsm, 0.0).then_inc(s_pool, 1)
            for h in range(H_B):
                if h:
                    pool.wait_ge(s_ost, 32 * h)
                pool.dma_start(S0, state_gla[0].rearrange("b h c v -> h c b v")[h]).then_inc(s_s0, 16)
                pool.memset(AT, 0.0).then_inc(s_at0, 1)
                if h == 0:
                    pool.wait_ge(s_pool, 2)
                pool.wait_ge(s_qs, h + 1)
                pool.tensor_copy(qsm.rearrange("p (b x) -> p b x", x=P + DEC_T)[:, :, 0:DEC_T],
                                 qs[:, SEQ:T].rearrange("p (b t) -> p b t", t=DEC_T)).then_inc(s_qsm, 1)
                for n in range(NT):
                    pool.wait_ge(s_ssq, NT * h + n + 1)
                    pool.tensor_scalar(ms[:, n:n + 1], ss[:, n:n + 1], 1.0 / DV, LN_EPS, ALU.mult, ALU.add).then_inc(s_msq, 1)
                    pool.wait_ge(s_msq, NT * h + n + 1)
                    pool.tensor_tensor(rstd[:, n:n + 1], ms[:, n:n + 1], nhalf, ALU.pow).then_inc(s_rst, 1)
                copied(pool, ("u", h, NP - 1))
                pool.dma_start(st_p[0, 0, h], St[:, NP % 3, :]).then_inc(s_ost, 16)
                copied(pool, *[("us", h, c) for c in range(4)])
                pool.dma_start(st_s[0].rearrange("b h c v -> h c b v")[h], S0).then_inc(s_ost, 16)
                copied(pool, *[("ot", h, n) for n in range(NT)])
                pool.dma_start(ob_out[:, h], obT).then_inc(s_obs, 16)

            pool.wait_ge(s_obs, 16 * H_B)
            pool.dma_start(oar, oa_out).then_inc(s_oai, 16)
            past_pe(pool, ("gb", KT - 1, 2))
            for h in range(H_B):
                pool.dma_start(obr[:, 2 * h:2 * h + 2, :], ob_out[:, h]).then_inc(s_obi, 16)

            for j in range(KT):
                for g in range(3):
                    t = slice(g * THIRD, (g + 1) * THIRD)
                    copied(pool, ("ya", j, g), ("yb", j, g))
                    pool.tensor_tensor(gate_a[:, j, t], gate_a[:, j, t], gate_b[:, j, t], ALU.add).then_inc(s_mr, 1)

            norms = [0]

            def row_rstd():
                i = norms[0]
                q = i % 4
                norms[0] += 1
                pool.wait_ge(s_var, i + 1)
                pool.tensor_scalar(lve[:, q:q + 1], mv[:, q, 1:2], LN_EPS, None, ALU.add).then_inc(s_lve, 1)
                pool.wait_ge(s_lve, i + 1)
                pool.tensor_tensor(lrs[:, q:q + 1], lve[:, q:q + 1], nhalf, ALU.pow).then_inc(s_lrs, 1)

            for n in range(NT):
                row_rstd()

            past_pe(pool, ("wo", 1, NT - 1))
            pool.wait_ge(s_x1, NT)
            pool.memset(U[:, :, 0:2], 0.0).then_inc(s_cg, 2)

            def cached(j, d, v):
                pool.wait_ge(s_cg, 4 * j + 2 * d + v + 1)
                u = U[:, v, SEQ + 2:SEQ + 146].rearrange("p (b t) -> p b t", t=18)
                src = cacheT.rearrange("p c (b r) -> p c b r", r=2)[:, bass.ds(2 * j + d + v * NC_FF, 1), :, :]
                pool.tensor_copy(u[:, :, 0:2], src.rearrange("p a b r -> p (a b) r")).then_inc(s_up, 1)

            def gather(j, d, v):
                if v == 0 and d:
                    pool.wait_ge(cn_free, 2 * j + d)
                pool.wait_ge(s_conv, 4 * j + 2 * d + v + 1)
                u = U[:, v, :]
                pool.tensor_tensor(cn[:, v, 0:2], u[:, SEQ:SEQ + 2], one.to_broadcast([P, 2]), ALU.mult)
                pool.tensor_copy(cn[:, v, 2:18].rearrange("p (b r) -> p b r", r=2),
                                 u[:, SEQ + 2:SEQ + 146].rearrange("p (b t) -> p b t", t=18)[:, :, 16:18]).then_inc(s_cg, 1)

            def store_new(j, d):
                pool.wait_ge(cn_free, 2 * j + d + 1)
                src = cno.rearrange("r (v p) -> r v p", v=2)
                for r0, r1, dst in ((0, 2, cv_p[0, 0]), (2, 18, cv_s[0].rearrange("b r c -> (b r) c"))):
                    pool.dma_start(dst.rearrange("r (v c) -> r v c", v=2)[:, :, bass.ds((2 * j + d) * P, P)], src[r0:r1])\
                        .then_inc(s_ocn, 16)

            def columns(j, d):
                cached(j, d, 0)
                cached(j, d, 1)
                if d:
                    store_new(j, d - 1)
                gather(j, d, 0)
                gather(j, d, 1)

            in_pairs(pool, columns)
            store_new(0, NC_FF - 1)

            for k in range(PLG_POOL):
                pool.wait_ge(s_ph, k + 1)
                pool.tensor_tensor(plgl[:, k, :], rplg[:, k, :], plgh[:, k, :].bitcast(F32), ALU.subtract).then_inc(s_pl, 1)
            row_rstd()
            row_rstd()
            for n in range(NT):
                if n + 2 < NT:
                    row_rstd()
                row_rstd()
                pool.wait_ge(s_y, n + 1)
                dst = y_p[0, n * P:(n + 1) * P, :] if n < NP else y_s.rearrange("b t d -> (b t) d")
                pool.dma_start(dst, z3[:, n % 3, :]).then_inc(s_oy[n % 3], 16)
            for i in range(3):
                pool.wait_ge(s_oy[i], 16 * 3)
            pool.wait_ge(s_ocn, 32 * NC_FF)
            for i in range(4):
                pool.wait_ge(s_ok[i], 16 * (NT // 4 + (i < NT % 4)))
            pool.wait_ge(s_ost, 32 * H_B)
            pool.wait_ge(s_ov, 32)
            pool.wait_ge(s_ol, 32)

        @block.sync
        def _(sp):
            def load(n):
                name, src, kt = chunks[n]
                if n >= W_SLOTS:
                    past_pe(sp, w_last[chunks[n - W_SLOTS][0]])
                s = n % W_SLOTS
                slot = ring[:, s, 0:kt, :] if n < w_index[("uv", 0)] else rawu[:, s // 2, s % 2]
                sp.dma_start(slot, src).then_inc(w_in_sem[s], 16)

            def tokens(p_, s_, n):
                return p_[n * P:(n + 1) * P, :] if n < NP else s_.rearrange("b t d -> (b t) d")

            def bcast(v, dst, s):
                sp.dma_start(dst, v.partition_broadcast(P)).then_inc(s, 16)

            sp.dma_start(keep[:, 0:C_LEV], consts[:, 0:C_LEV]).then_inc(s_ident, 16)
            for n in range(X_BUFS):
                sp.dma_start(xs[:, n, :], tokens(x_prompt[0], x_sample, n)).then_inc(s_xt[n], 16)
            sp.dma_start(keep[:, C_LEV:C_KEEP], consts[:, C_LEV:C_KEEP]).then_inc(s_const, 16)
            with nc.allow_non_contiguous_dma(reason="small columns"):
                sp.dma_start(bfg, b_fgate.rearrange("o h -> h o")).then_inc(s_small, 16)
                for c, o, w in ((0, O_F, H_A), (32, O_A1, RANK)):
                    sp.dma_start(wf[:, :, c:c + w], w_in[0].rearrange("(k p) n -> p k n", p=P)[:, :, o:o + w]).then_inc(s_small, 16)
                sp.dma_start(cvst, cache_ffn_conv[0].rearrange("b r c -> (b r) c")).then_inc(s_cv, 16)
                sp.dma_start(cwst[:, 0:3, :], conv_w[0].rearrange("j (c p) -> c j p", p=P)).then_inc(s_cv, 16)
                sp.dma_start(cwst[:, 3, :], conv_b[0].rearrange("(c p) -> c p", p=P)).then_inc(s_cv, 16)
                sp.dma_start(lfp.rearrange("p (b n) h -> p b n h", n=2), cache_fox_logf[0].rearrange("b (n p) h -> p b n h", p=P)).then_inc(s_lf, 16)
            for n in range(X_BUFS, NT):
                past_pe(sp, ("xT", n - X_BUFS))
                sp.dma_start(xs[:, n % X_BUFS, :], tokens(x_prompt[0], x_sample, n)).then_inc(s_xt[n], 16)
            for n in range(4):
                load(n)
            sp.dma_start(hc, consts[:, C_HSEL:C_SCAN]).then_inc(s_const2, 16)
            with nc.allow_non_contiguous_dma(reason="small columns"):
                sp.dma_start(ba2, b_a2[0].rearrange("(c p) -> p c", p=P)).then_inc(s_cols, 16)
                sp.dma_start(ggla, g_gla[0].rearrange("(c p) -> p c", p=P)).then_inc(s_cols, 16)
            for n in range(4, 16):
                load(n)
            copied(sp, *[("va", q, n) for q in range(2) for n in range(NT)])
            rows_p, rows_s = (lambda ap: ap[0, 0].rearrange("t h d -> t (h d)")), (lambda ap: ap[0].rearrange("b t h d -> (b t) (h d)"))
            for n in range(NT):
                copied(sp, ("kt", n))
                dst = rows_p(fk_p)[n * P:(n + 1) * P, :] if n < NP else rows_s(fk_s)
                sp.dma_start(dst, kst[:, n % 4, :]).then_inc(s_ok[n % 4], 16)
            sp.dma_start(rows_p(fv_p).rearrange("(n p) c -> p n c", p=P), va[:, 0:NP, :]).then_inc(s_ov, 16)
            sp.dma_start(rows_s(fv_s), va[:, NP, :]).then_inc(s_ov, 16)
            copied(sp, "lfT")
            with nc.allow_non_contiguous_dma(reason="8 log-forgets of a token in a row"):
                sp.dma_start(fl_p[0, 0].rearrange("(n p) h -> p n h", p=P), lfo[:, 0:NP, :]).then_inc(s_ol, 16)
                sp.dma_start(fl_s[0].rearrange("b t h -> (b t) h"), lfo[:, NP, :]).then_inc(s_ol, 16)

            NU = len(UNITS)
            sp.wait_ge(s_rl, 12)
            past_pe(sp, ("va", 1, NT - 1))
            copied(sp, ("va", 1, NT - 1))
            def past(b, *parts):
                for buf, src, s in parts:
                    sp.dma_start(buf[:, b % 4, :].rearrange("p (n c) -> p n c", n=2),
                                 src[0, b].rearrange("(n p) h d -> p n (h d)", p=P)).then_inc(s[b % 4], 16)

            k_part, v_part = (kp, cache_fox_k, s_kp), (vp, cache_fox_v, s_vp)
            for b in range(4):
                past(b, k_part)
            copied(sp, *[("pv", u) for u in range(NU - 4, NU)])
            for b in range(4):
                past(b, v_part)
            for key, b in (("k", 4), ("k", 5), ("k", 6), ("v", 4), ("k", 7), ("v", 5), ("v", 6), ("v", 7)):
                past_pe(sp, ("kpT" if key == "k" else "spv", b - 4))
                past(b, k_part if key == "k" else v_part)
                if key == "k" and b == 5:
                    sp.wait_ge(s_ov, 32)
                    for n in range(NT):
                        sp.dma_start(xs2[n], tokens(x_prompt[0], x_sample, n)).then_inc(s_xt[n], 16)
            copied(sp, ("soT", DEC_B - 1), ("soT", DEC_B - 2), ("spv", DEC_B - 1))
            sp.dma_start(wa2, w_a2[0]).then_inc(s_b, 16)
            sp.dma_start(scanm, consts[:, C_SCAN:C_ALL]).then_inc(s_b, 16)
            for n in range(16, FIRST_UP):
                load(n)
            wo_cols = w_o[0].rearrange("(k p) n -> p k n", p=P)
            past_pe(sp, ("ya", KT - 1, 2))
            sp.dma_start(wor[0], wo_cols[:, :, 0:512]).then_inc(s_wo[0], 16)
            past_pe(sp, ("yb", KT - 1, 2))
            for n in range(NT):
                sp.dma_start(x1[:, n, :], tokens(x_prompt[0], x_sample, n)).then_inc(s_xt[n], 16)
            sp.dma_start(wor[1], wo_cols[:, :, 512:1024]).then_inc(s_wo[1], 16)
            bcast(ln1_g[0], g1, s_g1)
            bcast(ln1_b[0], b1, s_g1)
            for n in range(FIRST_UP, FIRST_UP + W_SLOTS):
                load(n)
            def load_up(j, d):
                for v in range(2):
                    b, n = up_use(j, d - 2, v, 2)
                    sp.wait_ge(up_full[b], n + 1)
                    sp.dma_start(rawu[:, d % 2, v], w_up[0].rearrange("(k p) n -> p k n", p=P)
                                 [:, :, bass.ds((2 * j + d) * P + v * D_FF, P)]).then_inc(w_in_sem[2 * (d % 2) + v], 16)

            def load_down(j, d, wait=True):
                if wait:
                    b, n = dn_use(j, d - 2, 2 * NT - 1)
                    sp.wait_ge(dn_full[b], n + 1)
                sp.dma_start(rawd[:, d % 2, :], w_down[0, bass.ds((2 * j + d) * P, P), :]).then_inc(s_wdi[d % 2], 16)

            past_pe(sp, ("wo", 1, NT - 1))
            load_down(0, 0, wait=False)
            load_down(0, 1, wait=False)
            load_up(0, 2)
            with sp.Fori(0, NC_FF // 2 - 2) as j:
                for d in (1, 2):
                    load_up(j, d + 2)
                    load_down(j, d + 1)
            load_up(0, NC_FF - 1)
            load_down(0, NC_FF - 2)
            load_down(0, NC_FF - 1)
            for b in range(4):
                sp.wait_ge(up_full[b], 6 * NC_FF // 4)
            for n in range(2):
                sp.dma_start(pin[:, n, :], tokens(p_prompt[0, 0], p_sample[0], n)).then_inc(s_pin[n], 16)
            for k in range(KT):
                sp.dma_start(rplg[:, k, :], w_plg[0, k * P:(k + 1) * P, :]).then_inc(s_plg[k], 16)
                if k == 1:
                    for v, dst in ((ln2_g, g2), (ln2_b, b2), (ln3_g, g3), (ln3_b, b3)):
                        bcast(v[0], dst, s_g2)
            for b in range(3):
                sp.wait_ge(dn_full[b], 6 * NC_FF)
            sp.dma_start(rpl, w_pl[0].rearrange("(k p) n -> p k n", p=P)).then_inc(s_ple, 16)
            for n in range(2, NT):
                past_pe(sp, ("pT", n - 2))
                sp.dma_start(pin[:, n % 2, :], tokens(p_prompt[0, 0], p_sample[0], n)).then_inc(s_pin[n % 2], 16)


_INS = ["x_prompt", "x_sample", "cache_fox_k", "cache_fox_v", "cache_fox_logf", "state_gla", "cache_ffn_conv",
        "p_prompt", "p_sample", "w_in", "b_fgate", "w_a2", "b_a2", "g_gla", "w_a_out", "w_b_out", "w_o", "ln1_g",
        "ln1_b", "w_up", "conv_w", "conv_b", "w_down", "ln2_g", "ln2_b", "w_pl", "w_plg", "ln3_g", "ln3_b"]
_OUTS = [(1, SEQ, D), (DEC_B, DEC_T, D),
         (1, 1, SEQ, H_A, DH), (1, 1, SEQ, H_A, DH), (1, 1, SEQ, H_A), (1, 1, H_B, DK, DV), (1, 1, 2, 2 * D_FF),
         (1, DEC_B, DEC_T, H_A, DH), (1, DEC_B, DEC_T, H_A, DH), (1, DEC_B, DEC_T, H_A), (1, DEC_B, H_B, DK, DV),
         (1, DEC_B, 2, 2 * D_FF)]


def kernel(**inputs):
    import concourse.bacc as bacc
    from concourse.bass_utils import run_bass_kernel_spmd

    nc = bacc.Bacc("TRN2", target_bir_lowering=False, num_devices=1)
    arrays, args = {}, []
    for name in _INS:
        a = np.ascontiguousarray(inputs[name])
        arrays[f"in_{name}"] = a
        args.append(nc.dram_tensor(f"in_{name}", a.shape, F32, kind="ExternalInput").ap())
    arrays["in_consts"] = shape_constants()
    args.append(nc.dram_tensor("in_consts", arrays["in_consts"].shape, F32, kind="ExternalInput").ap())
    for i, shape in enumerate(_OUTS):
        args.append(nc.dram_tensor(f"out_{i}", shape, F32, kind="ExternalOutput").ap())
    build(nc, *args)
    r = run_bass_kernel_spmd(nc, [arrays], core_ids=[0])
    return tuple(r.results[0][f"out_{i}"] for i in range(len(_OUTS)))
```
